# Optimizing a Trainium2 kernel written in Bass

```python
import math
import jax, jax.numpy as jnp
from jax import lax
import numpy as np

D_MODEL = 1024
BATCH = 1
SEQ = 256
DEPTH = 2
DEC_BATCH = 8
DEC_SEQ = 1
PAST_LEN = 1024
PAGE_SIZE = 128

N_HEADS = 8
N_KV_HEADS = 2
GROUP = N_HEADS // N_KV_HEADS
HEAD_DIM = 64
WINDOW = 128
ATTN_BLOCK = 128
ROPE_THETA = 10000.0
DN_HEADS = 4
DN_DK = 128
DN_DV = 128
CONV_W = 4
DN_CHUNK = 64
D_FF = 2816
EPS = 1e-6

ATTN_Q = N_HEADS * HEAD_DIM
ATTN_KV = N_KV_HEADS * HEAD_DIM
DN_QK = DN_HEADS * DN_DK
DN_V = DN_HEADS * DN_DV
CONV_DIM = 2 * DN_QK + DN_V
SPLIT_SIZES = (ATTN_Q, ATTN_KV, ATTN_KV, CONV_DIM, DN_V, DN_HEADS, DN_HEADS, D_MODEL, D_MODEL)
IN_COLS = sum(SPLIT_SIZES)

kernel_name = "hybrid_swa_sink_gated_deltanet_macaron_step"

def rms_norm(x, w):
    xf = x.astype(jnp.float32)
    y = xf * lax.rsqrt(jnp.mean(xf * xf, axis=-1, keepdims=True) + EPS)
    return (y * w.astype(jnp.float32)).astype(x.dtype)

def l2_norm(x):
    return x * lax.rsqrt(jnp.sum(x * x, axis=-1, keepdims=True) + EPS)

def swiglu_ffn(x, w_gate_up, w_down):
    g, u = jnp.split(x @ w_gate_up, 2, axis=-1)
    return (jax.nn.silu(g) * u) @ w_down

def rope(x, pos):
    half = HEAD_DIM // 2
    inv = 1.0 / (ROPE_THETA ** (jnp.arange(half, dtype=jnp.float32) / half))
    ang = pos.astype(jnp.float32)[:, None] * inv[None, :]
    cos = jnp.cos(ang)[None, :, None, :]
    sin = jnp.sin(ang)[None, :, None, :]
    xf = x.astype(jnp.float32)
    x1, x2 = xf[..., :half], xf[..., half:]
    return jnp.concatenate([x1 * cos - x2 * sin, x2 * cos + x1 * sin], axis=-1).astype(x.dtype)

def split_in(p):
    idx = [int(i) for i in np.cumsum(SPLIT_SIZES)[:-1]]
    return jnp.split(p, idx, axis=-1)

def sink_attention(q, k, v, mask, sinks):
    s = jnp.einsum('bnqhgd,bnkhd->bnhgqk', q, k).astype(jnp.float32) / math.sqrt(HEAD_DIM)
    s = jnp.where(mask[None, :, None, None], s, -jnp.inf)
    sink = jnp.broadcast_to(sinks.astype(jnp.float32).reshape(N_KV_HEADS, GROUP)[None, None, :, :, None, None],
                            s.shape[:-1] + (1,))
    p = jax.nn.softmax(jnp.concatenate([s, sink], axis=-1), axis=-1)[..., :-1]
    return jnp.einsum('bnhgqk,bnkhd->bnqhgd', p.astype(v.dtype), v)

def swa_prompt(q, k, v, sinks):
    B, T = q.shape[:2]
    nb = T // ATTN_BLOCK
    qb = q.reshape(B, nb, ATTN_BLOCK, N_KV_HEADS, GROUP, HEAD_DIM)

    def band(x):
        xp = jnp.concatenate([jnp.zeros_like(x[:, :ATTN_BLOCK]), x], axis=1)
        xp = xp.reshape(B, nb + 1, ATTN_BLOCK, N_KV_HEADS, HEAD_DIM)
        return jnp.concatenate([xp[:, :-1], xp[:, 1:]], axis=2)

    kb, vb = band(k), band(v)
    a = jnp.arange(ATTN_BLOCK)[:, None]
    b = jnp.arange(2 * ATTN_BLOCK)[None, :]
    rel = ATTN_BLOCK + a - b
    in_band = (rel >= 0) & (rel <= WINDOW)
    valid = (jnp.arange(nb)[:, None, None] > 0) | (b[None] >= ATTN_BLOCK)
    mask = in_band[None] & valid
    o = sink_attention(qb, kb, vb, mask, sinks)
    return o.reshape(B, T, ATTN_Q)

def swa_sample(q, k, v, buf_k, buf_v, sinks):
    B, T = q.shape[:2]
    kc = jnp.concatenate([buf_k.astype(k.dtype), k], axis=1)
    vc = jnp.concatenate([buf_v.astype(v.dtype), v], axis=1)
    j = jnp.arange(T)[:, None]
    m = jnp.arange(WINDOW + T)[None, :]
    rel = WINDOW + j - m
    mask = ((rel >= 0) & (rel <= WINDOW))[None]
    o = sink_attention(q.reshape(B, 1, T, N_KV_HEADS, GROUP, HEAD_DIM), kc[:, None], vc[:, None], mask, sinks)
    return o.reshape(B, T, ATTN_Q), kc[:, -WINDOW:], vc[:, -WINDOW:]

def short_conv(x_raw, conv_buf, conv_w):
    T = x_raw.shape[1]
    xp = jnp.concatenate([conv_buf.astype(x_raw.dtype), x_raw], axis=1)
    y = xp[:, 0:T] * conv_w[0]
    for i in range(1, CONV_W):
        y = y + xp[:, i:i + T] * conv_w[i]
    return jax.nn.silu(y), xp[:, -(CONV_W - 1):]

def gdn_chunked(q, k, v, g, beta, S0):
    B, T, H, dk = q.shape
    dv = v.shape[-1]
    C = DN_CHUNK
    n = T // C

    def chunks(x):
        return x.reshape((B, n, C, H) + x.shape[3:]).swapaxes(2, 3)

    qc, kc, vc, gc, bc = chunks(q), chunks(k), chunks(v), chunks(g), chunks(beta)
    G = jnp.cumsum(gc, axis=-1)
    i = jnp.arange(C)[:, None]
    j = jnp.arange(C)[None, :]
    decay = jnp.exp(jnp.where(j <= i, G[..., :, None] - G[..., None, :], -jnp.inf))
    kk = jnp.einsum('bnhid,bnhjd->bnhij', kc, kc)
    A = jnp.where(j < i, bc[..., :, None] * kk * decay, 0.0)
    lhs = jnp.eye(C, dtype=A.dtype) + A
    rhs = jnp.concatenate([vc * bc[..., None], kc * (bc * jnp.exp(G))[..., None]], axis=-1)
    sol = lax.linalg.triangular_solve(lhs, rhs, left_side=True, lower=True, unit_diagonal=True)
    u_base, w = sol[..., :dv], sol[..., dv:]
    qk = jnp.einsum('bnhid,bnhjd->bnhij', qc, kc) * decay
    q_dec = qc * jnp.exp(G)[..., None]
    k_dec = kc * jnp.exp(G[..., -1:] - G)[..., None]
    g_last = jnp.exp(G[..., -1])

    def step(S, xs):
        u_b, w_c, qk_c, qd_c, kd_c, gl_c = xs
        u = u_b - jnp.einsum('bhcd,bhde->bhce', w_c, S)
        o = jnp.einsum('bhcd,bhde->bhce', qd_c, S) + jnp.einsum('bhij,bhje->bhie', qk_c, u)
        S = S * gl_c[..., None, None] + jnp.einsum('bhcd,bhce->bhde', kd_c, u)
        return S, o

    xs = tuple(x.swapaxes(0, 1) for x in (u_base, w, qk, q_dec, k_dec, g_last))
    S, o = lax.scan(step, S0, xs)
    return o.transpose(1, 0, 3, 2, 4).reshape(B, T, H, dv), S

def gdn_recurrent(q, k, v, g, beta, S0):
    def step(S, xs):
        q_t, k_t, v_t, g_t, b_t = xs
        S = S * jnp.exp(g_t)[..., None, None]
        pred = jnp.einsum('bhd,bhde->bhe', k_t, S)
        S = S + jnp.einsum('bhd,bhe->bhde', k_t, b_t[..., None] * (v_t - pred))
        return S, jnp.einsum('bhd,bhde->bhe', q_t, S)

    xs = tuple(x.swapaxes(0, 1) for x in (q, k, v, g, beta))
    S, o = lax.scan(step, S0, xs)
    return o.swapaxes(0, 1), S

def hybrid_layer(x, pos, lw, buf_k, buf_v, dn_state, conv_buf, is_prompt):
    B, T, _ = x.shape
    f32 = jnp.float32
    h = x + 0.5 * swiglu_ffn(rms_norm(x, lw['ffn1_norm']), lw['ffn1_w_gate_up'], lw['ffn1_w_down'])
    u = rms_norm(h, lw['mix_norm'])
    aq, ak, av, dn_raw, dn_z, dn_b, dn_a, gate_a, gate_d = split_in(u @ lw['w_in'])

    q = rope(rms_norm(aq.reshape(B, T, N_HEADS, HEAD_DIM), lw['q_norm']), pos)
    k = rope(rms_norm(ak.reshape(B, T, N_KV_HEADS, HEAD_DIM), lw['k_norm']), pos)
    v = av.reshape(B, T, N_KV_HEADS, HEAD_DIM)
    if is_prompt:
        o_a = swa_prompt(q, k, v, lw['attn_sinks'])
        new_k, new_v = k[:, -WINDOW:], v[:, -WINDOW:]
    else:
        o_a, new_k, new_v = swa_sample(q, k, v, buf_k, buf_v, lw['attn_sinks'])

    if is_prompt:
        conv_buf = jnp.zeros((B, CONV_W - 1, CONV_DIM), dn_raw.dtype)
    qkv, new_conv = short_conv(dn_raw, conv_buf, lw['conv_w'])
    dq, dk, dvv = jnp.split(qkv, [DN_QK, 2 * DN_QK], axis=-1)
    dq = l2_norm(dq.reshape(B, T, DN_HEADS, DN_DK).astype(f32)) * (DN_DK ** -0.5)
    dk = l2_norm(dk.reshape(B, T, DN_HEADS, DN_DK).astype(f32))
    dvv = dvv.reshape(B, T, DN_HEADS, DN_DV).astype(f32)
    beta = jax.nn.sigmoid(dn_b.astype(f32))
    g = -jnp.exp(lw['dn_A_log'].astype(f32)) * jax.nn.softplus(dn_a.astype(f32) + lw['dn_dt_bias'].astype(f32))
    if is_prompt:
        S0 = jnp.zeros((B, DN_HEADS, DN_DK, DN_DV), f32)
        o_d, S = gdn_chunked(dq, dk, dvv, g, beta, S0)
    else:
        o_d, S = gdn_recurrent(dq, dk, dvv, g, beta, dn_state.astype(f32))
    o_d = rms_norm(o_d, lw['dn_out_norm']) * jax.nn.silu(dn_z.reshape(B, T, DN_HEADS, DN_DV).astype(f32))
    o_d = o_d.reshape(B, T, DN_V).astype(x.dtype)

    br_a = o_a @ lw['w_attn_o']
    br_d = o_d @ lw['w_dn_o']
    h = h + (jax.nn.sigmoid(gate_a) * br_a + jax.nn.sigmoid(gate_d) * br_d) @ lw['w_out']
    y = h + 0.5 * swiglu_ffn(rms_norm(h, lw['ffn2_norm']), lw['ffn2_w_gate_up'], lw['ffn2_w_down'])
    return y, new_k, new_v, S.astype(x.dtype), new_conv

def setup_inputs(seed: int = 0) -> dict:
    key = jax.random.key(seed)
    ks = jax.random.split(key, 24)
    nrm = jax.random.normal
    f32 = jnp.float32
    dt = jnp.exp(jax.random.uniform(ks[14], (DEPTH, DN_HEADS), minval=math.log(1e-3), maxval=math.log(1e-1)))
    return {
        "x_prompt": nrm(ks[0], (BATCH, SEQ, D_MODEL), f32),
        "x_sample": nrm(ks[1], (DEC_BATCH, DEC_SEQ, D_MODEL), f32),
        "cache_swa_k": nrm(ks[2], (DEPTH, DEC_BATCH, WINDOW, N_KV_HEADS, HEAD_DIM), f32),
        "cache_swa_v": nrm(ks[3], (DEPTH, DEC_BATCH, WINDOW, N_KV_HEADS, HEAD_DIM), f32),
        "state_dn": 0.05 * nrm(ks[4], (DEPTH, DEC_BATCH, DN_HEADS, DN_DK, DN_DV), f32),
        "state_conv": nrm(ks[5], (DEPTH, DEC_BATCH, CONV_W - 1, CONV_DIM), f32),
        "ffn1_norm": 1.0 + 0.02 * nrm(ks[6], (DEPTH, D_MODEL), f32),
        "ffn1_w_gate_up": nrm(ks[7], (DEPTH, D_MODEL, 2 * D_FF), f32) * D_MODEL ** -0.5,
        "ffn1_w_down": nrm(ks[8], (DEPTH, D_FF, D_MODEL), f32) * D_FF ** -0.5,
        "mix_norm": 1.0 + 0.02 * nrm(ks[9], (DEPTH, D_MODEL), f32),
        "w_in": nrm(ks[10], (DEPTH, D_MODEL, IN_COLS), f32) * D_MODEL ** -0.5,
        "q_norm": 1.0 + 0.02 * nrm(ks[11], (DEPTH, HEAD_DIM), f32),
        "k_norm": 1.0 + 0.02 * nrm(ks[12], (DEPTH, HEAD_DIM), f32),
        "attn_sinks": 0.5 * nrm(ks[13], (DEPTH, N_HEADS), f32),
        "conv_w": nrm(ks[15], (DEPTH, CONV_W, CONV_DIM), f32) * CONV_W ** -0.5,
        "dn_A_log": jnp.log(jax.random.uniform(ks[16], (DEPTH, DN_HEADS), minval=1.0, maxval=16.0)),
        "dn_dt_bias": dt + jnp.log(-jnp.expm1(-dt)),
        "dn_out_norm": 1.0 + 0.02 * nrm(ks[17], (DEPTH, DN_DV), f32),
        "w_attn_o": nrm(ks[18], (DEPTH, ATTN_Q, D_MODEL), f32) * ATTN_Q ** -0.5,
        "w_dn_o": nrm(ks[19], (DEPTH, DN_V, D_MODEL), f32) * DN_V ** -0.5,
        "w_out": nrm(ks[20], (DEPTH, D_MODEL, D_MODEL), f32) * D_MODEL ** -0.5,
        "ffn2_norm": 1.0 + 0.02 * nrm(ks[21], (DEPTH, D_MODEL), f32),
        "ffn2_w_gate_up": nrm(ks[22], (DEPTH, D_MODEL, 2 * D_FF), f32) * D_MODEL ** -0.5,
        "ffn2_w_down": nrm(ks[23], (DEPTH, D_FF, D_MODEL), f32) * D_FF ** -0.5,
    }

def reference(x_prompt, x_sample, cache_swa_k, cache_swa_v, state_dn, state_conv,
              ffn1_norm, ffn1_w_gate_up, ffn1_w_down, mix_norm, w_in, q_norm, k_norm, attn_sinks,
              conv_w, dn_A_log, dn_dt_bias, dn_out_norm, w_attn_o, w_dn_o, w_out,
              ffn2_norm, ffn2_w_gate_up, ffn2_w_down):
    pos_p = jnp.arange(x_prompt.shape[1])
    pos_s = PAST_LEN + jnp.arange(x_sample.shape[1])
    yp, ys = x_prompt, x_sample
    kp_l, vp_l, sp_l, cp_l = [], [], [], []
    ks_l, vs_l, ss_l, cs_l = [], [], [], []
    for l in range(DEPTH):
        lw = dict(ffn1_norm=ffn1_norm[l], ffn1_w_gate_up=ffn1_w_gate_up[l], ffn1_w_down=ffn1_w_down[l],
                  mix_norm=mix_norm[l], w_in=w_in[l], q_norm=q_norm[l], k_norm=k_norm[l],
                  attn_sinks=attn_sinks[l], conv_w=conv_w[l], dn_A_log=dn_A_log[l],
                  dn_dt_bias=dn_dt_bias[l], dn_out_norm=dn_out_norm[l], w_attn_o=w_attn_o[l],
                  w_dn_o=w_dn_o[l], w_out=w_out[l], ffn2_norm=ffn2_norm[l],
                  ffn2_w_gate_up=ffn2_w_gate_up[l], ffn2_w_down=ffn2_w_down[l])
        yp, kp, vp, sp, cp = hybrid_layer(yp, pos_p, lw, None, None, None, None, True)
        ys, kss, vss, sss, css = hybrid_layer(ys, pos_s, lw, cache_swa_k[l], cache_swa_v[l],
                                              state_dn[l], state_conv[l], False)
        kp_l.append(kp); vp_l.append(vp); sp_l.append(sp); cp_l.append(cp)
        ks_l.append(kss); vs_l.append(vss); ss_l.append(sss); cs_l.append(css)
    return (yp, ys,
            jnp.stack(kp_l), jnp.stack(vp_l), jnp.stack(sp_l), jnp.stack(cp_l),
            jnp.stack(ks_l), jnp.stack(vs_l), jnp.stack(ss_l), jnp.stack(cs_l))


_drawn_inputs = setup_inputs


def setup_inputs(seed=0):
    import zlib

    import numpy as np

    out = dict(_drawn_inputs(seed))
    spreads = {}
    factors = {'ffn1_norm': 3.927,
     'q_norm': 31.858,
     'k_norm': 8.68,
     'attn_sinks': 56.016,
     'dn_out_norm': 28.328,
     'ffn2_norm': 5.007}
    for name, (base, spread) in spreads.items():
        noise = np.random.default_rng([zlib.crc32(name.encode()), seed]).standard_normal(out[name].shape)
        drawn = base * np.exp(spread * noise) if base else spread * noise
        out[name] = __import__('jax').numpy.asarray(drawn.astype(out[name].dtype))
    for name, factor in factors.items():
        out[name] = (out[name] * factor).astype(out[name].dtype)
    return out
```

```python
from contextlib import ExitStack

import numpy as np

import concourse.bass as bass
from concourse import mybir

F32 = mybir.dt.float32
F32R = mybir.dt.float32r
ACT = mybir.ActivationFunctionType
ALU = mybir.AluOpType
AX = mybir.AxisListType

P = 128
DEPTH, D_MODEL, D_FF = 2, 1024, 2816
T, B = 256, 8
N = T + B
PAST_LEN, WINDOW = 1024, 128
N_HEADS, N_KV, HEAD_DIM = 8, 2, 64
GROUP = N_HEADS // N_KV
H, DK, CONV_W = 4, 128, 4
EPS = 1e-6
KT = D_MODEL // P
FT = D_FF // P
UT = 16
RING = 3
AHEAD = 2
W_IN_TILES = 38
U_G1 = 0
U_D1 = U_G1 + FT
U_BA = U_D1 + 12
U_IN = U_BA + 1
U_AD = U_IN + W_IN_TILES // 2
U_WO = U_AD + 4
U_G2 = U_WO + 4
U_D2 = U_G2 + FT
UNITS = U_D2 + 12
assert UNITS == 96 and UNITS % RING == 0
STREAM = DEPTH * UNITS + AHEAD
DS_FFN = 6
DS_MIX = 1

C_N1, C_MIX, C_N2, C_N1NEXT = 0, 8, 16, 24
C_QW, C_QWR, C_KW, C_KWR = 32, 33, 34, 35
C_CONV = 36
C_ONORM = C_CONV + 48
C_SINK = C_ONORM + 1
C_SINKROW = C_SINK + 8
C_ALOG = C_SINKROW + 1
C_DT = C_ALOG + 4
NPAR = C_DT + 4

K_ID, K_ONES, K_LE, K_GT, K_PERM, K_BLK2 = 0, 128, 256, 384, 512, 640
K_COS, K_SIN = 642, 642 + N
K_M0 = K_SIN + N
K_LEV = K_M0 + 128
K_TRIL = K_LEV + 6 * 64
K_AM0, K_AM1 = K_TRIL + 128, K_TRIL + 256
K_SEL = K_AM1 + 256
K_MROW = K_SEL + 128
NCON = K_MROW + 32


class Signal:

    def __init__(self, sem, per_layer, before=0):
        self.sem, self.per_layer, self.before = sem, per_layer, before

    def at(self, layer, n):
        return layer * self.per_layer + (self.before + n)


class Steps:

    def __init__(self, sem, name, plan):
        self.sem, self.n = sem, 0
        self.seen = plan.setdefault(name, {})

    def mark(self, *name):
        self.n += 1
        self.seen[name] = self.n
        return 1

    def at(self, layer, *name):
        return layer * max(self.seen.values(), default=1) + self.seen.get(name, 1)


def host_constants():
    c = np.zeros((P, NCON), np.float32)
    i = np.arange(P)
    c[:, K_ID:K_ID + P] = np.eye(P)
    c[:, K_ONES:K_ONES + P] = 1
    c[:, K_LE:K_LE + P] = i[:, None] <= i[None]
    c[:, K_GT:K_GT + P] = i[:, None] > i[None]
    half = HEAD_DIM // 2
    for m in range(P):
        k = m + half if m % HEAD_DIM < half else m - half
        c[k, K_PERM + m] = -1.0 if m % HEAD_DIM < half else 1.0
        c[m, K_BLK2 + m // HEAD_DIM] = 1
    pos = np.concatenate([np.arange(T), np.full(B, PAST_LEN)]).astype(np.float32)
    inv = (1.0 / (np.float32(10000.0) ** (np.arange(half, dtype=np.float32) / half))).astype(np.float32)
    ang = pos[None] * inv[i % half][:, None]
    c[:, K_COS:K_COS + N] = np.cos(ang)
    c[:, K_SIN:K_SIN + N] = np.sin(ang)
    c[:, K_M0:K_M0 + P] = (i[:, None] // 2 == i[None] // 2) & (i[:, None] < i[None])
    for lv in range(1, 7):
        s = 2 ** lv
        j = np.array([b * 2 * s + e for b in range(P // (2 * s)) for e in range(s)])
        c[:, K_LEV + 64 * (lv - 1):K_LEV + 64 * lv] = (i[:, None] // (2 * s) == j[None] // (2 * s)) & (i[:, None] % (2 * s) >= s)
    c[:, K_TRIL:K_TRIL + P] = i[:, None] >= i[None]
    big = np.float32(-1e30)
    c[:, K_AM0:K_AM0 + P] = np.where(i[None] <= i[:, None], 0, big)
    c[:, K_AM1:K_AM1 + P] = np.where(i[None] >= i[:, None], 0, big)
    c[:, K_AM1 + P:K_AM1 + 2 * P] = c[:, K_AM0:K_AM0 + P]
    for r in range(64):
        kv, tb = r // 32, r % 32
        c[r, K_SEL + kv * 64:K_SEL + kv * 64 + 64] = 1
        c[r, K_MROW + tb] = 1
    return c


def tiles(w):
    l, k, m = w.shape
    return w.reshape(l, k // P, P, m // P, P).transpose(0, 3, 1, 2, 4)


def host_stream(a):
    out = np.zeros((STREAM, P, UT, P), np.float32)
    layers = out[:DEPTH * UNITS].reshape(DEPTH, UNITS, P, UT, P)

    def put(u, t, block):
        layers[:, u, :, t:t + block.shape[1]] = block.transpose(0, 2, 1, 3)

    for base, name in ((U_G1, "ffn1"), (U_G2, "ffn2")):
        gu, dn = tiles(a[name + "_w_gate_up"]), tiles(a[name + "_w_down"])
        for f in range(FT):
            put(base + f, 0, gu[:, f])
            put(base + f, KT, gu[:, FT + f])
        for m in range(0, KT, 2):
            both = np.concatenate([dn[:, m], dn[:, m + 1]], axis=1)
            for j in range(3):
                put(base + FT + m // 2 * 3 + j, 0, both[:, j * UT:(j + 1) * UT])
    w = a["w_in"]
    q, rest = w[:, :, :512], w[:, :, 512:]
    q = q.reshape(DEPTH, D_MODEL, N_KV, GROUP, HEAD_DIM).transpose(0, 1, 3, 2, 4).reshape(DEPTH, D_MODEL, 512)
    ak, av, dn = rest[:, :, :128], rest[:, :, 128:256], rest[:, :, 256:1792]
    z, ba, ga, gd = rest[:, :, 1792:2304], rest[:, :, 2304:2312], rest[:, :, 2312:3336], rest[:, :, 3336:]
    layers[:, U_BA, :, :KT, :8] = ba.reshape(DEPTH, KT, P, 8).transpose(0, 2, 1, 3)
    gates = np.stack([ga.reshape(DEPTH, D_MODEL, KT, P), gd.reshape(DEPTH, D_MODEL, KT, P)], axis=3)
    cols = np.concatenate([dn[:, :, 512:1024], dn[:, :, :512], dn[:, :, 1024:], ak, av, q, z,
                           gates.reshape(DEPTH, D_MODEL, 2048)], axis=2)
    t_in = tiles(cols)
    for i in range(W_IN_TILES):
        put(U_IN + i // 2, KT * (i % 2), t_in[:, i])
    ao = a["w_attn_o"].reshape(DEPTH, N_KV, GROUP, HEAD_DIM, D_MODEL).transpose(0, 2, 1, 3, 4).reshape(DEPTH, 512, D_MODEL)
    t_a, t_d, t_o = tiles(ao), tiles(a["w_dn_o"]), tiles(a["w_out"])
    for m in range(KT):
        put(U_AD + m // 2, KT * (m % 2), t_a[:, m])
        put(U_AD + m // 2, KT * (m % 2) + 4, t_d[:, m])
        put(U_WO + m // 2, KT * (m % 2), t_o[:, m])
    return out.reshape(STREAM, P, UT * P)


def host_params(a):
    p = np.zeros((DEPTH, P, NPAR), np.float32)

    def cols(at, w):
        p[:, :, at:at + KT] = w.reshape(DEPTH, KT, P).transpose(0, 2, 1)

    cols(C_N1, a["ffn1_norm"])
    cols(C_MIX, a["mix_norm"])
    cols(C_N2, a["ffn2_norm"])
    cols(C_N1NEXT, np.roll(a["ffn1_norm"], -1, axis=0))
    d = np.arange(P) % HEAD_DIM
    partner = (d + HEAD_DIM // 2) % HEAD_DIM
    p[:, :, C_QW], p[:, :, C_QWR] = a["q_norm"][:, d], a["q_norm"][:, partner]
    p[:, :, C_KW], p[:, :, C_KWR] = a["k_norm"][:, d], a["k_norm"][:, partner]
    cw = a["conv_w"].reshape(DEPTH, CONV_W, 3, H, P)[:, :, [1, 0, 2]]
    p[:, :, C_CONV:C_CONV + 48] = cw.transpose(0, 4, 2, 3, 1).reshape(DEPTH, P, 48)
    p[:, :, C_ONORM] = a["dn_out_norm"]
    s = a["attn_sinks"].reshape(DEPTH, N_KV, GROUP)
    p[:, :, C_SINK:C_SINK + 8] = s.transpose(0, 2, 1).reshape(DEPTH, 1, 8)
    p[:, :64, C_SINKROW] = np.repeat(s.reshape(DEPTH, 8), B, axis=1)
    p[:, :, C_ALOG:C_ALOG + 4] = a["dn_A_log"][:, None]
    p[:, :, C_DT:C_DT + 4] = a["dn_dt_bias"][:, None]
    return p.transpose(1, 0, 2).reshape(P, DEPTH * NPAR).copy()


def build(nc, stream, xT, params, consts, outs, ins, plan, mix=True):
    ctx = ExitStack()
    with ctx:
        top = [0]
        base0 = -(-nc.sbuf_base // 64) * 64

        def place(name, cols, dt=F32, at=None):
            off = top[0] if at is None else at
            t = nc.alloc_sbuf_tensor_at(name, [P, cols], dt, offset=base0 + 4 * off)
            if at is None:
                top[0] += -(-cols // 8) * 8
            return t

        raw = place("raw", RING * UT * P)
        whi = place("whi", RING * UT * P, F32R)
        wlo = place("wlo", RING * UT * P, F32R)
        x = place("x", KT * N)
        xh, xl = place("xh", KT * N, F32R), place("xl", KT * N, F32R)
        con = place("con", NCON)
        par_all = place("par_all", DEPTH * NPAR)
        par = place("par", NPAR)
        sq_at = top[0]
        sq = place("sq", 2 * N)
        acc = place("acc", N)
        var, rst, mhalf = place("var", 16), place("rst", 16), place("mhalf", 96)
        diag = place("diag", N)
        rs = place("rs", N)
        gbuf_at = top[0]
        gbuf, tbuf = place("gbuf", RING * N), place("tbuf", RING * N)
        arena = top[0]
        hh, hl = place("hh", FT * N, F32R), place("hl", FT * N, F32R)
        ffn_end = top[0]

        banks = [ctx.enter_context(nc.psum_tensor(f"bank{i}", [P, 512], F32)) for i in range(8)]
        STAT = banks[6]

        def tile_of(t, n, width=N):
            return t[:, n * width:(n + 1) * width]

        def slot(t, r, lo=0, hi=UT):
            return t[:, (r * UT + lo) * P:(r * UT + hi) * P]

        def sig(name, per_layer, before=0):
            return Signal(ctx.enter_context(nc.semaphore(name)), per_layer, before)

        w_loaded = [ctx.enter_context(nc.semaphore(f"w_loaded{r}")) for r in range(RING)]
        w_head = sig("w_head", UNITS)
        w_tail_p = sig("w_tail_p", UNITS)
        w_tail_v = sig("w_tail_v", UNITS)
        w_used = sig("w_used", UNITS, 1)
        consts_in = ctx.enter_context(nc.semaphore("consts_in"))
        x_in = ctx.enter_context(nc.semaphore("x_in"))
        ready0 = ctx.enter_context(nc.semaphore("ready0"))
        par_ready = sig("par_ready", 1)
        x_done = sig("x_done", 24, 8)
        xh_done = sig("xh_done", 24, 8)
        xl_done = sig("xl_done", 24, 8)
        sq_done = sig("sq_done", 24, 8)
        acc_done = sig("acc_done", 24, 8)
        ss_ready = sig("ss_ready", 3)
        var_ready = sig("var_ready", 3)
        acc_clear = sig("acc_clear", 3, 1)
        rstd_ready = sig("rstd_ready", 3)
        diag_ready = sig("diag_ready", 9)
        rsb_ready = sig("rsb_ready", 3)
        rs_ready = sig("rs_ready", 3)
        gate_ready = sig("gate_ready", 2 * FT)
        glu_g = sig("glu_g", 2 * FT)
        glu_t = sig("glu_t", 2 * FT)
        glu_a = sig("glu_a", 2 * FT)
        glu_free = sig("glu_free", 2 * FT, RING)
        glu_h = sig("glu_h", 2 * FT)
        glu_hh = sig("glu_hh", 2 * FT)
        h_ready = sig("h_ready", 2 * FT, RING)
        out_ready = sig("out_ready", 12)
        y_out = ctx.enter_context(nc.semaphore("y_out"))

        def split_head(L, u, r, use):
            nc.scalar.wait_ge(w_loaded[r], L * (16 * UNITS // RING) + (use * 16 + 16))
            nc.scalar.wait_ge(w_used.sem, w_used.at(L, u - 2))
            nc.scalar.copy(slot(whi, r), slot(raw, r)).then_inc(w_head.sem, 1)

        def split_tail(eng, done, L, u, r, lo, hi):
            eng.wait_ge(w_head.sem, w_head.at(L, u + 1))
            eng.tensor_tensor(slot(wlo, r, lo, hi), slot(raw, r, lo, hi), slot(whi, r, lo, hi).bitcast(F32),
                              ALU.subtract).then_inc(done.sem, 1)

        def product(out, r, t, mh, ml, start, stop, m=P):
            wh, wl = slot(whi, r, t, t + 1)[:, 0:m], slot(wlo, r, t, t + 1)[:, 0:m]
            nc.tensor.matmul(out, wh, mh, start=start, stop=False)
            nc.tensor.matmul(out, wh, ml, start=False, stop=False)
            return nc.tensor.matmul(out, wl, mh, start=False, stop=stop)

        def wait_unit(L, u):
            nc.tensor.wait_ge(w_tail_p.sem, w_tail_p.at(L, u + 1))
            nc.tensor.wait_ge(w_tail_v.sem, w_tail_v.at(L, u + 1))

        BLK = ((0, P, 0, P), (P, T, 0, P), (T, N, 0, B))

        def pe_sums(L, n):
            nc.tensor.wait_ge(acc_done.sem, acc_done.at(L, 8 * n))
            for b, (c0, c1, _, p1) in enumerate(BLK):
                mm = nc.tensor.matmul(STAT[0:p1, 300 + b:301 + b], acc[:, c0:c1], con[:, K_ONES:K_ONES + 1],
                                      start=True, stop=True)
            mm.then_inc(ss_ready.sem, 1)

        def dve_factor(L, n):
            nc.vector.wait_ge(ss_ready.sem, ss_ready.at(L, n + 1))
            nc.vector.tensor_scalar(var[:, 0:2], STAT[:, 300:302], 1.0 / D_MODEL, EPS, ALU.mult, ALU.add)
            nc.vector.tensor_scalar(var[0:B, 2:3], STAT[0:B, 302:303], 1.0 / D_MODEL, EPS, ALU.mult,
                                    ALU.add).then_inc(var_ready.sem, 1)
            nc.vector.memset(acc[:, :], 0.0).then_inc(acc_clear.sem, 1)
            nc.vector.wait_ge(rstd_ready.sem, rstd_ready.at(L, n + 1))
            for b, (c0, c1, _, p1) in enumerate(BLK):
                nc.vector.tensor_scalar(diag[0:p1, c0:c1], con[0:p1, K_ID:K_ID + p1], rst[0:p1, b:b + 1], None,
                                        ALU.mult).then_inc(diag_ready.sem, 1)

        def dve_spread(L, n):
            nc.vector.wait_ge(rsb_ready.sem, rsb_ready.at(L, n + 1))
            nc.vector.tensor_copy(rs[:, :], STAT[:, 0:N]).then_inc(rs_ready.sem, 1)
            nc.vector.wait_ge(rs_ready.sem, rs_ready.at(L, n + 1))

        def pool_factor(L, n):
            nc.gpsimd.wait_ge(var_ready.sem, var_ready.at(L, n + 1))
            nc.gpsimd.tensor_tensor(rst[:, 0:3], var[:, 0:3], mhalf[:, 0:3], ALU.pow).then_inc(rstd_ready.sem, 1)

        def pe_spread(L, n):
            nc.tensor.wait_ge(diag_ready.sem, diag_ready.at(L, 3 * n + 3))
            for b, (c0, c1, _, p1) in enumerate(BLK):
                mm = nc.tensor.matmul(STAT[:, c0:c1], con[0:p1, K_ONES:K_ONES + P], diag[0:p1, c0:c1],
                                      start=True, stop=True)
            mm.then_inc(rsb_ready.sem, 1)

        def dve_residual(L, e, m, last_unit, bank, scale):
            if m % 2:
                nc.vector.wait_ge(w_used.sem, w_used.at(L, last_unit + 1))
            else:
                nc.vector.wait_ge(out_ready.sem, out_ready.at(L, e // 2 + 1))
            nc.vector.scalar_tensor_tensor(out=tile_of(x, m), in0=bank[:, 0:N], scalar=scale, in1=tile_of(x, m),
                                           op0=ALU.mult, op1=ALU.add).then_inc(x_done.sem, 1)

        def dve_tail(L, e, m, col):
            nc.vector.wait_ge(xh_done.sem, xh_done.at(L, e + 1))
            nc.vector.scalar_tensor_tensor(out=tile_of(xl, m), in0=tile_of(x, m), scalar=par[:, col + m:col + m + 1],
                                           in1=tile_of(xh, m).bitcast(F32), op0=ALU.mult,
                                           op1=ALU.subtract).then_inc(xl_done.sem, 1)
            nc.vector.wait_ge(sq_done.sem, sq_done.at(L, e + 1))
            nc.vector.wait_ge(acc_done.sem, acc_done.at(L, e))
            if m == 0 and e >= 0:
                nc.vector.wait_ge(acc_clear.sem, acc_clear.at(L, e // 8 + 1))
            nc.vector.tensor_tensor(acc[:, :], acc[:, :], tile_of(sq, m % 2), ALU.add).then_inc(acc_done.sem, 1)

        def act_operand(L, e, m, col):
            nc.scalar.wait_ge(x_done.sem, x_done.at(L, e + 1))
            nc.scalar.activation(tile_of(xh, m), tile_of(x, m), ACT.Copy,
                                 scale=par[:, col + m:col + m + 1]).then_inc(xh_done.sem, 1)
            nc.scalar.wait_ge(acc_done.sem, acc_done.at(L, e - 1))
            nc.scalar.activation(tile_of(sq, m % 2), tile_of(x, m), ACT.Square).then_inc(sq_done.sem, 1)

        def pe_gate_up(L, ph):
            u0, n = (U_G1, U_G2)[ph], (0, 2)[ph]

            def unit(f, j, r, first=False):
                bg, bu = banks[2 * j], banks[2 * j + 1]
                wait_unit(L, u0 + f)
                nc.tensor.wait_ge(glu_free.sem, glu_free.at(L, ph * FT + f + 1 - RING))
                for k in range(KT):
                    if first:
                        nc.tensor.wait_ge(xl_done.sem, xl_done.at(L, 8 * n - 8 + k + 1))
                    mm = product(bg[:, 0:N], r, k, tile_of(xh, k), tile_of(xl, k), k == 0, k == KT - 1)
                mm.then_inc(gate_ready.sem, 1)
                if first:
                    pe_sums(L, n)
                for k in range(KT):
                    mm = product(bu[:, 0:N], r, KT + k, tile_of(xh, k), tile_of(xl, k), k == 0, k == KT - 1)
                mm.then_inc(w_used.sem, 1)
                if first:
                    pe_spread(L, n)

            unit(0, 1, u0 % RING, True)
            with nc.tensor.Fori(0, FT // RING) as i:
                for j in range(RING):
                    unit(3 * i + (1 + j), (2 + j) % RING, (u0 + 1 + j) % RING)

        def dve_gate_up(L, ph):
            u0, n = (U_G1, U_G2)[ph], (0, 2)[ph]

            def finish(f, j, split):
                g, t = tile_of(gbuf, j), tile_of(tbuf, j)
                e = ph * FT + f
                nc.vector.wait_ge(glu_t.sem, glu_t.at(L, e + 1))
                nc.vector.scalar_tensor_tensor(out=t, in0=t, scalar=1.0, in1=g, op0=ALU.add,
                                               op1=ALU.mult).then_inc(glu_a.sem, 1)
                nc.vector.wait_ge(w_used.sem, w_used.at(L, u0 + f + 1))
                nc.vector.wait_ge(glu_a.sem, glu_a.at(L, e + 1))
                nc.vector.tensor_tensor(g, t, banks[2 * j + 1][:, 0:N], ALU.mult).then_inc(glu_free.sem, 1)
                nc.vector.wait_ge(glu_free.sem, glu_free.at(L, e + 1))
                nc.vector.tensor_tensor(t, g, rs[:, :], ALU.mult).then_inc(glu_h.sem, 1)
                split()
                nc.vector.wait_ge(glu_hh.sem, glu_hh.at(L, e + 1))
                nc.vector.tensor_tensor(hl_tile(f), t, hh_tile(f).bitcast(F32), ALU.subtract).then_inc(h_ready.sem, 1)

            def unit(f, j, r, first=False):
                e = ph * FT + f
                nc.vector.wait_ge(gate_ready.sem, gate_ready.at(L, e + 1))
                if first:
                    dve_factor(L, n)
                    dve_spread(L, n)
                nc.vector.wait_ge(h_ready.sem, h_ready.at(L, e + 1 - RING))
                nc.vector.tensor_tensor(tile_of(gbuf, j), banks[2 * j][:, 0:N], rs[:, :], ALU.mult).then_inc(glu_g.sem, 1)
                finish(f, j, lambda: split_tail(nc.vector, w_tail_v, L, u0 + f + AHEAD, (r + AHEAD) % RING,
                                                UT - DS_FFN, UT))

            unit(0, 1, u0 % RING, True)
            with nc.vector.Fori(0, FT // RING) as i:
                for j in range(RING):
                    unit(3 * i + (1 + j), (2 + j) % RING, (u0 + 1 + j) % RING)

        def hh_tile(f):
            return tile_of(hh, f) if isinstance(f, int) else hh[:, bass.ds(f * N, N)]

        def hl_tile(f):
            return tile_of(hl, f) if isinstance(f, int) else hl[:, bass.ds(f * N, N)]

        def act_gate_up(L, ph):
            u0 = (U_G1, U_G2)[ph]

            def unit(f, j, r, use):
                e = ph * FT + f
                split_head(L, u0 + f + AHEAD, (r + AHEAD) % RING, use)
                nc.scalar.wait_ge(glu_g.sem, glu_g.at(L, e + 1))
                nc.scalar.activation(tile_of(tbuf, j), tile_of(gbuf, j), ACT.Tanh, scale=0.5).then_inc(glu_t.sem, 1)
                nc.scalar.wait_ge(glu_h.sem, glu_h.at(L, e + 1))
                nc.scalar.copy(hh_tile(f), tile_of(tbuf, j)).then_inc(glu_hh.sem, 1)

            unit(0, 1, u0 % RING, (u0 + AHEAD) // RING)
            with nc.scalar.Fori(0, FT // RING) as i:
                for j in range(RING):
                    unit(3 * i + (1 + j), (2 + j) % RING, (u0 + 1 + j) % RING, i + (u0 + 1 + j + AHEAD) // RING)

        def pool_units(L, u0, count, share):
            if count // RING:
                with nc.gpsimd.Fori(0, count // RING) as i:
                    for j in range(RING):
                        split_tail(nc.gpsimd, w_tail_p, L, 3 * i + (u0 + AHEAD + j), (u0 + AHEAD + j) % RING, 0, UT - share)
            for u in range(u0 + count // RING * RING, u0 + count):
                split_tail(nc.gpsimd, w_tail_p, L, u + AHEAD, (u + AHEAD) % RING, 0, UT - share)

        def pe_down(L, ph):
            u0 = (U_D1, U_D2)[ph]
            e0 = (0, 16)[ph]
            with nc.tensor.Fori(0, KT // 2) as i:
                for j in range(3):
                    wait_unit(L, 3 * i + (u0 + j))
                    if j == 0:
                        nc.tensor.wait_ge(h_ready.sem, h_ready.at(L, ph * FT + FT - 2))
                    for n in range(UT * j, min(UT * (j + 1), 2 * FT)):
                        m, f = n // FT, n % FT
                        if f == 0:
                            nc.tensor.wait_ge(x_done.sem, x_done.at(L, 2 * i + (e0 + m - 1)))
                        if n == FT - 2:
                            nc.tensor.wait_ge(h_ready.sem, h_ready.at(L, ph * FT + FT))
                        mm = product(banks[7 if m == 0 else 0][:, 0:N], (u0 + j) % RING, n % UT, tile_of(hh, f),
                                     tile_of(hl, f), f == 0, f == FT - 1)
                        if n == FT - 1:
                            mm.then_inc(out_ready.sem, 1)
                        elif n % UT == UT - 1 or n == 2 * FT - 1:
                            mm.then_inc(w_used.sem, 1)

        def dve_down(L, ph):
            u0, e0 = (U_D1, U_D2)[ph], (0, 16)[ph]
            col = (C_MIX, C_N1NEXT)[ph]
            for m in range(KT):
                for u in {0: (0,), 1: (1, 2)}[m % 2]:
                    u += u0 + m // 2 * 3
                    split_tail(nc.vector, w_tail_v, L, u + AHEAD, (u + AHEAD) % RING, UT - DS_FFN, UT)
                dve_residual(L, e0 + m, m, u0 + m // 2 * 3 + 2, banks[0 if m % 2 else 7], 0.25)
                dve_tail(L, e0 + m, m, col)

        def act_down(L, ph):
            u0, e0 = (U_D1, U_D2)[ph], (0, 16)[ph]
            col = (C_MIX, C_N1NEXT)[ph]
            for m in range(KT):
                for u in {0: (0,), 1: (1, 2)}[m % 2]:
                    u += u0 + m // 2 * 3
                    split_head(L, u + AHEAD, (u + AHEAD) % RING, (u + AHEAD) // RING)
                act_operand(L, e0 + m, m, col)
        def steps(name):
            return Steps(ctx.enter_context(nc.semaphore(name)), name, plan)

        gt = place("gt", 16 * N, at=arena)
        z = place("z", H * N, at=arena + 16 * N)
        CW = T + 3 + B
        craw_at = arena + 20 * N
        craw = place("craw", 12 * CW, at=craw_at)
        cv_at = craw_at + -(-12 * CW // 8) * 8
        cv = place("cv", 12 * N, at=cv_at)
        top[0] = max(top[0], -(-(cv_at + 12 * N) // 8) * 8)
        mixh = place("mixh", KT * N, F32R, at=craw_at)
        mixl = place("mixl", KT * N, F32R, at=craw_at + KT * N)
        assert 2 * KT * N <= 12 * CW + 4 * N
        odh = place("odh", H * N, F32R, at=cv_at + 4 * N)
        odl = place("odl", H * N, F32R, at=cv_at + 8 * N)
        act_scr, sq4, z_scr, k_scr = gt[:, 0:4 * N], gt[:, 4 * N:8 * N], gt[:, 8 * N:12 * N], gt[:, 12 * N:13 * N]
        rope_a, rope_b = gt[:, 13 * N:14 * N], gt[:, 14 * N:15 * N]
        aq_at = top[0]
        aq = place("aq", 4 * N)
        oah = place("oah", 4 * N, F32R, at=aq_at)
        oal = place("oal", 4 * N, F32R, at=top[0])
        ak, av = place("ak", N), place("av", N)
        kT = place("kT", N)
        cst = place("cst", 12 * 3 * B)
        assert 3 * N + 12 * 3 * B >= 4 * N
        kc = place("kc", B * P)
        vc = place("vc", B * P)
        st_at = top[0] - 2 * B * P
        states = place("states", 2 * B * P, at=st_at)
        rows1 = place("rows1", 512, at=top[0])
        ktok, vtok = place("ktok", 3 * P), place("vtok", 3 * P)
        otok = place("otok", 2 * 512)
        names = ("K", "T", "U", "Y", "B", "P")
        m0T_at = top[0] + 512
        M = [{n: place("m0" + n, 512) for n in names},
             {n: place("m1" + n, 512, at=craw_at + 512 * i) for i, n in enumerate(names)}]
        sm_at = top[0]
        smx = nc.alloc_sbuf_tensor_at("smx", [P, 4 * 384], F32, offset=base0 + 4 * gbuf_at)
        sm = [smx[:, 384 * i:384 * (i + 1)] for i in range(2)]
        ptb = [smx[:, 384 * (2 + i):384 * (3 + i)] for i in range(2)]
        drow = smx
        states2 = nc.alloc_sbuf_tensor_at("states2", [P, 2 * B * P], F32, offset=base0 + 4 * m0T_at)
        ba8 = place("ba8", N)
        bt = place("bt", 24)
        small = place("small", 12 * 12)
        x2, ab, e1, lnv, sp_, g_, bet, th, negA, egx = [small[:, 12 * i:12 * (i + 1)] for i in range(10)]
        eg = place("eg", 24)
        kbs, hbs, rqg = place("kbs", 8), place("hbs", 8), place("rqg", 8)
        dx, abc = place("dx", 64), place("abc", 64)
        pa_, pb_ = place("pa_", 32), place("pb_", 32)
        st, rkq = place("st", 80), place("rkq", 80)
        kq2 = place("kq2", 64)
        avar, arst = place("avar", 6), place("arst", 6)
        qvar, rqa = place("qvar", 16), place("rqa", 16)
        svar, srst = place("svar", 1), place("srst", 1)
        mx, nm, den, esk, rec = [place(n, 16) for n in ("mx", "nm", "den", "esk", "rec")]
        sT, sl, pts = place("sT", 64), place("sl", 130), place("pts", 64)
        rmat, pvs, oas = [place(n, 32) for n in ("rmat", "pvs", "oas")]
        prod, qsq = place("prod", 64), place("qsq", 64)
        smax, snm, sden, sesk, srec = [place(n, 1) for n in ("smax", "snm", "sden", "sesk", "srec")]
        oss, ovar, orst = place("oss", 8), place("ovar", 8), place("orst", 8)
        qkp, qkb, dlt, tmp32, osq, osv, osr = [place(n, 32) for n in ("qkp", "qkb", "dlt", "tmp32", "osq", "osv", "osr")]
        rows0 = place("rows0", 512, at=sq_at)
        assert base0 + 4 * top[0] <= nc.sbuf_usable_end, (top[0], nc.sbuf_usable_end)

        win_ready = sig("win_ready", 19)
        win_free = sig("win_free", 38, 2)
        ba_ready = sig("ba_ready", 1)
        pe_ba, pe_dn, pe_at, pe_sd = steps("pe_ba"), steps("pe_dn"), steps("pe_at"), steps("pe_sd")
        v_ba, v_conv, v_dn, v_at, v_sd = steps("v_ba"), steps("v_conv"), steps("v_dn"), steps("v_at"), steps("v_sd")
        a_ba, a_conv, a_dn, a_at, a_sd = steps("a_ba"), steps("a_conv"), steps("a_dn"), steps("a_at"), steps("a_sd")
        g_mix = steps("g_mix")
        v_gate, a_gate = steps("v_gate"), steps("a_gate")
        pe_ad, v_ad, a_ad = steps("pe_ad"), steps("v_ad"), steps("a_ad")
        d_cst, d_kc, d_vc = sig("d_cst", 16), sig("d_kc", 16), sig("d_vc", 16)
        d_state = [sig("d_state0", 16), sig("d_state1", 16)]
        d_stout = sig("d_stout", 64)
        d_conv = sig("d_conv", 48)
        d_kv = sig("d_kv", 64)
        d_s2 = sig("d_s2", 16)
        d_shift = ctx.enter_context(nc.semaphore("d_shift"))

        TE, VE, SE, GE = nc.tensor, nc.vector, nc.scalar, nc.gpsimd
        one_col = con[:, K_ONES:K_ONES + 1]
        ident, ones = con[:, K_ID:K_ID + P], con[:, K_ONES:K_ONES + P]

        def turn(out, src):
            n = src.shape[0]
            if n == P and src.shape[1] == P:
                return TE.transpose(out, src, ident)
            return TE.matmul(out, src, con[0:n, K_ID:K_ID + n], start=True, stop=True)

        def hd4(t):
            return t.rearrange("p (h d) -> p h d", h=4)

        def hs(t, h):
            return t[:, h * P:(h + 1) * P]

        def cvt(group, h):
            n = {"q": 0, "k": 4, "v": 8}[group] + h
            return cv[:, n * N:(n + 1) * N]

        def cv4(group):
            n = {"q": 0, "k": 4, "v": 8}[group]
            return cv[:, n * N:(n + 4) * N].rearrange("p (h t) -> p h t", h=4)

        def bc(ap, n):
            return ap.unsqueeze(2).to_broadcast([ap.shape[0], ap.shape[1], n])

        def bcm(ap, n):
            return ap.unsqueeze(1).to_broadcast([ap.shape[0], n, ap.shape[1]])

        def tok(c):
            return slice(c * P, (c + 1) * P)

        BA_, B7 = banks[6], banks[7]
        CB = [(banks[2], banks[3]), (banks[4], banks[5])]

        def pe_win(L, i, mid):
            u, t0 = U_IN + i // 2, KT * (i % 2)
            if i % 2 == 0:
                wait_unit(L, u)
            TE.wait_ge(win_free.sem, win_free.at(L, i - 1))
            if i == 1:
                TE.wait_ge(v_ba.sem, v_ba.at(L, "ba8"))
            for k in range(KT):
                if k == KT // 2:
                    mid()
                mm = product(banks[i % 2][:, 0:N], u % RING, t0 + k, tile_of(xh, k), tile_of(xl, k), k == 0, k == KT - 1)
            if i % 2:
                mm.then_inc(w_used.sem, 1)
            else:
                mm.then_inc(win_ready.sem, 1)

        def dve_evac(L, i, out):
            if i % 2:
                VE.wait_ge(w_used.sem, w_used.at(L, U_IN + i // 2 + 1))
            else:
                VE.wait_ge(win_ready.sem, win_ready.at(L, i // 2 + 1))
            VE.tensor_tensor(out, banks[i % 2][:, 0:N], rs[:, :], ALU.mult).then_inc(win_free.sem, 1)

        def pe_ba_product(L):
            wait_unit(L, U_BA)
            for k in range(KT):
                TE.wait_ge(xl_done.sem, xl_done.at(L, k + 1))
                mm = product(banks[1][:, 0:N], U_BA % RING, k, tile_of(xh, k), tile_of(xl, k), k == 0, k == KT - 1)
            mm.then_inc(w_used.sem, 1)

        def dve_ba_scale(L):
            VE.wait_ge(w_used.sem, w_used.at(L, U_BA + 1))
            VE.tensor_tensor(ba8[0:8, :], banks[1][0:8, 0:N], rs[0:8, :], ALU.mult).then_inc(v_ba.sem, v_ba.mark("ba8"))

        def pe_ba_turn(L):
            TE.wait_ge(v_ba.sem, v_ba.at(L, "ba8"))
            for b, (c0, c1, _, p1) in enumerate(BLK):
                mm = turn(BA_[0:p1, 272 + 8 * b:280 + 8 * b], ba8[0:8, c0:c1])
            mm.then_inc(pe_ba.sem, pe_ba.mark("turned"))

        def dve_ba(L):
            VE.wait_ge(pe_ba.sem, pe_ba.at(L, "turned"))
            VE.tensor_copy(bt[:, 0:16], BA_[:, 272:288]).then_inc(v_ba.sem, v_ba.mark("bt"))
            VE.tensor_copy(bt[0:B, 16:24], BA_[0:B, 288:296]).then_inc(v_ba.sem, v_ba.mark("bt2"))
            VE.wait_ge(v_ba.sem, v_ba.at(L, "bt2"))
            btv = bt[:, :].rearrange("p (b c) -> p b c", b=3)
            VE.tensor_tensor(x2.rearrange("p (b c) -> p b c", b=3), btv[:, :, 4:8], bcm(par[:, C_DT:C_DT + 4], 3),
                             ALU.add).then_inc(v_ba.sem, v_ba.mark("x2"))
            VE.wait_ge(v_ba.sem, v_ba.at(L, "x2"))
            VE.scalar_tensor_tensor(out=ab, in0=x2, scalar=-1.0, in1=x2, op0=ALU.mult,
                                    op1=ALU.max).then_inc(v_ba.sem, v_ba.mark("abs"))
            VE.wait_ge(a_ba.sem, a_ba.at(L, "exp"))
            VE.tensor_scalar(e1, e1, 1.0, None, ALU.add).then_inc(v_ba.sem, v_ba.mark("1+e"))
            VE.tensor_scalar(bet, th, 0.5, 0.5, ALU.mult, ALU.add).then_inc(v_ba.sem, v_ba.mark("beta"))
            VE.wait_ge(a_ba.sem, a_ba.at(L, "ln"))
            VE.scalar_tensor_tensor(out=sp_, in0=x2, scalar=0.0, in1=lnv, op0=ALU.max,
                                    op1=ALU.add).then_inc(v_ba.sem, v_ba.mark("softplus"))
            VE.wait_ge(v_ba.sem, v_ba.at(L, "softplus"))
            VE.scalar_tensor_tensor(out=g_.rearrange("p (b c) -> p b c", b=3), in0=sp_.rearrange("p (b c) -> p b c", b=3),
                                    scalar=-1.0, in1=bcm(negA[:, 0:4], 3), op0=ALU.mult,
                                    op1=ALU.mult).then_inc(v_ba.sem, v_ba.mark("g"))
            VE.tensor_scalar(hbs[:, :], bet[:, 0:8], 0.5, None, ALU.mult).then_inc(v_ba.sem, v_ba.mark("hb"))
            VE.wait_ge(a_ba.sem, a_ba.at(L, "sample decay"))
            d4 = dx[0:B, :].rearrange("p (v h b) -> p v h b", v=2, h=4)
            VE.tensor_tensor(d4[:, 0], bc(egx[0:B, 0:4], B), bcm(con[0:B, K_ID:K_ID + B], 4),
                             ALU.mult).then_inc(v_ba.sem, v_ba.mark("dx0"))
            VE.tensor_tensor(d4[:, 1], bc(bet[0:B, 8:12], B), bcm(con[0:B, K_ID:K_ID + B], 4),
                             ALU.mult).then_inc(v_ba.sem, v_ba.mark("dx"))

        def act_ba(L):
            SE.wait_ge(v_ba.sem, v_ba.at(L, "bt2"))
            SE.activation(th.rearrange("p (b c) -> p b c", b=3), bt[:, :].rearrange("p (b c) -> p b c", b=3)[:, :, 0:4],
                          ACT.Tanh, scale=0.5).then_inc(a_ba.sem, a_ba.mark("tanh"))
            SE.activation(negA[:, 0:4], par[:, C_ALOG:C_ALOG + 4], ACT.Exp).then_inc(a_ba.sem, a_ba.mark("A"))
            SE.wait_ge(v_ba.sem, v_ba.at(L, "abs"))
            SE.activation(e1, ab, ACT.Exp, scale=-1.0).then_inc(a_ba.sem, a_ba.mark("exp"))
            SE.wait_ge(v_ba.sem, v_ba.at(L, "1+e"))
            SE.activation(lnv, e1, ACT.Ln).then_inc(a_ba.sem, a_ba.mark("ln"))
            SE.wait_ge(v_ba.sem, v_ba.at(L, "g"))
            SE.activation(egx[0:B, 0:4], g_[0:B, 8:12], ACT.Exp).then_inc(a_ba.sem, a_ba.mark("sample decay"))

        def pe_decays(L):
            TE.wait_ge(v_ba.sem, v_ba.at(L, "dx"))
            for n, k in enumerate((K_LE, K_GT, K_ONES)):
                TE.matmul(BA_[:, 304 + 8 * n:312 + 8 * n], con[:, k:k + P], g_[:, 0:8], start=True, stop=True)
            TE.matmul(BA_[:, 336:400], con[0:B, K_ONES:K_ONES + P], dx[0:B, :], start=True,
                      stop=True).then_inc(pe_ba.sem, pe_ba.mark("decays"))

        def act_decays(L):
            SE.wait_ge(pe_ba.sem, pe_ba.at(L, "decays"))
            SE.activation(eg[:, :], BA_[:, 304:328], ACT.Exp).then_inc(a_ba.sem, a_ba.mark("eg"))

        def dve_decays(L):
            VE.wait_ge(pe_ba.sem, pe_ba.at(L, "decays"))
            VE.wait_ge(a_ba.sem, a_ba.at(L, "eg"))
            VE.tensor_copy(abc[:, :], BA_[:, 336:400]).then_inc(v_ba.sem, v_ba.mark("abc"))
            VE.tensor_tensor(kbs[:, :], bet[:, 0:8], eg[:, 0:8], ALU.mult).then_inc(v_ba.sem, v_ba.mark("kb"))

        GRP = ("k", "q", "v")

        def dve_conv(L, i):
            src = craw[:, i * CW:(i + 1) * CW]
            out = cvt(GRP[i // 4], i % 4)[:, 0:T]
            VE.wait_ge(win_free.sem, win_free.at(L, i + 1))
            VE.tensor_scalar(out, src[:, 0:T], par[:, C_CONV + 4 * i:C_CONV + 4 * i + 1], None,
                             ALU.mult).then_inc(v_conv.sem, v_conv.mark("tap0", i))
            for tap in range(1, CONV_W):
                VE.wait_ge(v_conv.sem, v_conv.at(L, f"tap{tap - 1}", i))
                VE.scalar_tensor_tensor(out=out, in0=src[:, tap:tap + T], scalar=par[:, C_CONV + 4 * i + tap:C_CONV + 4 * i + tap + 1],
                                        in1=out, op0=ALU.mult, op1=ALU.add).then_inc(v_conv.sem, v_conv.mark(f"tap{tap}", i))

        def pool_conv(L, g):
            GE.wait_ge(win_free.sem, win_free.at(L, 4 * g + 4))
            if g == 0:
                GE.wait_ge(d_cst.sem, d_cst.at(L, 16))
            cs = cst[:, g * 96:(g + 1) * 96].rearrange("p (c t b) -> p c t b", c=4, t=3)
            new = craw[:, 4 * g * CW:(4 * g + 4) * CW].rearrange("p (c w) -> p c w", c=4)[:, :, T + 3:CW]
            pa4, pb4 = [t[:, :].rearrange("p (c b) -> p c b", c=4) for t in (pa_, pb_)]
            for tap in range(CONV_W):
                w = bc(par[:, C_CONV + 16 * g:C_CONV + 16 * g + 16].rearrange("p (c t) -> p c t", t=4)[:, :, tap], B)
                GE.tensor_tensor(pb4 if tap else pa4, cs[:, :, tap] if tap < 3 else new, w,
                                 ALU.mult).then_inc(g_mix.sem, g_mix.mark("mul", g, tap))
                GE.wait_ge(g_mix.sem, g_mix.at(L, "mul", g, tap))
                if tap:
                    out = pa4 if tap < 3 else cv4(GRP[g])[:, :, T:N]
                    GE.tensor_tensor(out, pa4, pb4, ALU.add).then_inc(g_mix.sem, g_mix.mark("add", g, tap))
                    GE.wait_ge(g_mix.sem, g_mix.at(L, "add", g, tap))

        def act_conv(L, g):
            grp = GRP[g]
            SE.wait_ge(v_conv.sem, v_conv.at(L, "tap3", 4 * g + 3))
            SE.wait_ge(g_mix.sem, g_mix.at(L, "add", g, 3))
            if g:
                SE.wait_ge(v_conv.sem, v_conv.at(L, "silu", g - 1))
            SE.activation(act_scr, cv[:, cv_off(grp):cv_off(grp) + 4 * N], ACT.Tanh,
                          scale=0.5).then_inc(a_conv.sem, a_conv.mark("tanh", g))

        def act_conv_sq(L, g):
            grp = GRP[g]
            SE.wait_ge(v_conv.sem, v_conv.at(L, "silu", g))
            if grp == "q":
                SE.wait_ge(pe_dn.sem, pe_dn.at(L, "stats", "k"))
            SE.activation(sq4, cv[:, cv_off(grp):cv_off(grp) + 4 * N], ACT.Square).then_inc(a_conv.sem, a_conv.mark("sq", grp))

        def cv_off(grp):
            return {"q": 0, "k": 4, "v": 8}[grp] * N

        def dve_silu(L, g):
            grp = GRP[g]
            VE.wait_ge(a_conv.sem, a_conv.at(L, "tanh", g))
            t = cv[:, cv_off(grp):cv_off(grp) + 4 * N]
            VE.scalar_tensor_tensor(out=t, in0=act_scr, scalar=1.0, in1=t, op0=ALU.add,
                                    op1=ALU.mult).then_inc(v_conv.sem, v_conv.mark("silu", g))

        def pe_stats(L, grp):
            o = {"k": 400, "q": 440}[grp]
            TE.wait_ge(a_conv.sem, a_conv.at(L, "sq", grp))
            if grp == "k":
                TE.wait_ge(rs_ready.sem, rs_ready.at(L, 2))
            s3 = sq4.rearrange("p (h t) -> p h t", h=4)
            for c in range(2):
                for h in range(H):
                    TE.matmul(B7[:, o + 4 * c + h:o + 4 * c + h + 1], s3[:, h, tok(c)], one_col, start=True, stop=True)
            TE.matmul(B7[:, o + 8:o + 40], ones, s3[:, :, T:N], start=True,
                      stop=True).then_inc(pe_dn.sem, pe_dn.mark("stats", grp))

        def dve_stats(L, grp):
            o = {"k": 0, "q": 40}[grp]
            VE.wait_ge(pe_dn.sem, pe_dn.at(L, "stats", grp))
            VE.tensor_scalar(st[:, o:o + 40], B7[:, 400 + o:440 + o], 1.0, 4 * EPS, ALU.mult,
                             ALU.add).then_inc(v_dn.sem, v_dn.mark("ss", grp))

        def pool_stats(L, grp):
            o = {"k": 0, "q": 40}[grp]
            GE.wait_ge(v_dn.sem, v_dn.at(L, "ss", grp))
            GE.tensor_tensor(rkq[:, o:o + 40], st[:, o:o + 40], mhalf[:, 0:40],
                             ALU.pow).then_inc(g_mix.sem, g_mix.mark("rsqrt", grp))

        def dve_sample_kq(L, grp):
            o = {"k": 0, "q": 40}[grp]
            VE.wait_ge(g_mix.sem, g_mix.at(L, "rsqrt", grp))
            if grp == "q":
                VE.tensor_scalar(rkq[:, 40:80], rkq[:, 40:80], float(DK) ** -0.5, None,
                                 ALU.mult).then_inc(v_dn.sem, v_dn.mark("rq"))
                VE.wait_ge(v_dn.sem, v_dn.at(L, "rq"))
                VE.tensor_tensor(rqg[:, :], rkq[:, 40:48], eg[:, 0:8], ALU.mult).then_inc(v_dn.sem, v_dn.mark("rqg"))
            n = {"k": 0, "q": 32}[grp]
            VE.tensor_tensor(kq2[:, n:n + 32].rearrange("p (h b) -> p h b", h=4), cv4(grp)[:, :, T:N],
                             rkq[:, o + 8:o + 40].rearrange("p (h b) -> p h b", h=4),
                             ALU.mult).then_inc(v_dn.sem, v_dn.mark("sample", grp))

        def dve_decay_lhs(L, c):
            if c:
                VE.wait_ge(d_conv.sem, d_conv.at(L, 48))
                VE.wait_ge(g_mix.sem, g_mix.at(L, "add", 2, 3))
            for h in range(H):
                VE.tensor_scalar(hs(M[c]["B"], h), con[:, K_LE:K_LE + P], g_[:, 4 * c + h:4 * c + h + 1], None,
                                 ALU.mult).then_inc(v_dn.sem, v_dn.mark("tg", c, h))

        def pe_decay(L, c):
            TE.wait_ge(v_dn.sem, v_dn.at(L, "tg", c, 3))
            for h in range(H):
                mm = TE.matmul(hs(CB[c][0], h), hs(M[c]["B"], h), con[:, K_GT:K_GT + P], start=True, stop=True)
            mm.then_inc(pe_dn.sem, pe_dn.mark("D", c))

        def act_decay(L, c):
            SE.wait_ge(pe_dn.sem, pe_dn.at(L, "D", c))
            SE.activation(M[c]["P"][:, :], CB[c][0][:, :], ACT.Exp).then_inc(a_dn.sem, a_dn.mark("E", c))

        def dve_decay(L, c):
            VE.wait_ge(a_dn.sem, a_dn.at(L, "E", c))
            VE.tensor_tensor(hd4(M[c]["P"][:, :]), hd4(M[c]["P"][:, :]), bcm(con[:, K_TRIL:K_TRIL + P], 4),
                             ALU.mult).then_inc(v_dn.sem, v_dn.mark("E", c))

        def pe_turn(L, c, src, bank, name, wait):
            TE.wait_ge(wait[0].sem, wait[0].at(L, *wait[1]))
            for h in range(H):
                mm = TE.transpose(hs(bank, h), src(h), ident)
            mm.then_inc(pe_dn.sem, pe_dn.mark(name, c))

        def pe_k_turn(L, c):
            TE.wait_ge(a_dn.sem, a_dn.at(L, "E", c))
            pe_turn(L, c, lambda h: cvt("k", h)[:, tok(c)], CB[c][0], "k tok", (v_conv, ("silu", 0)))

        def dve_kn(L, c):
            VE.wait_ge(pe_dn.sem, pe_dn.at(L, "k tok", c))
            VE.wait_ge(g_mix.sem, g_mix.at(L, "rsqrt", "k"))
            VE.tensor_tensor(hd4(M[c]["K"][:, :]), hd4(CB[c][0][:, :]), bc(rkq[:, 4 * c:4 * c + 4], P),
                             ALU.mult).then_inc(v_dn.sem, v_dn.mark("K", c))

        def pe_kT(L, c):
            pe_turn(L, c, lambda h: hs(M[c]["K"], h), CB[c][1], "kT", (v_dn, ("K", c)))

        def act_kT(L, c):
            SE.wait_ge(pe_dn.sem, pe_dn.at(L, "kT", c))
            SE.copy(M[c]["T"][:, :], CB[c][1][:, :]).then_inc(a_dn.sem, a_dn.mark("kT", c))

        def pe_kk(L, c):
            TE.wait_ge(a_dn.sem, a_dn.at(L, "kT", c))
            for h in range(H):
                mm = TE.matmul(hs(CB[c][0], h), hs(M[c]["T"], h), hs(M[c]["T"], h), start=True, stop=True)
            mm.then_inc(pe_dn.sem, pe_dn.mark("kk", c))

        def dve_A(L, c):
            VE.wait_ge(pe_dn.sem, pe_dn.at(L, "kk", c))
            VE.wait_ge(v_dn.sem, v_dn.at(L, "E", c))
            for h in range(H):
                VE.scalar_tensor_tensor(out=hs(M[c]["Y"], h), in0=hs(CB[c][0], h), scalar=bet[:, 4 * c + h:4 * c + h + 1],
                                        in1=hs(M[c]["P"], h), op0=ALU.mult, op1=ALU.mult).then_inc(v_dn.sem, v_dn.mark("A", c, h))

        def pe_B(L, c):
            pe_turn(L, c, lambda h: hs(M[c]["Y"], h), CB[c][1], "B", (v_dn, ("A", c, 3)))

        def act_B(L, c):
            SE.wait_ge(pe_dn.sem, pe_dn.at(L, "B", c))
            SE.copy(M[c]["B"][:, :], CB[c][1][:, :]).then_inc(a_dn.sem, a_dn.mark("B", c))

        def dve_U0(L, c):
            VE.wait_ge(a_dn.sem, a_dn.at(L, "B", c))
            VE.tensor_tensor(hd4(M[c]["U"][:, :]), hd4(M[c]["B"][:, :]), bcm(con[:, K_M0:K_M0 + P], 4),
                             ALU.mult).then_inc(v_dn.sem, v_dn.mark("U00", c))
            VE.wait_ge(v_dn.sem, v_dn.at(L, "U00", c))
            VE.tensor_tensor(hd4(M[c]["U"][:, :]), bcm(ident, 4), hd4(M[c]["U"][:, :]),
                             ALU.subtract).then_inc(v_dn.sem, v_dn.mark("U0", c))

        def pe_T0(L, c):
            TE.wait_ge(a_dn.sem, a_dn.at(L, "B", c))
            pe_turn(L, c, lambda h: hs(M[c]["U"], h), CB[c][1], "T0", (v_dn, ("U0", c)))

        def act_T0(L, c):
            SE.wait_ge(pe_dn.sem, pe_dn.at(L, "T0", c))
            SE.copy(M[c]["T"][:, :], CB[c][1][:, :]).then_inc(a_dn.sem, a_dn.mark("T0", c))

        def even(t, h, s):
            return hs(t, h).rearrange("p (n two e) -> p n two e", two=2, e=s)[:, :, 0]

        def pe_Y(L, c, lv):
            if lv == 1:
                TE.wait_ge(a_dn.sem, a_dn.at(L, "T0", c))
            else:
                TE.wait_ge(a_dn.sem, a_dn.at(L, "U", c, lv - 1))
            for h in range(H):
                mm = TE.matmul(CB[c][0][:, 64 * h:64 * h + 64], hs(M[c]["B"], h), even(M[c]["T"], h, 2 ** lv),
                               start=True, stop=True)
            mm.then_inc(pe_dn.sem, pe_dn.mark("Y", c, lv))

        def dve_Y(L, c, lv):
            VE.wait_ge(pe_dn.sem, pe_dn.at(L, "Y", c, lv))
            VE.tensor_tensor(hd4(M[c]["Y"][:, 0:256]), hd4(CB[c][0][:, 0:256]),
                             bcm(con[:, K_LEV + 64 * (lv - 1):K_LEV + 64 * lv], 4),
                             ALU.mult).then_inc(v_dn.sem, v_dn.mark("Y", c, lv))

        def pe_Z(L, c, lv):
            TE.wait_ge(v_dn.sem, v_dn.at(L, "Y", c, lv))
            if lv > 1:
                TE.wait_ge(a_dn.sem, a_dn.at(L, "U", c, lv - 1))
            for h in range(H):
                mm = TE.matmul(CB[c][1][:, 64 * h:64 * h + 64], hs(M[c]["U"], h), M[c]["Y"][:, 64 * h:64 * h + 64],
                               start=True, stop=True)
            mm.then_inc(pe_dn.sem, pe_dn.mark("Z", c, lv))

        def dve_Z(L, c, lv):
            VE.wait_ge(pe_dn.sem, pe_dn.at(L, "Z", c, lv))
            s = 2 ** lv
            t = M[c]["T"][:, :].rearrange("p (n two e) -> p n two e", two=2, e=s)[:, :, 0]
            VE.tensor_tensor(t, t, CB[c][1][:, 0:256].rearrange("p (n e) -> p n e", e=s),
                             ALU.subtract).then_inc(v_dn.sem, v_dn.mark("T", c, lv))

        def pe_U(L, c, lv):
            pe_turn(L, c, lambda h: hs(M[c]["T"], h), CB[c][0], f"U{lv}", (v_dn, ("T", c, lv)))

        def act_U(L, c, lv):
            SE.wait_ge(pe_dn.sem, pe_dn.at(L, f"U{lv}", c))
            SE.copy(M[c]["U"][:, :], CB[c][0][:, :]).then_inc(a_dn.sem, a_dn.mark("U", c, lv))

        QKB = BA_

        def pe_qk_product(L, c):
            TE.wait_ge(v_conv.sem, v_conv.at(L, "silu", 1))
            TE.wait_ge(a_dn.sem, a_dn.at(L, "kT", c))
            if c:
                TE.wait_ge(a_at.sem, a_at.at(L, "vtok"))
            else:
                TE.wait_ge(v_ba.sem, v_ba.at(L, "kb"))
            for h in range(H):
                mm = TE.matmul(hs(QKB, h), cvt("q", h)[:, tok(c)], hs(M[c]["T"], h), start=True, stop=True)
            mm.then_inc(pe_dn.sem, pe_dn.mark("qk", c))

        def dve_qk(L, c):
            VE.wait_ge(pe_dn.sem, pe_dn.at(L, "qk", c))
            VE.wait_ge(v_dn.sem, v_dn.at(L, "rq"))
            for h in range(H):
                VE.scalar_tensor_tensor(out=hs(M[c]["P"], h), in0=hs(QKB, h), scalar=rkq[:, 40 + 4 * c + h:41 + 4 * c + h],
                                        in1=hs(M[c]["P"], h), op0=ALU.mult, op1=ALU.mult).then_inc(v_dn.sem, v_dn.mark("P", c, h))

        def pe_PT(L, c):
            pe_turn(L, c, lambda h: hs(M[c]["P"], h), QKB, "PT", (v_dn, ("P", c, 3)))

        def act_PT(L, c):
            SE.wait_ge(pe_dn.sem, pe_dn.at(L, "PT", c))
            SE.copy(M[c]["P"][:, :], QKB[:, :]).then_inc(a_dn.sem, a_dn.mark("PT", c))

        def pe_v_turn(L, c):
            TE.wait_ge(v_dn.sem, v_dn.at(L, "T", c, 6))
            pe_turn(L, c, lambda h: cvt("v", h)[:, tok(c)], CB[c][1], "v tok", (v_conv, ("silu", 2)))

        def dve_bV(L, c):
            VE.wait_ge(pe_dn.sem, pe_dn.at(L, "v tok", c))
            VE.tensor_tensor(hd4(M[c]["B"][:, :]), hd4(CB[c][1][:, :]), bc(hbs[:, 4 * c:4 * c + 4], P),
                             ALU.mult).then_inc(v_dn.sem, v_dn.mark("bV", c))
            if c:
                VE.wait_ge(pe_dn.sem, pe_dn.at(L, "U6", c))
                VE.tensor_tensor(hd4(M[c]["T"][:, :]), hd4(M[c]["K"][:, :]), bc(kbs[:, 4 * c:4 * c + 4], P),
                                 ALU.mult).then_inc(v_dn.sem, v_dn.mark("Kb"))
            VE.tensor_tensor(hd4(M[c]["Y"][:, :]), hd4(M[c]["K"][:, :]), bc(eg[:, 8 + 4 * c:12 + 4 * c], P),
                             ALU.mult).then_inc(v_dn.sem, v_dn.mark("Kdec", c))

        def pe_u0(L):
            TE.wait_ge(v_dn.sem, v_dn.at(L, "Kdec", 1))
            TE.wait_ge(a_dn.sem, a_dn.at(L, "U", 0, 6))
            TE.wait_ge(a_dn.sem, a_dn.at(L, "U", 1, 6))
            for h in range(H):
                mm = TE.matmul(hs(CB[0][0], h), hs(M[0]["U"], h), hs(M[0]["B"], h), start=True, stop=True)
            mm.then_inc(pe_dn.sem, pe_dn.mark("u0"))
            for h in range(H):
                mm = TE.matmul(hs(CB[1][1], h), hs(M[1]["T"], h), hs(M[1]["U"], h), start=True, stop=True)
            mm.then_inc(pe_dn.sem, pe_dn.mark("wT"))

        def act_u0(L):
            SE.wait_ge(pe_dn.sem, pe_dn.at(L, "u0"))
            SE.copy(M[0]["K"][:, :], CB[0][0][:, :]).then_inc(a_dn.sem, a_dn.mark("u0"))
            SE.wait_ge(pe_dn.sem, pe_dn.at(L, "wT"))
            SE.activation(M[0]["T"][:, :], CB[1][1][:, :], ACT.Copy, scale=-1.0).then_inc(a_dn.sem, a_dn.mark("wT"))

        def pe_S1(L):
            TE.wait_ge(a_dn.sem, a_dn.at(L, "u0"))
            for h in range(H):
                mm = TE.matmul(hs(CB[0][0], h), hs(M[0]["Y"], h), hs(M[0]["K"], h), start=True, stop=True)
            mm.then_inc(pe_dn.sem, pe_dn.mark("S1"))
            for h in range(H):
                mm = TE.matmul(hs(CB[0][1], h), hs(M[0]["P"], h), hs(M[0]["K"], h), start=True, stop=True)
            mm.then_inc(pe_dn.sem, pe_dn.mark("o0"))

        def act_S1(L):
            SE.wait_ge(pe_dn.sem, pe_dn.at(L, "S1"))
            SE.copy(M[0]["U"][:, :], CB[0][0][:, :]).then_inc(a_dn.sem, a_dn.mark("S1"))

        def dve_o0(L):
            VE.wait_ge(pe_dn.sem, pe_dn.at(L, "o0"))
            VE.tensor_copy(M[0]["B"][:, :], CB[0][1][:, :]).then_inc(v_dn.sem, v_dn.mark("o", 0))

        def pe_u1(L):
            TE.wait_ge(a_dn.sem, a_dn.at(L, "S1"))
            for h in range(H):
                TE.matmul(hs(CB[1][0], h), hs(M[1]["U"], h), hs(M[1]["B"], h), start=True, stop=False)
                mm = TE.matmul(hs(CB[1][0], h), hs(M[0]["T"], h), hs(M[0]["U"], h), start=False, stop=True)
            mm.then_inc(pe_dn.sem, pe_dn.mark("u1"))
            for h in range(H):
                mm = TE.matmul(hs(CB[1][1], h), cvt("q", h)[:, tok(1)], hs(M[0]["U"], h), start=True, stop=True)
            mm.then_inc(pe_dn.sem, pe_dn.mark("qS"))

        def act_u1(L):
            SE.wait_ge(pe_dn.sem, pe_dn.at(L, "u1"))
            SE.copy(M[1]["K"][:, :], CB[1][0][:, :]).then_inc(a_dn.sem, a_dn.mark("u1"))

        def dve_qS(L):
            VE.wait_ge(pe_dn.sem, pe_dn.at(L, "qS"))
            VE.tensor_tensor(hd4(M[0]["P"][:, :]), hd4(CB[1][1][:, :]), bc(rqg[:, 4:8], P),
                             ALU.mult).then_inc(v_dn.sem, v_dn.mark("qS"))

        def pe_o1(L):
            TE.wait_ge(a_dn.sem, a_dn.at(L, "u1"))
            TE.wait_ge(v_dn.sem, v_dn.at(L, "o", 0))
            for h in range(H):
                mm = TE.matmul(hs(CB[0][1], h), hs(M[1]["P"], h), hs(M[1]["K"], h), start=True, stop=True)
            mm.then_inc(pe_dn.sem, pe_dn.mark("o1"))
            for h in range(H):
                mm = TE.matmul(hs(CB[0][0], h), hs(M[1]["Y"], h), hs(M[1]["K"], h), start=True, stop=True)
            mm.then_inc(pe_dn.sem, pe_dn.mark("S2"))

        def dve_o1(L):
            VE.wait_ge(pe_dn.sem, pe_dn.at(L, "o1"))
            VE.wait_ge(v_dn.sem, v_dn.at(L, "qS"))
            VE.tensor_tensor(M[1]["B"][:, :], CB[0][1][:, :], M[0]["P"][:, :], ALU.add).then_inc(v_dn.sem, v_dn.mark("o", 1))
            VE.wait_ge(pe_dn.sem, pe_dn.at(L, "S2"))
            for h in range(H):
                VE.scalar_tensor_tensor(out=hs(M[0]["K"], h), in0=hs(M[0]["U"], h), scalar=eg[:, 20 + h:21 + h],
                                        in1=hs(CB[0][0], h), op0=ALU.mult, op1=ALU.add).then_inc(v_dn.sem, v_dn.mark("S2", h))

        def act_onorm(L, c):
            SE.wait_ge(v_dn.sem, v_dn.at(L, "o", c))
            for h in range(H):
                SE.activation(hs(M[0][("T", "Y")[c]], h), hs(M[c]["B"], h), ACT.Square,
                              accum_out=oss[:, 4 * c + h:4 * c + h + 1]).then_inc(a_dn.sem, a_dn.mark("oss", c, h))

        def dve_onorm(L):
            VE.wait_ge(a_dn.sem, a_dn.at(L, "oss", 1, 3))
            VE.tensor_scalar(ovar[:, :], oss[:, :], 1.0 / DK, EPS, ALU.mult, ALU.add).then_inc(v_dn.sem, v_dn.mark("ovar"))

        def pool_onorm(L):
            GE.wait_ge(v_dn.sem, v_dn.at(L, "ovar"))
            GE.tensor_tensor(orst[:, :], ovar[:, :], mhalf[:, 0:8], ALU.pow).then_inc(g_mix.sem, g_mix.mark("orst"))

        def dve_oscale(L):
            VE.wait_ge(g_mix.sem, g_mix.at(L, "orst"))
            for c in range(2):
                VE.tensor_tensor(hd4(M[c]["B"][:, :]), hd4(M[c]["B"][:, :]), bc(orst[:, 4 * c:4 * c + 4], P),
                                 ALU.mult).then_inc(v_dn.sem, v_dn.mark("on", c))

        def pe_oT(L, c):
            if c == 0:
                TE.wait_ge(a_dn.sem, a_dn.at(L, "u1"))
            else:
                TE.wait_ge(v_dn.sem, v_dn.at(L, "qS"))
            pe_turn(L, c, lambda h: hs(M[c]["B"], h), CB[1][c], "oT", (v_dn, ("on", c)))

        def dve_oT(L, c):
            VE.wait_ge(pe_dn.sem, pe_dn.at(L, "oT", c))
            if c == 0:
                VE.wait_ge(v_gate.sem, v_gate.at(L, "z"))
            z4 = z[:, :].rearrange("p (h t) -> p h t", h=4)
            VE.tensor_tensor(z4[:, :, tok(c)], hd4(CB[1][c][:, :]), z4[:, :, tok(c)],
                             ALU.mult).then_inc(v_dn.sem, v_dn.mark("od", c))

        def act_od(L):
            SE.wait_ge(v_dn.sem, v_dn.at(L, "od", 1))
            SE.wait_ge(v_sd.sem, v_sd.at(L, "od"))
            SE.wait_ge(pe_sd.sem, pe_sd.at(L, "pred"))
            SE.copy(odh[:, :], z[:, :]).then_inc(a_dn.sem, a_dn.mark("odh"))

        def dve_od(L):
            VE.wait_ge(a_dn.sem, a_dn.at(L, "odh"))
            VE.tensor_tensor(odl[:, :], z[:, :], odh[:, :].bitcast(F32), ALU.subtract).then_inc(v_dn.sem, v_dn.mark("odl"))

        def act_z(L):
            SE.wait_ge(win_free.sem, win_free.at(L, 22))
            SE.activation(z_scr, z[:, :], ACT.Tanh, scale=0.5).then_inc(a_gate.sem, a_gate.mark("z"))

        def dve_z(L):
            VE.wait_ge(a_gate.sem, a_gate.at(L, "z"))
            VE.scalar_tensor_tensor(out=z[:, :], in0=z_scr, scalar=1.0, in1=z[:, :], op0=ALU.add,
                                    op1=ALU.mult).then_inc(v_gate.sem, v_gate.mark("z0"))
            VE.wait_ge(v_gate.sem, v_gate.at(L, "z0"))
            VE.tensor_scalar(z[:, :], z[:, :], par[:, C_ONORM:C_ONORM + 1], 0.5, ALU.mult,
                             ALU.mult).then_inc(v_gate.sem, v_gate.mark("z"))

        def act_gate(L, m):
            SE.wait_ge(win_free.sem, win_free.at(L, 22 + 2 * m + 2))
            t = gt[:, 2 * m * N:(2 * m + 2) * N]
            SE.activation(t, t, ACT.Tanh, scale=0.5).then_inc(a_gate.sem, a_gate.mark("gate", m))
        def act_k_sq(L):
            SE.wait_ge(win_free.sem, win_free.at(L, 13))
            SE.activation(k_scr, ak[:, :], ACT.Square).then_inc(a_at.sem, a_at.mark("k sq"))

        def pe_k_rope(L):
            TE.wait_ge(win_free.sem, win_free.at(L, 13))
            TE.matmul(B7[:, 0:N], con[:, K_PERM:K_PERM + P], ak[:, :], start=True, stop=True)
            TE.wait_ge(a_at.sem, a_at.at(L, "k sq"))
            for b, (c0, c1, _, p1) in enumerate(BLK):
                mm = TE.matmul(B7[0:p1, 300 + 2 * b:302 + 2 * b], k_scr[:, c0:c1], con[:, K_BLK2:K_BLK2 + 2],
                               start=True, stop=True)
            mm.then_inc(pe_at.sem, pe_at.mark("k rope"))

        def dve_rope(L, src, out, w, wr, key):
            VE.scalar_tensor_tensor(out=rope_a, in0=src, scalar=par[:, w:w + 1], in1=con[:, K_COS:K_COS + N],
                                    op0=ALU.mult, op1=ALU.mult).then_inc(v_at.sem, v_at.mark("cos", key))
            VE.scalar_tensor_tensor(out=rope_b, in0=B7[:, 0:N], scalar=par[:, wr:wr + 1], in1=con[:, K_SIN:K_SIN + N],
                                    op0=ALU.mult, op1=ALU.mult).then_inc(v_at.sem, v_at.mark("sin", key))
            VE.wait_ge(v_at.sem, v_at.at(L, "sin", key))
            VE.tensor_tensor(out, rope_a, rope_b, ALU.add).then_inc(v_at.sem, v_at.mark("rope", key))

        def dve_k_rope(L):
            VE.wait_ge(pe_at.sem, pe_at.at(L, "k rope"))
            VE.tensor_scalar(avar[:, 0:4], B7[:, 300:304], 1.0 / HEAD_DIM, EPS, ALU.mult, ALU.add).then_inc(v_at.sem, v_at.mark("kv0"))
            VE.tensor_scalar(avar[0:B, 4:6], B7[0:B, 304:306], 1.0 / HEAD_DIM, EPS, ALU.mult, ALU.add).then_inc(v_at.sem, v_at.mark("kvar"))
            dve_rope(L, ak[:, :], kT[:, :], C_KW, C_KWR, "k")

        def pool_k(L):
            GE.wait_ge(v_at.sem, v_at.at(L, "kvar"))
            GE.tensor_tensor(arst[:, :], avar[:, :], mhalf[:, 0:6], ALU.pow).then_inc(g_mix.sem, g_mix.mark("k rsqrt"))

        def pe_k_turn_att(L):
            TE.wait_ge(v_at.sem, v_at.at(L, "rope", "k"))
            TE.wait_ge(a_dn.sem, a_dn.at(L, "PT", 0))
            for b, (c0, c1, _, p1) in enumerate(BLK):
                mm = turn(BA_[0:p1, b * P:(b + 1) * P], kT[:, c0:c1])
            mm.then_inc(pe_at.sem, pe_at.mark("k tok"))

        def dve_k_norm(L):
            VE.wait_ge(pe_at.sem, pe_at.at(L, "k tok"))
            VE.wait_ge(g_mix.sem, g_mix.at(L, "k rsqrt"))
            k3 = ktok[:, 0:2 * P].rearrange("p (g d) -> p g d", d=HEAD_DIM)
            VE.tensor_tensor(k3, BA_[:, 0:2 * P].rearrange("p (g d) -> p g d", d=HEAD_DIM), bc(arst[:, 0:4], HEAD_DIM),
                             ALU.mult).then_inc(v_at.sem, v_at.mark("ktok0"))
            VE.tensor_tensor(ktok[0:B, 2 * P:3 * P].rearrange("p (g d) -> p g d", d=HEAD_DIM),
                             BA_[0:B, 2 * P:3 * P].rearrange("p (g d) -> p g d", d=HEAD_DIM), bc(arst[0:B, 4:6], HEAD_DIM),
                             ALU.mult).then_inc(v_at.sem, v_at.mark("ktok"))

        def pe_k_back(L):
            TE.wait_ge(v_at.sem, v_at.at(L, "ktok"))
            for b, (c0, c1, _, p1) in enumerate(BLK):
                mm = turn(B7[:, c0:c1], ktok[0:p1, b * P:(b + 1) * P])
            mm.then_inc(pe_at.sem, pe_at.mark("kT"))

        def dve_k_back(L):
            VE.wait_ge(pe_at.sem, pe_at.at(L, "kT"))
            VE.tensor_copy(kT[:, :], B7[:, 0:N]).then_inc(v_at.sem, v_at.mark("kT"))

        def pe_v_turn_att(L):
            TE.wait_ge(win_free.sem, win_free.at(L, 14))
            TE.wait_ge(v_at.sem, v_at.at(L, "ktok"))
            for b, (c0, c1, _, p1) in enumerate(BLK):
                mm = turn(BA_[0:p1, b * P:(b + 1) * P], av[:, c0:c1])
            mm.then_inc(pe_at.sem, pe_at.mark("v tok"))

        def act_v_tok(L):
            SE.wait_ge(pe_at.sem, pe_at.at(L, "v tok"))
            SE.copy(vtok[:, 0:2 * P], BA_[:, 0:2 * P]).then_inc(a_at.sem, a_at.mark("vtok0"))
            SE.copy(vtok[0:B, 2 * P:3 * P], BA_[0:B, 2 * P:3 * P]).then_inc(a_at.sem, a_at.mark("vtok"))

        def act_q_sq(L, t):
            SE.wait_ge(win_free.sem, win_free.at(L, 15 + t))
            if t == 0:
                SE.wait_ge(pe_dn.sem, pe_dn.at(L, "stats", "q"))
            SE.activation(sq4[:, t * N:(t + 1) * N], tile_of(aq, t), ACT.Square).then_inc(a_at.sem, a_at.mark("q sq", t))

        def pe_q_rope(L, t):
            TE.wait_ge(win_free.sem, win_free.at(L, 15 + t))
            if t == 0:
                TE.wait_ge(v_at.sem, v_at.at(L, "kT"))
            else:
                TE.wait_ge(v_at.sem, v_at.at(L, "sin", t - 1))
            TE.matmul(B7[:, 0:N], con[:, K_PERM:K_PERM + P], tile_of(aq, t), start=True,
                      stop=True).then_inc(pe_at.sem, pe_at.mark("q rot", t))

        def dve_q_rope(L, t):
            VE.wait_ge(pe_at.sem, pe_at.at(L, "q rot", t))
            VE.wait_ge(v_at.sem, v_at.at(L, "rope", "k" if t == 0 else t - 1))
            VE.wait_ge(a_at.sem, a_at.at(L, "q sq", t))
            dve_rope(L, tile_of(aq, t), tile_of(aq, t), C_QW, C_QWR, t)

        def fence(L, mm, name):
            mm.then_inc(pe_at.sem, pe_at.mark(name))
            TE.wait_ge(pe_at.sem, pe_at.at(L, name))

        def dve_q_sq(L):
            VE.wait_ge(a_at.sem, a_at.at(L, "q sq", 3))
            for kv in range(2):
                half = slice(64 * kv, 64 * kv + 64)
                VE.tensor_copy(qsq[half, 32 * kv:32 * kv + 32].rearrange("p (t b) -> p t b", t=4),
                               sq4.rearrange("p (h t) -> p h t", h=4)[half, :, T:N]).then_inc(v_at.sem, v_at.mark("q sq", kv))

        def pe_q_stats(L):
            TE.wait_ge(v_at.sem, v_at.at(L, "q sq", 1))
            TE.wait_ge(a_at.sem, a_at.at(L, "q sq", 3))
            TE.wait_ge(a_dn.sem, a_dn.at(L, "PT", 1))
            s3 = sq4.rearrange("p (h t) -> p h t", h=4)
            for t in range(4):
                for b in range(2):
                    TE.matmul(BA_[:, 400 + 8 * b + 2 * t:402 + 8 * b + 2 * t], s3[:, t, tok(b)], con[:, K_BLK2:K_BLK2 + 2],
                              start=True, stop=True)
            mm = TE.matmul(BA_[0:64, 65:66], qsq[:, :], one_col, start=True, stop=True)
            mm.then_inc(pe_at.sem, pe_at.mark("q stats"))

        def dve_q_stats(L):
            VE.wait_ge(pe_at.sem, pe_at.at(L, "q stats"))
            VE.tensor_scalar(qvar[:, :], BA_[:, 400:416], 1.0 / HEAD_DIM, EPS, ALU.mult, ALU.add).then_inc(v_at.sem, v_at.mark("qvar"))
            VE.tensor_scalar(svar[0:64, :], BA_[0:64, 65:66], 1.0 / HEAD_DIM, EPS, ALU.mult, ALU.add).then_inc(v_at.sem, v_at.mark("svar"))
            VE.wait_ge(v_at.sem, v_at.at(L, "rope", 3))
            for kv in range(2):
                half = slice(64 * kv, 64 * kv + 64)
                VE.tensor_tensor(prod[half, 32 * kv:32 * kv + 32].rearrange("p (t b) -> p t b", t=4),
                                 aq[:, :].rearrange("p (t n) -> p t n", t=4)[half, :, T:N], bcm(kT[half, T:N], 4),
                                 ALU.mult).then_inc(v_at.sem, v_at.mark("prod", kv))
            VE.wait_ge(g_mix.sem, g_mix.at(L, "q rsqrt"))
            VE.tensor_scalar(rqa[:, :], rqa[:, :], HEAD_DIM ** -0.5, None, ALU.mult).then_inc(v_at.sem, v_at.mark("rqa"))

        def pool_q(L):
            GE.wait_ge(v_at.sem, v_at.at(L, "svar"))
            GE.tensor_tensor(rqa[:, :], qvar[:, :], mhalf[:, 0:16], ALU.pow).then_inc(g_mix.sem, g_mix.mark("q rsqrt"))
            GE.tensor_tensor(srst[0:64, :], svar[0:64, :], mhalf[0:64, 0:1], ALU.pow).then_inc(g_mix.sem, g_mix.mark("s rsqrt"))

        def pe_s_scores(L):
            TE.wait_ge(d_kc.sem, d_kc.at(L, 16))
            TE.wait_ge(v_at.sem, v_at.at(L, "prod", 1))
            q3 = aq[:, :].rearrange("p (t n) -> p t n", t=4)
            for kv in range(2):
                half = slice(64 * kv, 64 * kv + 64)
                if kv:
                    fence(L, mm, "s scores 0")
                for b in range(B):
                    mm = TE.matmul(BA_[:, 32 * kv + b:32 * kv + b + 25:8], kc[half, b * P:(b + 1) * P], q3[half, :, T + b],
                              start=True, stop=True)
            fence(L, mm, "s scores 1")
            mm = TE.matmul(BA_[0:64, 64:65], prod[:, :], one_col, start=True, stop=True)
            mm.then_inc(pe_at.sem, pe_at.mark("s scores"))

        def dve_s_scores(L):
            VE.wait_ge(pe_at.sem, pe_at.at(L, "s scores"))
            VE.tensor_copy(sT[:, :], BA_[:, 0:64]).then_inc(v_at.sem, v_at.mark("sT"))
            VE.wait_ge(g_mix.sem, g_mix.at(L, "s rsqrt"))
            VE.tensor_scalar(sl[0:64, P:P + 1], BA_[0:64, 64:65], srst[0:64, :], HEAD_DIM ** -0.5, ALU.mult,
                             ALU.mult).then_inc(v_at.sem, v_at.mark("s new"))

        def pe_s_turn(L):
            TE.wait_ge(v_at.sem, v_at.at(L, "s new"))
            turn(BA_[0:64, P:2 * P], sT[:, :]).then_inc(pe_at.sem, pe_at.mark("s turn"))

        def dve_s_soft(L):
            VE.wait_ge(pe_at.sem, pe_at.at(L, "s turn"))
            VE.tensor_scalar(sl[0:64, 0:P], BA_[0:64, P:2 * P], srst[0:64, :], HEAD_DIM ** -0.5, ALU.mult,
                             ALU.mult).then_inc(v_at.sem, v_at.mark("sl"))
            VE.wait_ge(v_at.sem, v_at.at(L, "sl"))
            VE.tensor_reduce(smax[0:64, :], sl[0:64, 0:P + 1], AX.X, ALU.max).then_inc(v_at.sem, v_at.mark("smax"))
            VE.wait_ge(v_at.sem, v_at.at(L, "smax"))
            VE.tensor_scalar(snm[0:64, :], smax[0:64, :], par[0:64, C_SINKROW:C_SINKROW + 1], -1.0, ALU.max,
                             ALU.mult).then_inc(v_at.sem, v_at.mark("snm"))

        def act_s_soft(L):
            SE.wait_ge(v_at.sem, v_at.at(L, "snm"))
            SE.activation(sl[0:64, 0:P + 1], sl[0:64, 0:P + 1], ACT.Exp, bias=snm[0:64, :],
                          accum_out=sden[0:64, :]).then_inc(a_at.sem, a_at.mark("s exp"))
            SE.activation(sesk[0:64, :], par[0:64, C_SINKROW:C_SINKROW + 1], ACT.Exp,
                          bias=snm[0:64, :]).then_inc(a_at.sem, a_at.mark("s sink"))

        def dve_s_probs(L):
            VE.wait_ge(a_at.sem, a_at.at(L, "s sink"))
            VE.tensor_tensor(sden[0:64, :], sden[0:64, :], sesk[0:64, :], ALU.add).then_inc(v_at.sem, v_at.mark("sden"))
            VE.wait_ge(v_at.sem, v_at.at(L, "sden"))
            VE.reciprocal(srec[0:64, :], sden[0:64, :]).then_inc(v_at.sem, v_at.mark("srec"))
            VE.wait_ge(v_at.sem, v_at.at(L, "srec"))
            VE.tensor_scalar(sl[0:64, 0:P + 1], sl[0:64, 0:P + 1], srec[0:64, :], None, ALU.mult).then_inc(v_at.sem, v_at.mark("probs"))
            VE.wait_ge(v_at.sem, v_at.at(L, "probs"))
            VE.tensor_scalar(rmat[0:64, :], con[0:64, K_MROW:K_MROW + 32], sl[0:64, P:P + 1], None,
                             ALU.mult).then_inc(v_at.sem, v_at.mark("rmat"))

        def pe_s_probs(L):
            TE.wait_ge(v_at.sem, v_at.at(L, "rmat"))
            turn(BA_[:, 256:320], sl[0:64, 0:P])
            TE.matmul(BA_[:, 320:352], con[0:64, K_SEL:K_SEL + P], rmat[0:64, :], start=True,
                      stop=True).then_inc(pe_at.sem, pe_at.mark("s probs"))

        def dve_s_new(L):
            VE.wait_ge(pe_at.sem, pe_at.at(L, "s probs"))
            VE.tensor_copy(pts[:, :], BA_[:, 256:320]).then_inc(v_at.sem, v_at.mark("pts"))
            VE.tensor_tensor(pvs[:, :].rearrange("p (t b) -> p t b", t=4), BA_[:, 320:352].rearrange("p (t b) -> p t b", t=4),
                             bcm(av[:, T:N], 4), ALU.mult).then_inc(v_at.sem, v_at.mark("pvs"))

        def pe_s_pv(L):
            TE.wait_ge(d_vc.sem, d_vc.at(L, 16))
            TE.wait_ge(v_at.sem, v_at.at(L, "pvs"))
            for kv in range(2):
                half = slice(64 * kv, 64 * kv + 64)
                for b in range(B):
                    mm = TE.matmul(BA_[half, 352 + b:352 + b + 25:8], vc[:, b * P + 64 * kv:b * P + 64 * kv + 64],
                                   pts[:, 32 * kv + b:32 * kv + b + 25:8], start=True, stop=True)
            mm.then_inc(pe_at.sem, pe_at.mark("s pv"))

        def dve_s_pv(L):
            VE.wait_ge(pe_at.sem, pe_at.at(L, "s pv"))
            VE.tensor_tensor(oas[:, :], BA_[:, 352:384], pvs[:, :], ALU.add).then_inc(v_at.sem, v_at.mark("oas"))

        def pe_scores(L, n):
            t, kv = n // 2, n % 2
            half, bk = slice(64 * kv, 64 * kv + 64), banks[6 + n % 2]
            if n >= 2:
                TE.wait_ge(a_at.sem, a_at.at(L, "otok", n - 2))
            elif n == 1:
                TE.wait_ge(v_at.sem, v_at.at(L, "rope", 3))
                TE.wait_ge(v_dn.sem, v_dn.at(L, "ss", "q"))
            else:
                TE.wait_ge(v_at.sem, v_at.at(L, "oas"))
            q = tile_of(aq, t)
            TE.matmul(bk[:, 0:P], q[half, 0:P], kT[half, 0:P], start=True, stop=True)
            TE.matmul(bk[:, P:3 * P], q[half, P:T], kT[half, 0:T], start=True,
                      stop=True).then_inc(pe_at.sem, pe_at.mark("scores", n))

        def dve_scores(L, n):
            VE.wait_ge(pe_at.sem, pe_at.at(L, "scores", n))
            if n >= 2:
                VE.wait_ge(pe_at.sem, pe_at.at(L, "probs", n - 2))
            s, bk = sm[n % 2], banks[6 + n % 2]
            for b, (lo, hi, m) in enumerate(((0, P, K_AM0), (P, 3 * P, K_AM1))):
                VE.scalar_tensor_tensor(out=s[:, lo:hi], in0=bk[:, lo:hi], scalar=rqa[:, 8 * b + n:8 * b + n + 1],
                                        in1=con[:, m:m + hi - lo], op0=ALU.mult, op1=ALU.add).then_inc(v_at.sem, v_at.mark("logits", n, b))
            for b, (lo, hi) in enumerate(((0, P), (P, 3 * P))):
                VE.wait_ge(v_at.sem, v_at.at(L, "logits", n, b))
                VE.tensor_reduce(mx[:, 8 * b + n:8 * b + n + 1], s[:, lo:hi], AX.X, ALU.max).then_inc(v_at.sem, v_at.mark("max", n, b))
            VE.wait_ge(v_at.sem, v_at.at(L, "max", n, 1))
            VE.tensor_scalar(nm[:, n:n + 9:8], mx[:, n:n + 9:8], par[:, C_SINK + n:C_SINK + n + 1], -1.0, ALU.max,
                             ALU.mult).then_inc(v_at.sem, v_at.mark("nm", n))

        def act_exp(L, n):
            SE.wait_ge(v_at.sem, v_at.at(L, "nm", n))
            for b, (lo, hi) in enumerate(((0, P), (P, 3 * P))):
                SE.activation(sm[n % 2][:, lo:hi], sm[n % 2][:, lo:hi], ACT.Exp, bias=nm[:, 8 * b + n:8 * b + n + 1],
                              accum_out=den[:, 8 * b + n:8 * b + n + 1]).then_inc(a_at.sem, a_at.mark("exp", n, b))

        def pe_probs(L, n):
            TE.wait_ge(a_at.sem, a_at.at(L, "exp", n, 1))
            for j in range(3):
                mm = TE.transpose(banks[6 + n % 2][:, j * P:(j + 1) * P], sm[n % 2][:, j * P:(j + 1) * P], ident)
            mm.then_inc(pe_at.sem, pe_at.mark("probs", n))

        def act_probs(L, n):
            SE.wait_ge(pe_at.sem, pe_at.at(L, "probs", n))
            if n >= 2:
                SE.wait_ge(pe_at.sem, pe_at.at(L, "pv", n - 2))
            SE.copy(ptb[n % 2], banks[6 + n % 2][:, 0:3 * P]).then_inc(a_at.sem, a_at.mark("probs", n))

        def pe_pv(L, n):
            kv, bk, p = n % 2, banks[6 + n % 2], ptb[n % 2]
            TE.wait_ge(a_at.sem, a_at.at(L, "probs", n))
            d = slice(64 * kv, 64 * kv + 64)
            TE.matmul(bk[:, 384:448], p[:, 0:P], vtok[:, 0:P][:, d], start=True, stop=True)
            TE.matmul(bk[:, 448:512], p[:, P:2 * P], vtok[:, 0:P][:, d], start=True, stop=False)
            TE.matmul(bk[:, 448:512], p[:, 2 * P:3 * P], vtok[:, P:2 * P][:, d], start=False,
                      stop=True).then_inc(pe_at.sem, pe_at.mark("pv", n))

        def act_pv(L, n):
            SE.wait_ge(pe_at.sem, pe_at.at(L, "pv", n))
            SE.copy(otok[:, :].rearrange("p (b c) -> p b c", b=2)[:, :, 64 * n:64 * n + 64],
                    banks[6 + n % 2][:, 384:512].rearrange("p (b c) -> p b c", b=2)).then_inc(a_at.sem, a_at.mark("otok", n))

        def dve_den(L):
            VE.wait_ge(v_at.sem, v_at.at(L, "nm", 7))
            VE.tensor_tensor(esk[:, :].rearrange("p (b n) -> p b n", b=2), nm[:, :].rearrange("p (b n) -> p b n", b=2),
                             bcm(par[:, C_SINK:C_SINK + 8], 2), ALU.add).then_inc(v_at.sem, v_at.mark("esk"))
            VE.wait_ge(a_at.sem, a_at.at(L, "sink"))
            VE.tensor_tensor(den[:, :], den[:, :], esk[:, :], ALU.add).then_inc(v_at.sem, v_at.mark("den"))
            VE.wait_ge(v_at.sem, v_at.at(L, "den"))
            VE.reciprocal(rec[:, :], den[:, :]).then_inc(v_at.sem, v_at.mark("rec"))
            VE.wait_ge(v_at.sem, v_at.at(L, "rec"))
            VE.wait_ge(a_at.sem, a_at.at(L, "otok", 7))
            for b in range(2):
                o3 = otok[:, 512 * b:512 * b + 512].rearrange("p (n d) -> p n d", d=HEAD_DIM)
                VE.tensor_tensor(o3, o3, bc(rec[:, 8 * b:8 * b + 8], HEAD_DIM), ALU.mult).then_inc(v_at.sem, v_at.mark("on", b))

        def act_sink(L):
            SE.wait_ge(v_at.sem, v_at.at(L, "esk"))
            SE.activation(esk[:, :], esk[:, :], ACT.Exp).then_inc(a_at.sem, a_at.mark("sink"))

        def pe_o_turn(L):
            for b in range(2):
                TE.wait_ge(v_at.sem, v_at.at(L, "on", b))
                for t in range(4):
                    mm = TE.transpose(banks[6 + b][:, t * P:(t + 1) * P], otok[:, 512 * b + t * P:512 * b + (t + 1) * P], ident)
                mm.then_inc(pe_at.sem, pe_at.mark("oT", b))

        def act_oa(L):
            h3 = oah[:, :].rearrange("p (t n) -> p t n", t=4)
            for b in range(2):
                SE.wait_ge(pe_at.sem, pe_at.at(L, "oT", b))
                SE.copy(h3[:, :, tok(b)], banks[6 + b][:, :].rearrange("p (t n) -> p t n", t=4)).then_inc(a_at.sem, a_at.mark("oah", b))
            SE.copy(h3[:, :, T:N], oas[:, :].rearrange("p (t b) -> p t b", t=4)).then_inc(a_at.sem, a_at.mark("oah", 2))

        def dve_oa(L):
            h3 = oah[:, :].rearrange("p (t n) -> p t n", t=4).bitcast(F32)
            l3 = oal[:, :].rearrange("p (t n) -> p t n", t=4)
            for b in range(2):
                VE.wait_ge(a_at.sem, a_at.at(L, "oah", b))
                VE.tensor_tensor(l3[:, :, tok(b)], banks[6 + b][:, :].rearrange("p (t n) -> p t n", t=4), h3[:, :, tok(b)],
                                 ALU.subtract).then_inc(v_at.sem, v_at.mark("oal", b))
            VE.wait_ge(a_at.sem, a_at.at(L, "oah", 2))
            VE.tensor_tensor(l3[:, :, T:N], oas[:, :].rearrange("p (t b) -> p t b", t=4), h3[:, :, T:N],
                             ALU.subtract).then_inc(v_at.sem, v_at.mark("oal", 2))

        def state(h, b):
            return (states, states2)[h // 2][:, (h % 2) * B * P + b * P:(h % 2) * B * P + (b + 1) * P]

        def col16(t, r):
            return t[:, 16 * r:16 * r + 16]

        def dve_qk_sample(L):
            VE.wait_ge(v_dn.sem, v_dn.at(L, "sample", "q"))
            VE.tensor_tensor(qkp[:, :], kq2[:, 0:32], kq2[:, 32:64], ALU.mult).then_inc(v_sd.sem, v_sd.mark("qkp"))

        def pe_pred(L, r):
            SDB = banks[3]
            if r == 0:
                TE.wait_ge(v_dn.sem, v_dn.at(L, "S2", 3))
                TE.wait_ge(v_sd.sem, v_sd.at(L, "qkp"))
                TE.matmul(SDB[:, 64:96], ones, qkp[:, :], start=True, stop=True)
            else:
                TE.wait_ge(v_sd.sem, v_sd.at(L, "S", 0, 7))
            TE.wait_ge(d_state[r].sem, d_state[r].at(L, 16))
            k3 = kq2[:, :].rearrange("p (v s) -> p v s", v=2)
            for h in (2 * r, 2 * r + 1):
                for b in range(B):
                    s = 8 * h + b
                    mm = TE.matmul(SDB[:, 2 * s:2 * s + 2], state(h, b), k3[:, :, s], start=True, stop=True)
            mm.then_inc(pe_sd.sem, pe_sd.mark("pred", r))

        def dve_delta(L, r):
            SDB = banks[3]
            VE.wait_ge(pe_sd.sem, pe_sd.at(L, "pred", r))
            if r == 0:
                VE.tensor_copy(qkb[:, :], SDB[:, 64:96]).then_inc(v_sd.sem, v_sd.mark("qkb"))
            pr = SDB[:, 32 * r:32 * r + 32].rearrange("p (s v) -> p s v", v=2)
            a, bt_, d, t = col16(abc, r), abc[:, 32 + 16 * r:48 + 16 * r], col16(dlt, r), col16(tmp32, r)
            VE.tensor_tensor(d, pr[:, :, 0], a, ALU.mult).then_inc(v_sd.sem, v_sd.mark("a pk", r))
            VE.tensor_tensor(t, pr[:, :, 1], a, ALU.mult).then_inc(v_sd.sem, v_sd.mark("a pq", r))
            VE.wait_ge(v_sd.sem, v_sd.at(L, "a pk", r))
            v2 = cv4("v")[:, 2 * r:2 * r + 2, T:N]
            VE.scalar_tensor_tensor(out=d.rearrange("p (h b) -> p h b", h=2), in0=v2, scalar=0.5,
                                    in1=d.rearrange("p (h b) -> p h b", h=2), op0=ALU.mult,
                                    op1=ALU.subtract).then_inc(v_sd.sem, v_sd.mark("v-", r))
            VE.wait_ge(v_sd.sem, v_sd.at(L, "v-", r))
            VE.tensor_tensor(d, d, bt_, ALU.mult).then_inc(v_sd.sem, v_sd.mark("delta", r))
            VE.wait_ge(v_sd.sem, v_sd.at(L, "delta", r))
            VE.tensor_tensor(col16(osq, r), col16(qkb, r), d, ALU.mult).then_inc(v_sd.sem, v_sd.mark("qk d", r))
            VE.wait_ge(v_sd.sem, v_sd.at(L, "qk d", r))
            VE.tensor_tensor(t, t, col16(osq, r), ALU.add).then_inc(v_sd.sem, v_sd.mark("o", r))
            if r:
                VE.wait_ge(v_sd.sem, v_sd.at(L, "o", 1))
                VE.tensor_tensor(osq[:, :], tmp32[:, :], tmp32[:, :], ALU.mult).then_inc(v_sd.sem, v_sd.mark("o sq"))

        def pe_rows(L, r):
            TE.wait_ge(v_sd.sem, v_sd.at(L, "delta", r))
            if r:
                TE.wait_ge(v_sd.sem, v_sd.at(L, "S", 0, 7))
            for j in range(2):
                s = 8 * (2 * r + j)
                turn(hs(banks[2][0:B, :], j), dlt[:, s:s + B])
                mm = turn(hs(banks[2][0:B, :], 2 + j), kq2[:, s:s + B])
            mm.then_inc(pe_sd.sem, pe_sd.mark("rows", r))

        def act_rows(L, r):
            SE.wait_ge(pe_sd.sem, pe_sd.at(L, "rows", r))
            if r:
                SE.wait_ge(d_kv.sem, d_kv.at(L, 64))
            SE.copy((rows0, rows1)[r][0:B, :], banks[2][0:B, :]).then_inc(a_sd.sem, a_sd.mark("rows", r))

        def drow(h):
            return (otok, smx)[h % 2][0:B, 0:B * P]

        def dve_drow(L, h):
            r, j = h // 2, h % 2
            VE.wait_ge(a_sd.sem, a_sd.at(L, "rows", r))
            if h == 0:
                VE.wait_ge(pe_at.sem, pe_at.at(L, "oT", 1))
            if r:
                VE.wait_ge(pe_sd.sem, pe_sd.at(L, "outer", h - 2))
            d = (rows0, rows1)[r][0:B, P * j:P * j + P]
            VE.tensor_tensor(drow(h).rearrange("p (b e) -> p b e", b=B), bcm(d, B), bc(con[0:B, K_ID:K_ID + B], P),
                             ALU.mult).then_inc(v_sd.sem, v_sd.mark("drow", h))

        def outer_banks(h):
            return ((banks[2], banks[3]), (banks[4], banks[5]))[h % 2]

        def pe_outer(L, h):
            r, j = h // 2, h % 2
            TE.wait_ge(v_sd.sem, v_sd.at(L, "drow", h))
            if h == 0:
                TE.wait_ge(v_sd.sem, v_sd.at(L, "o", 0))
            if h == 1:
                TE.wait_ge(v_dn.sem, v_dn.at(L, "od", 1))
            if h == 2:
                TE.wait_ge(v_sd.sem, v_sd.at(L, "osv"))
            if h == 3:
                TE.wait_ge(v_sd.sem, v_sd.at(L, "S", 1, 7))
            krow = (rows0, rows1)[r][0:B, P * (2 + j):P * (3 + j)]
            for n in range(2):
                mm = TE.matmul(outer_banks(h)[n][:, :], krow, drow(h)[:, 512 * n:512 * n + 512], start=True, stop=True)
            mm.then_inc(pe_sd.sem, pe_sd.mark("outer", h))

        def dve_state(L, h):
            VE.wait_ge(pe_sd.sem, pe_sd.at(L, "outer", h))
            for b in range(B):
                s = 8 * h + b
                VE.scalar_tensor_tensor(out=state(h, b), in0=state(h, b), scalar=abc[:, s:s + 1],
                                        in1=hs(outer_banks(h)[b // 4], b % 4), op0=ALU.mult,
                                        op1=ALU.add).then_inc(v_sd.sem, v_sd.mark("S", h, b))

        def act_state_out(L, h):
            SE.wait_ge(v_sd.sem, v_sd.at(L, "S", h, 7))
            o = h * B * P
            SE.dma_start(outs["dns"][L, :, o:o + B * P], (states, states2)[h // 2][:, (h % 2) * B * P:(h % 2 + 1) * B * P]
                         ).then_inc(d_stout.sem, 16)

        def pe_onorm(L):
            TE.wait_ge(v_sd.sem, v_sd.at(L, "o sq"))
            TE.matmul(banks[3][:, 128:160], ones, osq[:, :], start=True, stop=True).then_inc(pe_sd.sem, pe_sd.mark("oss"))

        def dve_onorm_sample(L):
            VE.wait_ge(pe_sd.sem, pe_sd.at(L, "oss"))
            VE.tensor_scalar(osv[:, :], banks[3][:, 128:160], 1.0 / DK, EPS, ALU.mult, ALU.add).then_inc(v_sd.sem, v_sd.mark("osv"))

        def pool_onorm_sample(L):
            GE.wait_ge(v_sd.sem, v_sd.at(L, "osv"))
            GE.tensor_tensor(osr[:, :], osv[:, :], mhalf[:, 0:32], ALU.pow).then_inc(g_mix.sem, g_mix.mark("osr"))

        def dve_od_sample(L):
            VE.wait_ge(g_mix.sem, g_mix.at(L, "osr"))
            VE.tensor_tensor(tmp32[:, :], tmp32[:, :], osr[:, :], ALU.mult).then_inc(v_sd.sem, v_sd.mark("on"))
            VE.wait_ge(v_sd.sem, v_sd.at(L, "on"))
            z3 = z[:, :].rearrange("p (h t) -> p h t", h=4)[:, :, T:N]
            VE.tensor_tensor(z3, z3, tmp32[:, :].rearrange("p (h b) -> p h b", h=4),
                             ALU.mult).then_inc(v_sd.sem, v_sd.mark("od"))

        def pe_branches(L, m):
            u, t0 = U_AD + m // 2, KT * (m % 2)
            if m % 2 == 0:
                wait_unit(L, u)
            if m == 0:
                TE.wait_ge(v_at.sem, v_at.at(L, "oal", 2))
                TE.wait_ge(win_free.sem, win_free.at(L, 38))
            if m >= 2:
                TE.wait_ge(v_ad.sem, v_ad.at(L, "d", m - 2))
            for t in range(4):
                mm = product(banks[m % 2][:, 0:N], u % RING, t0 + t, tile_of(oah, t), tile_of(oal, t), t == 0, t == 3)
            mm.then_inc(pe_ad.sem, pe_ad.mark("a", m))
            if m == 0:
                TE.wait_ge(v_dn.sem, v_dn.at(L, "odl"))
            for t in range(4):
                mm = product(banks[6 + m % 2][:, 0:N], u % RING, t0 + 4 + t, tile_of(odh, t), tile_of(odl, t), t == 0, t == 3)
            if m % 2:
                mm.then_inc(w_used.sem, 1)
            else:
                mm.then_inc(pe_ad.sem, pe_ad.mark("d", m))

        def dve_branches(L, m):
            ga, gd = tile_of(gt, 2 * m), tile_of(gt, 2 * m + 1)
            VE.wait_ge(a_gate.sem, a_gate.at(L, "gate", m))
            VE.wait_ge(pe_ad.sem, pe_ad.at(L, "a", m))
            VE.scalar_tensor_tensor(out=ga, in0=ga, scalar=1.0, in1=banks[m % 2][:, 0:N], op0=ALU.add,
                                    op1=ALU.mult).then_inc(v_ad.sem, v_ad.mark("a", m))
            if m % 2:
                VE.wait_ge(w_used.sem, w_used.at(L, U_AD + m // 2 + 1))
            else:
                VE.wait_ge(pe_ad.sem, pe_ad.at(L, "d", m))
            VE.scalar_tensor_tensor(out=gd, in0=gd, scalar=1.0, in1=banks[6 + m % 2][:, 0:N], op0=ALU.add,
                                    op1=ALU.mult).then_inc(v_ad.sem, v_ad.mark("d", m))
            VE.wait_ge(v_ad.sem, v_ad.at(L, "d", m))
            VE.tensor_tensor(ga, ga, gd, ALU.add).then_inc(v_ad.sem, v_ad.mark("mix", m))

        def act_branches(L, m):
            SE.wait_ge(v_ad.sem, v_ad.at(L, "mix", m))
            SE.copy(tile_of(mixh, m), tile_of(gt, 2 * m)).then_inc(a_ad.sem, a_ad.mark("mixh", m))

        def dve_mix_tail(L, m):
            VE.wait_ge(a_ad.sem, a_ad.at(L, "mixh", m))
            VE.tensor_tensor(tile_of(mixl, m), tile_of(gt, 2 * m), tile_of(mixh, m).bitcast(F32),
                             ALU.subtract).then_inc(v_ad.sem, v_ad.mark("mixl", m))

        def pe_out(L, m):
            u, t0 = U_WO + m // 2, KT * (m % 2)
            if m % 2 == 0:
                wait_unit(L, u)
            if m < 2:
                TE.wait_ge(v_ad.sem, v_ad.at(L, "d", 7))
            else:
                TE.wait_ge(x_done.sem, x_done.at(L, 8 + m - 1))
            for k in range(KT):
                if m == 0:
                    TE.wait_ge(v_ad.sem, v_ad.at(L, "mixl", k))
                mm = product(banks[0 if m % 2 else 7][:, 0:N], u % RING, t0 + k, tile_of(mixh, k), tile_of(mixl, k),
                             k == 0, k == KT - 1)
            mm.then_inc(w_used.sem if m % 2 else out_ready.sem, 1)

        LEV0, LEV1 = 24, 36

        def pe_slot(L, s):
            if s == 1:
                pe_ba_turn(L)
            if s == 6:
                pe_decays(L)
            if s == 9:
                pe_decay(L, 0)
            if s == 13:
                pe_stats(L, "k")
                pe_k_turn(L, 0)
            if s == 15:
                pe_kT(L, 0)
            if s == 16:
                pe_kk(L, 0)
            if s == 18:
                pe_B(L, 0)
            if s == 20:
                pe_stats(L, "q")
            if s == 21:
                pe_qk_product(L, 0)
            if s == 22:
                pe_PT(L, 0)
            if s == 23:
                pe_T0(L, 0)
            for c, s0 in ((0, LEV0), (1, LEV1)):
                if s0 <= s < s0 + 18:
                    (pe_Y, pe_Z, pe_U)[(s - s0) % 3](L, c, (s - s0) // 3 + 1)
            if s == 26:
                pe_k_rope(L)
            if s == 28:
                pe_k_turn_att(L)
                pe_decay(L, 1)
            if s == 29:
                pe_k_turn(L, 1)
            if s == 30:
                pe_k_back(L)
            if s == 31:
                pe_kT(L, 1)
                pe_v_turn_att(L)
            if s == 32:
                pe_kk(L, 1)
                pe_q_rope(L, 0)
            if s == 33:
                pe_qk_product(L, 1)
                pe_B(L, 1)
            if s == 34:
                pe_PT(L, 1)
                pe_q_rope(L, 1)
            if s == 35:
                pe_T0(L, 1)
            if s == 36:
                pe_q_rope(L, 2)
            if s == 38:
                pe_q_rope(L, 3)
            if s == 40:
                pe_q_stats(L)
            if s == 42:
                pe_v_turn(L, 0)
                pe_s_scores(L)
            if s == 43:
                pe_s_turn(L)
            if s == 46:
                pe_s_probs(L)
            if s == 47:
                pe_s_pv(L)
            for n in range(8):
                if s == 49 + 2 * n:
                    pe_scores(L, n)
                if s == 51 + 2 * n:
                    pe_probs(L, n)
                if s == 52 + 2 * n:
                    pe_pv(L, n)
            if s == 54:
                pe_v_turn(L, 1)
            if s == 56:
                pe_u0(L)
            if s == 57:
                pe_S1(L)
            if s == 58:
                pe_u1(L)
            if s == 60:
                pe_o1(L)
            if s == 62:
                pe_pred(L, 0)
            if s == 64:
                pe_rows(L, 0)
            if s == 65:
                pe_oT(L, 0)
                pe_oT(L, 1)
            if s == 69:
                pe_o_turn(L)
            if s == 71:
                pe_outer(L, 0)
            if s == 72:
                pe_outer(L, 1)
            if s == 74:
                pe_pred(L, 1)
            if s == 75:
                pe_rows(L, 1)
                pe_onorm(L)

        def dve_slot(L, s):
            if s == 1:
                dve_ba(L)
            if s == 6:
                dve_decays(L)
            if s == 7:
                dve_decay_lhs(L, 0)
            if s == 10:
                dve_silu(L, 0)
                dve_decay(L, 0)
            if s == 13:
                dve_stats(L, "k")
                dve_kn(L, 0)
                dve_sample_kq(L, "k")
            if s == 16:
                dve_A(L, 0)
            if s == 18:
                dve_silu(L, 1)
                dve_U0(L, 0)
            if s == 20:
                dve_stats(L, "q")
            if s == 21:
                dve_sample_kq(L, "q")
                dve_qk(L, 0)
            for c, s0 in ((0, LEV0), (1, LEV1)):
                if s0 <= s < s0 + 18 and (s - s0) % 3 < 2:
                    (dve_Y, dve_Z)[(s - s0) % 3](L, c, (s - s0) // 3 + 1)
            if s == 26:
                dve_silu(L, 2)
                dve_k_rope(L)
            if s == 27:
                dve_decay_lhs(L, 1)
            if s == 28:
                dve_k_norm(L)
                dve_decay(L, 1)
            if s == 29:
                dve_kn(L, 1)
            if s == 30:
                dve_k_back(L)
            if s == 32:
                dve_q_rope(L, 0)
                dve_A(L, 1)
            if s == 33:
                dve_qk(L, 1)
                dve_U0(L, 1)
            if s == 34:
                dve_q_rope(L, 1)
            if s == 36:
                dve_q_rope(L, 2)
            if s == 38:
                dve_q_rope(L, 3)
            if s == 39:
                dve_q_sq(L)
            if s == 40:
                dve_q_stats(L)
            if s == 42:
                dve_bV(L, 0)
                dve_s_scores(L)
            if s == 43:
                dve_s_soft(L)
            if s == 44:
                dve_z(L)
            if s == 45:
                dve_s_probs(L)
            if s == 46:
                dve_s_new(L)
            if s == 47:
                dve_s_pv(L)
            for n in range(8):
                if s == 49 + 2 * n:
                    dve_scores(L, n)
            if s == 54:
                dve_bV(L, 1)
                dve_qk_sample(L)
            if s == 57:
                dve_o0(L)
            if s == 58:
                dve_qS(L)
            if s == 60:
                dve_o1(L)
            if s == 62:
                dve_delta(L, 0)
                dve_onorm(L)
                dve_oscale(L)
            if s == 65:
                dve_oT(L, 0)
                dve_oT(L, 1)
            if s == 67:
                dve_den(L)
            if s == 69:
                dve_oa(L)
                dve_drow(L, 0)
                dve_drow(L, 1)
            if s == 71:
                dve_state(L, 0)
            if s == 72:
                dve_state(L, 1)
            if s == 74:
                dve_delta(L, 1)
            if s == 75:
                dve_onorm_sample(L)
                dve_od_sample(L)

        def act_slot(L, s):
            if s == 1:
                act_ba(L)
            if s == 6:
                act_decays(L)
            if s == 9:
                act_conv(L, 0)
                act_decay(L, 0)
            if s == 11:
                act_conv_sq(L, 0)
            if s == 15:
                act_kT(L, 0)
            if s == 17:
                act_conv(L, 1)
            if s == 18:
                act_B(L, 0)
            if s == 19:
                act_conv_sq(L, 1)
            if s == 22:
                act_PT(L, 0)
            if s == 23:
                act_T0(L, 0)
            if s == 24:
                act_conv_out(L)
            if s == 25:
                act_conv(L, 2)
                act_k_sq(L)
            for c, s0 in ((0, LEV0), (1, LEV1)):
                if s0 <= s < s0 + 18 and (s - s0) % 3 == 2:
                    act_U(L, c, (s - s0) // 3 + 1)
            if s == 28:
                act_decay(L, 1)
            if s == 31:
                act_kT(L, 1)
                act_v_tok(L)
                act_q_sq(L, 0)
            if s == 33:
                act_B(L, 1)
                act_q_sq(L, 1)
            if s == 34:
                act_PT(L, 1)
                act_kv_out(L)
            if s == 35:
                act_T0(L, 1)
                act_q_sq(L, 2)
            if s == 37:
                act_q_sq(L, 3)
            if s == 43:
                act_s_soft(L)
                act_z(L)
            if s == 47:
                act_states_in(L, 0)
            for n in range(8):
                if s == 49 + 2 * n:
                    act_exp(L, n)
                if s == 51 + 2 * n:
                    act_probs(L, n)
                if s == 52 + 2 * n:
                    act_pv(L, n)
            if s == 56:
                act_u0(L)
            if s == 57:
                act_S1(L)
            if s == 58:
                act_u1(L)
            if s == 60:
                act_onorm(L, 0)
                act_onorm(L, 1)
            if s == 64:
                act_s2_out(L)
                act_rows(L, 0)
            if s == 65:
                act_states_in(L, 1)
            if s == 67:
                act_sink(L)
            if s == 69:
                act_oa(L)
            if s >= 49 and s % 4 == 1 and (s - 49) // 4 < 7:
                act_gate(L, (s - 49) // 4)
            if s == 75:
                act_gate(L, 7)
                act_rows(L, 1)
                act_od(L)

        def pool_slot(L, s):
            if s in (8, 16, 24):
                pool_conv(L, (s - 8) // 8)
            if s == 13:
                pool_stats(L, "k")
            if s == 20:
                pool_stats(L, "q")
            if s == 27:
                pool_k(L)
            if s == 40:
                pool_q(L)
            if s == 62:
                pool_onorm(L)
            if s == 75:
                pool_onorm_sample(L)

        def act_loads(L):
            SE.dma_start(cst[:, :], ins["cst"][L, :, :]).then_inc(d_cst.sem, 16)
            SE.dma_start(kc[:, :], ins["kct"][L, :, :]).then_inc(d_kc.sem, 16)
            SE.dma_start(vc[:, :], ins["vct"][L, :, :]).then_inc(d_vc.sem, 16)

        def act_conv_out(L):
            raw3 = craw[:, :].rearrange("p (c w) -> p c w", c=12)
            SE.wait_ge(win_free.sem, win_free.at(L, 12))
            SE.dma_start(outs["convp"][L, :, :].rearrange("p (c t) -> p c t", c=12), raw3[:, :, T:T + 3]).then_inc(d_conv.sem, 16)
            o4 = outs["convs"][L, :, :].rearrange("p (c t) -> p c t", c=12)
            SE.dma_start(o4[:, :, 16:24], raw3[:, :, T + 3:CW]).then_inc(d_conv.sem, 16)
            SE.dma_start(o4[:, :, 0:16], cst[:, :].rearrange("p (c t) -> p c t", c=12)[:, :, 8:24]).then_inc(d_conv.sem, 16)

        def act_kv_out(L):
            SE.wait_ge(v_at.sem, v_at.at(L, "ktok"))
            SE.wait_ge(a_at.sem, a_at.at(L, "vtok"))
            for name, t in (("k", ktok), ("v", vtok)):
                SE.dma_start(outs[name + "p"][L, :, :], t[:, P:2 * P]).then_inc(d_kv.sem, 16)
                SE.dma_start(outs[name + "s"][L, :, WINDOW - 1, :], t[0:B, 2 * P:3 * P]).then_inc(d_kv.sem, 16)

        def act_states_in(L, r):
            if r == 0:
                SE.wait_ge(pe_at.sem, pe_at.at(L, "s pv"))
            else:
                SE.wait_ge(pe_dn.sem, pe_dn.at(L, "oT", 0))
            SE.dma_start((states, states2)[r][:, :], ins["states"][L, :, r * 2 * B * P:(r + 1) * 2 * B * P]
                         ).then_inc(d_state[r].sem, 16)

        def act_s2_out(L):
            SE.wait_ge(v_dn.sem, v_dn.at(L, "S2", 3))
            SE.dma_start(outs["dnp"][L, :, :], M[0]["K"][:, :]).then_inc(d_s2.sem, 16)

        def act_out_done(L):
            for s in (d_conv, d_kv, d_s2, d_stout):
                SE.wait_ge(s.sem, s.at(L, s.per_layer))

        def pe_mix(L):
            pe_ba_product(L)
            for i in range(W_IN_TILES):
                if i == 0:
                    pe_win(L, 0, lambda: (pe_sums(L, 1), pe_spread(L, 1)))
                else:
                    pe_win(L, i, lambda: pe_slot(L, 2 * i))
                pe_slot(L, 2 * i + 1)
            for m in range(KT):
                pe_branches(L, m)
                if m == 1:
                    pe_outer(L, 2)
                if m == 3:
                    pe_outer(L, 3)
            for m in range(KT):
                pe_out(L, m)

        def evac_target(i):
            if i < 12:
                return craw[:, i * CW + 3:(i + 1) * CW]
            if i < 14:
                return (ak, av)[i - 12][:, :]
            if i < 18:
                return tile_of(aq, i - 14)
            if i < 22:
                return tile_of(z, i - 18)
            return tile_of(gt, i - 22)

        def dve_mix(L):
            split_tail(VE, w_tail_v, L, U_BA + AHEAD, (U_BA + AHEAD) % RING, UT - DS_MIX, UT)
            VE.wait_ge(out_ready.sem, out_ready.at(L, 4))
            VE.memset(craw[:, :].rearrange("p (c w) -> p c w", c=12)[:, :, 0:3], 0.0).then_inc(v_conv.sem, v_conv.mark("pad"))
            dve_factor(L, 1)
            dve_spread(L, 1)
            dve_ba_scale(L)
            for i in range(W_IN_TILES):
                if i % 2 == 0:
                    u = U_IN + i // 2 + AHEAD
                    split_tail(VE, w_tail_v, L, u, u % RING, UT - DS_MIX, UT)
                if i:
                    dve_slot(L, 2 * i)
                if i == 22:
                    VE.wait_ge(v_conv.sem, v_conv.at(L, "silu", 2))
                dve_evac(L, i, evac_target(i))
                if i < 12:
                    if i == 0:
                        VE.wait_ge(v_conv.sem, v_conv.at(L, "pad"))
                    dve_conv(L, i)
                dve_slot(L, 2 * i + 1)
            dve_od(L)
            for m in range(KT):
                if m % 2 == 0:
                    u = U_AD + m // 2 + AHEAD
                    split_tail(VE, w_tail_v, L, u, u % RING, UT - DS_MIX, UT)
                dve_branches(L, m)
                dve_mix_tail(L, m)
                if m == 0:
                    dve_drow(L, 2)
                    dve_drow(L, 3)
                if m == 2:
                    dve_state(L, 2)
                if m == 4:
                    dve_state(L, 3)
            for m in range(KT):
                if m % 2 == 0:
                    u = U_WO + m // 2 + AHEAD
                    split_tail(VE, w_tail_v, L, u, u % RING, UT - DS_MIX, UT)
                dve_residual(L, 8 + m, m, U_WO + m // 2, banks[0 if m % 2 else 7], 0.5)
                dve_tail(L, 8 + m, m, C_N2)

        def act_mix(L):
            split_head(L, U_BA + AHEAD, (U_BA + AHEAD) % RING, (U_BA + AHEAD) // RING)
            for i in range(W_IN_TILES):
                if i % 2 == 0:
                    u = U_IN + i // 2 + AHEAD
                    split_head(L, u, u % RING, u // RING)
                if i:
                    act_slot(L, 2 * i)
                act_slot(L, 2 * i + 1)
            for m in range(KT):
                if m % 2 == 0:
                    u = U_AD + m // 2 + AHEAD
                    split_head(L, u, u % RING, u // RING)
                act_branches(L, m)
                if m == 1:
                    act_state_out(L, 0)
                    act_state_out(L, 1)
                if m == 3:
                    act_state_out(L, 2)
                if m == 5:
                    act_state_out(L, 3)
            for m in range(KT):
                if m % 2 == 0:
                    u = U_WO + m // 2 + AHEAD
                    split_head(L, u, u % RING, u // RING)
                act_operand(L, 8 + m, m, C_N2)

        def pool_tail(L, u):
            split_tail(GE, w_tail_p, L, u, u % RING, 0, UT - DS_MIX)

        def pool_mix(L):
            pool_tail(L, U_BA + AHEAD)
            pool_factor(L, 1)
            for i in range(W_IN_TILES):
                if i % 2 == 0:
                    pool_tail(L, U_IN + i // 2 + AHEAD)
                if i:
                    pool_slot(L, 2 * i)
                pool_slot(L, 2 * i + 1)
            for u in range(U_AD, U_WO + 4):
                pool_tail(L, u + AHEAD)

        def mix_sync(sp):
            sp.wait_ge(d_shift, 64)
            for s in (d_conv, d_kv, d_s2, d_stout):
                sp.wait_ge(s.sem, DEPTH * s.per_layer)

        def act_end(act):
            pass

        DBG = not mix
        layers = 1 if DBG else DEPTH
        block = ctx.enter_context(nc.Block())

        @block.sync
        def _(sp):
            sp.dma_start(x[:, :], xT).then_inc(x_in, 16)
            sp.dma_start(par_all[:, :], params).then_inc(consts_in, 16)

            def load(u, r, free):
                if free is not None:
                    sp.wait_ge(w_head.sem, free)
                    sp.wait_ge(w_tail_p.sem, free)
                    sp.wait_ge(w_tail_v.sem, free)
                src = stream[u] if isinstance(u, int) else stream[u, :, :]
                sp.dma_start(raw[:, r * UT * P:(r + 1) * UT * P], src).then_inc(w_loaded[r], 16)

            total = (U_BA + AHEAD) if DBG else STREAM
            load(0, 0, None)
            sp.dma_start(con[:, :], consts).then_inc(consts_in, 16)
            for r in range(1, RING):
                load(r, r, None)
            with sp.Fori(1, total // RING) as i:
                for r in range(RING):
                    load(RING * i + r, r, RING * i + (r - RING + 1))
            for u in range(total // RING * RING, total):
                load(u, u % RING, u - RING + 1)
            sp.wait_ge(x_done.sem, x_done.at(0 if DBG else DEPTH, 8 if DBG else 0))
            sp.dma_start(outs["y"], x[:, :]).then_inc(y_out, 16)
            sp.wait_ge(y_out, 16)
            mix_sync(sp)

        @block.gpsimd
        def _(pool):
            if not DBG:
                for name in ("k", "v"):
                    for l in range(DEPTH):
                        pool.dma_start(outs[name + "s"][l, :, 0:WINDOW - 1, :], ins[name + "cache"][l, :, 1:WINDOW, :]
                                       ).then_inc(d_shift, 16)
            nc.gpsimd.memset(mhalf[:, :], -0.5).then_inc(ready0, 1)
            pool.wait_ge(ready0, 4 if DBG else 9)
            for u in range(AHEAD):
                split_tail(nc.gpsimd, w_tail_p, 0, u, u, 0, UT - DS_FFN)
            with pool.Fori(0, layers) as L:
                pool_units(L, 0, 1, DS_FFN)
                pool_factor(L, 0)
                pool_units(L, 1, U_BA - 1, DS_FFN)
                if not DBG:
                    pool_mix(L)
                    pool_units(L, U_G2, 1, DS_FFN)
                    pool_factor(L, 2)
                    pool_units(L, U_G2 + 1, UNITS - U_G2 - 1, DS_FFN)

        @block.scalar
        def _(act):
            act.wait_ge(x_in, 16)
            act.wait_ge(consts_in, 32)
            for m in range(KT):
                nc.scalar.activation(tile_of(xh, m), tile_of(x, m), ACT.Copy,
                                     scale=par_all[:, C_N1 + m:C_N1 + m + 1]).then_inc(xh_done.sem, 1)
                if m >= 2:
                    act.wait_ge(acc_done.sem, m - 1)
                nc.scalar.activation(tile_of(sq, m % 2), tile_of(x, m), ACT.Square).then_inc(sq_done.sem, 1)
                if m < AHEAD:
                    act.wait_ge(w_loaded[m], 16)
                    nc.scalar.copy(slot(whi, m), slot(raw, m)).then_inc(w_head.sem, 1)
            with act.Fori(0, layers) as L:
                if not DBG:
                    act_loads(L)
                act.wait_ge(par_ready.sem, par_ready.at(L, 1))
                act_gate_up(L, 0)
                act_down(L, 0)
                if not DBG:
                    act_mix(L)
                    act_gate_up(L, 1)
                    act_down(L, 1)
                    act_out_done(L)
            act_end(act)

        @block.tensor
        def _(pe):
            nc.tensor.sem_inc(w_used.sem, 1)
            with pe.Fori(0, layers) as L:
                pe_gate_up(L, 0)
                pe_down(L, 0)
                if not DBG:
                    pe_mix(L)
                    pe_gate_up(L, 1)
                    pe_down(L, 1)

        @block.vector
        def _(dve):
            nc.vector.memset(acc[:, :], 0.0).then_inc(acc_clear.sem, 1)
            if not DBG:
                nc.vector.memset(small[:, :], 0.0).then_inc(ready0, 1)
                nc.vector.memset(bt[:, :], 0.0).then_inc(ready0, 1)
                nc.vector.memset(avar[:, :], 1.0).then_inc(ready0, 1)
                nc.vector.memset(prod[:, :], 0.0).then_inc(ready0, 1)
                nc.vector.memset(qsq[:, :], 0.0).then_inc(ready0, 1)
                nc.vector.sem_inc(win_free.sem, 2)
            nc.vector.memset(var[:, :], 1.0).then_inc(ready0, 1)
            nc.vector.memset(rst[:, :], 1.0).then_inc(ready0, 1)
            nc.vector.memset(rs[:, :], 1.0).then_inc(ready0, 1)
            nc.vector.sem_inc(glu_free.sem, RING)
            nc.vector.sem_inc(h_ready.sem, RING)
            nc.vector.sem_inc(x_done.sem, KT)
            dve.wait_ge(x_in, 16)
            dve.wait_ge(consts_in, 32)
            dve.wait_ge(acc_clear.sem, 1)
            for m in range(KT):
                dve.wait_ge(xh_done.sem, m + 1)
                nc.vector.scalar_tensor_tensor(out=tile_of(xl, m), in0=tile_of(x, m), scalar=par_all[:, C_N1 + m:C_N1 + m + 1],
                                               in1=tile_of(xh, m).bitcast(F32), op0=ALU.mult,
                                               op1=ALU.subtract).then_inc(xl_done.sem, 1)
                dve.wait_ge(sq_done.sem, m + 1)
                if m:
                    dve.wait_ge(acc_done.sem, m)
                nc.vector.tensor_tensor(acc[:, :], acc[:, :], tile_of(sq, m % 2), ALU.add).then_inc(acc_done.sem, 1)
                if m < AHEAD:
                    split_tail(nc.vector, w_tail_v, 0, m, m, UT - DS_FFN, UT)
            with dve.Fori(0, layers) as L:
                dve.wait_ge(xh_done.sem, xh_done.at(L, 0))
                dve.wait_ge(xl_done.sem, xl_done.at(L, 0))
                nc.vector.tensor_copy(par[:, :], par_all[:, bass.ds(L * NPAR, NPAR)]).then_inc(par_ready.sem, 1)
                dve.wait_ge(par_ready.sem, par_ready.at(L, 1))
                dve_gate_up(L, 0)
                dve_down(L, 0)
                if not DBG:
                    dve_mix(L)
                    dve_gate_up(L, 1)
                    dve_down(L, 1)


def kernel(**inputs):
    import concourse.bacc as bacc
    from concourse.bass_utils import run_bass_kernel_spmd as run

    a = {k: np.asarray(v) for k, v in inputs.items()}
    tokens = np.concatenate([a["x_prompt"][0], a["x_sample"][:, 0]], axis=0)
    kcache, vcache = (a[n].reshape(DEPTH, B, WINDOW, P) for n in ("cache_swa_k", "cache_swa_v"))
    conv = a["state_conv"].reshape(DEPTH, B, CONV_W - 1, 3, H, P)[:, :, :, [1, 0, 2]]
    arrays = {
        "stream": host_stream(a),
        "xT": tokens.T.reshape(KT, P, N).transpose(1, 0, 2).reshape(P, KT * N).copy(),
        "params": host_params(a),
        "consts": host_constants(),
        "kct": kcache.transpose(0, 3, 1, 2).reshape(DEPTH, P, B * P).copy(),
        "vct": vcache.transpose(0, 2, 1, 3).reshape(DEPTH, P, B * P).copy(),
        "kcache": kcache.copy(),
        "vcache": vcache.copy(),
        "cst": conv.transpose(0, 5, 3, 4, 2, 1).reshape(DEPTH, P, 12 * 3 * B).copy(),
        "states": a["state_dn"].transpose(0, 3, 2, 1, 4).reshape(DEPTH, DK, H * B * DK).copy(),
    }
    shapes = {
        "y": (P, KT * N),
        "kp": (DEPTH, WINDOW, P), "vp": (DEPTH, WINDOW, P),
        "ks": (DEPTH, B, WINDOW, P), "vs": (DEPTH, B, WINDOW, P),
        "dnp": (DEPTH, DK, H * DK), "dns": (DEPTH, DK, H * B * DK),
        "convp": (DEPTH, P, 12 * 3), "convs": (DEPTH, P, 12 * 3 * B),
    }
    plan = {}
    for _ in range(2):
        nc = bacc.Bacc("TRN2", target_bir_lowering=False, num_devices=1)
        args = {k: nc.dram_tensor(k, v.shape, F32, kind="ExternalInput").ap() for k, v in arrays.items()}
        outs = {k: nc.dram_tensor("out_" + k, s, F32, kind="ExternalOutput").ap() for k, s in shapes.items()}
        build(nc, args["stream"], args["xT"], args["params"], args["consts"], outs, args, plan)
    r = run(nc, [arrays], core_ids=[0]).results[0]
    y = r["out_y"].reshape(P, KT, N).transpose(2, 1, 0).reshape(N, D_MODEL)
    heads = (N_KV, HEAD_DIM)

    def conv_rows(t, n):
        t = t.reshape(DEPTH, P, 3, H, 3, n)[:, :, [1, 0, 2]]
        return t.transpose(0, 5, 4, 2, 3, 1).reshape(DEPTH, n, 3, 12 * P)

    return (y[:T].reshape(1, T, D_MODEL), y[T:].reshape(B, 1, D_MODEL),
            r["out_kp"].reshape(DEPTH, 1, WINDOW, *heads), r["out_vp"].reshape(DEPTH, 1, WINDOW, *heads),
            r["out_dnp"].reshape(DEPTH, 1, DK, H, DK).transpose(0, 1, 3, 2, 4), conv_rows(r["out_convp"], 1),
            r["out_ks"].reshape(DEPTH, B, WINDOW, *heads), r["out_vs"].reshape(DEPTH, B, WINDOW, *heads),
            r["out_dns"].reshape(DEPTH, DK, H, B, DK).transpose(0, 3, 2, 1, 4), conv_rows(r["out_convs"], B))
```

```python
from contextlib import ExitStack

import numpy as np

import concourse.bass as bass
from concourse import mybir

F32 = mybir.dt.float32
F32R = mybir.dt.float32r
ACT = mybir.ActivationFunctionType
ALU = mybir.AluOpType
AX = mybir.AxisListType

P = 128
DEPTH, D_MODEL, D_FF = 2, 1024, 2816
T, B = 256, 8
N = T + B
PAST_LEN, WINDOW = 1024, 128
N_HEADS, N_KV, HEAD_DIM = 8, 2, 64
GROUP = N_HEADS // N_KV
H, DK, CONV_W = 4, 128, 4
EPS = 1e-6
KT = D_MODEL // P
FT = D_FF // P
UT = 16
RING = 3
AHEAD = 2
W_IN_TILES = 38
U_G1 = 0
U_D1 = U_G1 + FT
U_BA = U_D1 + 12
U_IN = U_BA + 1
U_AD = U_IN + W_IN_TILES // 2
U_WO = U_AD + 4
U_G2 = U_WO + 4
U_D2 = U_G2 + FT
UNITS = U_D2 + 12
assert UNITS == 96 and UNITS % RING == 0
STREAM = DEPTH * UNITS + AHEAD
DS_FFN = 6
DS_MIX = 1
DS_FIRST = 5

C_N1, C_MIX, C_N2, C_N1NEXT = 0, 8, 16, 24
C_QW, C_QWR, C_KW, C_KWR = 32, 33, 34, 35
C_CONV = 36
C_ONORM = C_CONV + 48
C_SINK = C_ONORM + 1
C_SINKROW = C_SINK + 8
C_ALOG = C_SINKROW + 1
C_DT = C_ALOG + 4
NPAR = C_DT + 4

K_ID, K_ONES, K_LE, K_GT, K_PERM, K_BLK2 = 0, 128, 256, 384, 512, 640
K_COS, K_SIN = 642, 642 + N
K_M0 = K_SIN + N
K_LEV = K_M0 + 128
K_TRIL = K_LEV + 6 * 64
K_AM0, K_AM1 = K_TRIL + 128, K_TRIL + 256
K_SEL = K_AM1 + 256
K_MROW = K_SEL + 128
NCON = K_MROW + 32


class Signal:

    def __init__(self, sem, per_layer, before=0):
        self.sem, self.per_layer, self.before = sem, per_layer, before

    def at(self, layer, n):
        return layer * self.per_layer + (self.before + n)


class Steps:

    def __init__(self, sem, name, plan):
        self.sem, self.n = sem, 0
        self.seen = plan.setdefault(name, {})

    def mark(self, *name):
        self.n += 1
        self.seen[name] = self.n
        return 1

    def at(self, layer, *name):
        return layer * max(self.seen.values(), default=1) + self.seen.get(name, 1)


def host_constants():
    c = np.zeros((P, NCON), np.float32)
    i = np.arange(P)
    c[:, K_ID:K_ID + P] = np.eye(P)
    c[:, K_ONES:K_ONES + P] = 1
    c[:, K_LE:K_LE + P] = i[:, None] <= i[None]
    c[:, K_GT:K_GT + P] = i[:, None] > i[None]
    half = HEAD_DIM // 2
    for m in range(P):
        k = m + half if m % HEAD_DIM < half else m - half
        c[k, K_PERM + m] = -1.0 if m % HEAD_DIM < half else 1.0
        c[m, K_BLK2 + m // HEAD_DIM] = 1
    pos = np.concatenate([np.arange(T), np.full(B, PAST_LEN)]).astype(np.float32)
    inv = (1.0 / (np.float32(10000.0) ** (np.arange(half, dtype=np.float32) / half))).astype(np.float32)
    ang = pos[None] * inv[i % half][:, None]
    c[:, K_COS:K_COS + N] = np.cos(ang)
    c[:, K_SIN:K_SIN + N] = np.sin(ang)
    c[:, K_M0:K_M0 + P] = (i[:, None] // 2 == i[None] // 2) & (i[:, None] < i[None])
    for lv in range(1, 7):
        s = 2 ** lv
        j = np.array([b * 2 * s + e for b in range(P // (2 * s)) for e in range(s)])
        c[:, K_LEV + 64 * (lv - 1):K_LEV + 64 * lv] = (i[:, None] // (2 * s) == j[None] // (2 * s)) & (i[:, None] % (2 * s) >= s)
    c[:, K_TRIL:K_TRIL + P] = i[:, None] >= i[None]
    big = np.float32(-1e30)
    c[:, K_AM0:K_AM0 + P] = np.where(i[None] <= i[:, None], 0, big)
    c[:, K_AM1:K_AM1 + P] = np.where(i[None] >= i[:, None], 0, big)
    c[:, K_AM1 + P:K_AM1 + 2 * P] = c[:, K_AM0:K_AM0 + P]
    for r in range(64):
        kv, tb = r // 32, r % 32
        c[r, K_SEL + kv * 64:K_SEL + kv * 64 + 64] = 1
        c[r, K_MROW + tb] = 1
    return c


def tiles(w):
    l, k, m = w.shape
    return w.reshape(l, k // P, P, m // P, P).transpose(0, 3, 1, 2, 4)


def host_stream(a):
    out = np.zeros((STREAM, P, UT, P), np.float32)
    layers = out[:DEPTH * UNITS].reshape(DEPTH, UNITS, P, UT, P)

    def put(u, t, block):
        layers[:, u, :, t:t + block.shape[1]] = block.transpose(0, 2, 1, 3)

    for base, name in ((U_G1, "ffn1"), (U_G2, "ffn2")):
        gu, dn = tiles(a[name + "_w_gate_up"]), tiles(a[name + "_w_down"])
        for f in range(FT):
            put(base + f, 0, gu[:, f])
            put(base + f, KT, gu[:, FT + f])
        for m in range(0, KT, 2):
            both = np.concatenate([dn[:, m], dn[:, m + 1]], axis=1)
            for j in range(3):
                put(base + FT + m // 2 * 3 + j, 0, both[:, j * UT:(j + 1) * UT])
    w = a["w_in"]
    q, rest = w[:, :, :512], w[:, :, 512:]
    q = q.reshape(DEPTH, D_MODEL, N_KV, GROUP, HEAD_DIM).transpose(0, 1, 3, 2, 4).reshape(DEPTH, D_MODEL, 512)
    ak, av, dn = rest[:, :, :128], rest[:, :, 128:256], rest[:, :, 256:1792]
    z, ba, ga, gd = rest[:, :, 1792:2304], rest[:, :, 2304:2312], rest[:, :, 2312:3336], rest[:, :, 3336:]
    layers[:, U_BA, :, :KT, :8] = ba.reshape(DEPTH, KT, P, 8).transpose(0, 2, 1, 3)
    gates = np.stack([ga.reshape(DEPTH, D_MODEL, KT, P), gd.reshape(DEPTH, D_MODEL, KT, P)], axis=3)
    cols = np.concatenate([dn[:, :, 512:1024], dn[:, :, :512], dn[:, :, 1024:], ak, av, q, z,
                           gates.reshape(DEPTH, D_MODEL, 2048)], axis=2)
    t_in = tiles(cols)
    for i in range(W_IN_TILES):
        put(U_IN + i // 2, KT * (i % 2), t_in[:, i])
    ao = a["w_attn_o"].reshape(DEPTH, N_KV, GROUP, HEAD_DIM, D_MODEL).transpose(0, 2, 1, 3, 4).reshape(DEPTH, 512, D_MODEL)
    t_a, t_d, t_o = tiles(ao), tiles(a["w_dn_o"]), tiles(a["w_out"])
    for m in range(KT):
        put(U_AD + m // 2, KT * (m % 2), t_a[:, m])
        put(U_AD + m // 2, KT * (m % 2) + 4, t_d[:, m])
        put(U_WO + m // 2, KT * (m % 2), t_o[:, m])
    return out.reshape(STREAM, P, UT * P)


def host_params(a):
    p = np.zeros((DEPTH, P, NPAR), np.float32)

    def cols(at, w):
        p[:, :, at:at + KT] = w.reshape(DEPTH, KT, P).transpose(0, 2, 1)

    cols(C_N1, a["ffn1_norm"])
    cols(C_MIX, a["mix_norm"])
    cols(C_N2, a["ffn2_norm"])
    cols(C_N1NEXT, np.roll(a["ffn1_norm"], -1, axis=0))
    d = np.arange(P) % HEAD_DIM
    partner = (d + HEAD_DIM // 2) % HEAD_DIM
    p[:, :, C_QW], p[:, :, C_QWR] = a["q_norm"][:, d], a["q_norm"][:, partner]
    p[:, :, C_KW], p[:, :, C_KWR] = a["k_norm"][:, d], a["k_norm"][:, partner]
    cw = a["conv_w"].reshape(DEPTH, CONV_W, 3, H, P)[:, :, [1, 0, 2]]
    p[:, :, C_CONV:C_CONV + 48] = cw.transpose(0, 4, 2, 3, 1).reshape(DEPTH, P, 48)
    p[:, :, C_ONORM] = a["dn_out_norm"]
    s = a["attn_sinks"].reshape(DEPTH, N_KV, GROUP)
    p[:, :, C_SINK:C_SINK + 8] = s.transpose(0, 2, 1).reshape(DEPTH, 1, 8)
    p[:, :64, C_SINKROW] = np.repeat(s.reshape(DEPTH, 8), B, axis=1)
    p[:, :, C_ALOG:C_ALOG + 4] = a["dn_A_log"][:, None]
    p[:, :, C_DT:C_DT + 4] = a["dn_dt_bias"][:, None]
    return p.transpose(1, 0, 2).reshape(P, DEPTH * NPAR).copy()


def build(nc, stream, xT, params, consts, outs, ins, plan):
    ctx = ExitStack()
    with ctx:
        top = [0]
        base0 = -(-nc.sbuf_base // 64) * 64

        def place(name, cols, dt=F32, at=None):
            off = top[0] if at is None else at
            t = nc.alloc_sbuf_tensor_at(name, [P, cols], dt, offset=base0 + 4 * off)
            if at is None:
                top[0] += -(-cols // 8) * 8
            return t

        raw = place("raw", RING * UT * P)
        whi = place("whi", RING * UT * P, F32R)
        wlo = place("wlo", RING * UT * P, F32R)
        x = place("x", KT * N)
        xh, xl = place("xh", KT * N, F32R), place("xl", KT * N, F32R)
        con = place("con", NCON)
        par_all = place("par_all", DEPTH * NPAR)
        par = place("par", NPAR)
        sq_at = top[0]
        sq = place("sq", 2 * N)
        acc = place("acc", N)
        var, rst, mhalf = place("var", 16), place("rst", 16), place("mhalf", 96)
        diag = place("diag", N)
        rs = place("rs", N)
        gbuf_at = top[0]
        gbuf, tbuf = place("gbuf", RING * N), place("tbuf", RING * N)
        arena = top[0]
        hh, hl = place("hh", FT * N, F32R), place("hl", FT * N, F32R)
        ffn_end = top[0]

        banks = [ctx.enter_context(nc.psum_tensor(f"bank{i}", [P, 512], F32)) for i in range(8)]
        STAT = banks[6]

        def tile_of(t, n, width=N):
            return t[:, n * width:(n + 1) * width]

        def slot(t, r, lo=0, hi=UT):
            return t[:, (r * UT + lo) * P:(r * UT + hi) * P]

        def sig(name, per_layer, before=0):
            return Signal(ctx.enter_context(nc.semaphore(name)), per_layer, before)

        w_loaded = [ctx.enter_context(nc.semaphore(f"w_loaded{r}")) for r in range(RING)]
        w_head = sig("w_head", UNITS)
        w_tail_p = sig("w_tail_p", UNITS)
        w_tail_v = sig("w_tail_v", UNITS)
        w_used = sig("w_used", UNITS, 1)
        consts_in = ctx.enter_context(nc.semaphore("consts_in"))
        par_in = ctx.enter_context(nc.semaphore("par_in"))
        ones_in = ctx.enter_context(nc.semaphore("ones_in"))
        x_in = [ctx.enter_context(nc.semaphore(f"x_in{n}")) for n in range(2)]
        ready0 = ctx.enter_context(nc.semaphore("ready0"))
        par_ready = sig("par_ready", 1)
        x_done = sig("x_done", 24, 8)
        xh_done = sig("xh_done", 24, 8)
        xl_done = sig("xl_done", 24, 8)
        sq_done = sig("sq_done", 24, 8)
        acc_done = sig("acc_done", 24, 8)
        ss_ready = sig("ss_ready", 3)
        var_ready = sig("var_ready", 3)
        acc_clear = sig("acc_clear", 3, 1)
        rstd_ready = sig("rstd_ready", 3)
        diag_ready = sig("diag_ready", 9)
        rsb_ready = sig("rsb_ready", 3)
        rs_ready = sig("rs_ready", 3)
        gate_ready = sig("gate_ready", 2 * FT)
        glu_g = sig("glu_g", 2 * FT)
        glu_t = sig("glu_t", 2 * FT)
        glu_a = sig("glu_a", 2 * FT)
        glu_free = sig("glu_free", 2 * FT, RING)
        glu_h = sig("glu_h", 2 * FT)
        glu_hh = sig("glu_hh", 2 * FT)
        h_ready = sig("h_ready", 2 * FT, RING)
        out_ready = sig("out_ready", 12)
        y_out = ctx.enter_context(nc.semaphore("y_out"))

        def split_head(L, u, r, use):
            nc.scalar.wait_ge(w_loaded[r], L * (16 * UNITS // RING) + (use * 16 + 16))
            nc.scalar.wait_ge(w_used.sem, w_used.at(L, u - 2))
            nc.scalar.copy(slot(whi, r), slot(raw, r)).then_inc(w_head.sem, 1)

        def split_tail(eng, done, L, u, r, lo, hi):
            eng.wait_ge(w_head.sem, w_head.at(L, u + 1))
            op = eng.tensor_tensor(slot(wlo, r, lo, hi), slot(raw, r, lo, hi), slot(whi, r, lo, hi).bitcast(F32),
                                   ALU.subtract)
            if done is not None:
                op.then_inc(done.sem, 1)

        def product(out, r, t, mh, ml, start, stop, m=P):
            wh, wl = slot(whi, r, t, t + 1)[:, 0:m], slot(wlo, r, t, t + 1)[:, 0:m]
            nc.tensor.matmul(out, wh, mh, start=start, stop=False)
            nc.tensor.matmul(out, wh, ml, start=False, stop=False)
            return nc.tensor.matmul(out, wl, mh, start=False, stop=stop)

        def wait_unit(L, u):
            nc.tensor.wait_ge(w_tail_p.sem, w_tail_p.at(L, u + 1))
            nc.tensor.wait_ge(w_tail_v.sem, w_tail_v.at(L, u + 1))

        BLK = ((0, P, 0, P), (P, T, 0, P), (T, N, 0, B))

        def pe_sums(L, n):
            if n == 0:
                nc.tensor.wait_ge(ones_in, 16)
            nc.tensor.wait_ge(acc_done.sem, acc_done.at(L, 8 * n))
            for b, (c0, c1, _, p1) in enumerate(BLK):
                mm = nc.tensor.matmul(STAT[0:p1, 300 + b:301 + b], acc[:, c0:c1], con[:, K_ONES:K_ONES + 1],
                                      start=True, stop=True)
            mm.then_inc(ss_ready.sem, 1)

        def dve_factor(L, n, meanwhile=lambda: None):
            nc.vector.wait_ge(ss_ready.sem, ss_ready.at(L, n + 1))
            nc.vector.tensor_scalar(var[:, 0:2], STAT[:, 300:302], 1.0 / D_MODEL, EPS, ALU.mult, ALU.add)
            nc.vector.tensor_scalar(var[0:B, 2:3], STAT[0:B, 302:303], 1.0 / D_MODEL, EPS, ALU.mult,
                                    ALU.add).then_inc(var_ready.sem, 1)
            nc.vector.memset(acc[:, :], 0.0).then_inc(acc_clear.sem, 1)
            meanwhile()
            nc.vector.wait_ge(rstd_ready.sem, rstd_ready.at(L, n + 1))
            for b, (c0, c1, _, p1) in enumerate(BLK):
                nc.vector.tensor_scalar(diag[0:p1, c0:c1], con[0:p1, K_ID:K_ID + p1], rst[0:p1, b:b + 1], None,
                                        ALU.mult).then_inc(diag_ready.sem, 1)

        def dve_spread(L, n):
            nc.vector.wait_ge(rsb_ready.sem, rsb_ready.at(L, n + 1))
            nc.vector.tensor_copy(rs[:, :], STAT[:, 0:N]).then_inc(rs_ready.sem, 1)
            nc.vector.wait_ge(rs_ready.sem, rs_ready.at(L, n + 1))

        def pool_factor(L, n):
            nc.gpsimd.wait_ge(var_ready.sem, var_ready.at(L, n + 1))
            nc.gpsimd.tensor_tensor(rst[:, 0:3], var[:, 0:3], mhalf[:, 0:3], ALU.pow).then_inc(rstd_ready.sem, 1)

        def pe_spread(L, n):
            nc.tensor.wait_ge(diag_ready.sem, diag_ready.at(L, 3 * n + 3))
            for b, (c0, c1, _, p1) in enumerate(BLK):
                mm = nc.tensor.matmul(STAT[:, c0:c1], con[0:p1, K_ONES:K_ONES + P], diag[0:p1, c0:c1],
                                      start=True, stop=True)
            mm.then_inc(rsb_ready.sem, 1)

        def dve_residual(L, e, m, last_unit, bank, scale):
            if m % 2:
                nc.vector.wait_ge(w_used.sem, w_used.at(L, last_unit + 1))
            else:
                nc.vector.wait_ge(out_ready.sem, out_ready.at(L, e // 2 + 1))
            nc.vector.scalar_tensor_tensor(out=tile_of(x, m), in0=bank[:, 0:N], scalar=scale, in1=tile_of(x, m),
                                           op0=ALU.mult, op1=ALU.add).then_inc(x_done.sem, 1)

        def dve_tail(L, e, m, col):
            nc.vector.wait_ge(xh_done.sem, xh_done.at(L, e + 1))
            nc.vector.scalar_tensor_tensor(out=tile_of(xl, m), in0=tile_of(x, m), scalar=par[:, col + m:col + m + 1],
                                           in1=tile_of(xh, m).bitcast(F32), op0=ALU.mult,
                                           op1=ALU.subtract).then_inc(xl_done.sem, 1)
            nc.vector.wait_ge(sq_done.sem, sq_done.at(L, e + 1))
            nc.vector.wait_ge(acc_done.sem, acc_done.at(L, e))
            if m == 0 and e >= 0:
                nc.vector.wait_ge(acc_clear.sem, acc_clear.at(L, e // 8 + 1))
            nc.vector.tensor_tensor(acc[:, :], acc[:, :], tile_of(sq, m % 2), ALU.add).then_inc(acc_done.sem, 1)

        def act_operand(L, e, m, col):
            nc.scalar.wait_ge(x_done.sem, x_done.at(L, e + 1))
            nc.scalar.activation(tile_of(xh, m), tile_of(x, m), ACT.Copy,
                                 scale=par[:, col + m:col + m + 1]).then_inc(xh_done.sem, 1)
            nc.scalar.wait_ge(acc_done.sem, acc_done.at(L, e - 1))
            nc.scalar.activation(tile_of(sq, m % 2), tile_of(x, m), ACT.Square).then_inc(sq_done.sem, 1)

        def pe_gate_up(L, ph):
            u0, n = (U_G1, U_G2)[ph], (0, 2)[ph]

            def unit(f, j, r, first=False, second=False):
                bg, bu = banks[2 * j], banks[2 * j + 1]
                wait_unit(L, u0 + f)
                nc.tensor.wait_ge(glu_free.sem, glu_free.at(L, ph * FT + f + 1 - RING))
                for k in range(KT):
                    if first:
                        nc.tensor.wait_ge(xl_done.sem, xl_done.at(L, 8 * n - 8 + k + 1))
                    mm = product(bg[:, 0:N], r, k, tile_of(xh, k), tile_of(xl, k), k == 0, k == KT - 1)
                mm.then_inc(gate_ready.sem, 1)
                if first:
                    pe_sums(L, n)
                if second:
                    pe_spread(L, n)
                for k in range(KT):
                    mm = product(bu[:, 0:N], r, KT + k, tile_of(xh, k), tile_of(xl, k), k == 0, k == KT - 1)
                mm.then_inc(w_used.sem, 1)

            unit(0, 1, u0 % RING, True)
            for j in range(RING):
                unit(1 + j, (2 + j) % RING, (u0 + 1 + j) % RING, second=j == 0)
            with nc.tensor.Fori(1, FT // RING) as i:
                for j in range(RING):
                    unit(3 * i + (1 + j), (2 + j) % RING, (u0 + 1 + j) % RING)

        def dve_gate_up(L, ph):
            u0, n = (U_G1, U_G2)[ph], (0, 2)[ph]

            def finish(f, j, split):
                g, t = tile_of(gbuf, j), tile_of(tbuf, j)
                e = ph * FT + f
                nc.vector.wait_ge(glu_t.sem, glu_t.at(L, e + 1))
                nc.vector.scalar_tensor_tensor(out=t, in0=t, scalar=1.0, in1=g, op0=ALU.add,
                                               op1=ALU.mult).then_inc(glu_a.sem, 1)
                nc.vector.wait_ge(w_used.sem, w_used.at(L, u0 + f + 1))
                nc.vector.wait_ge(glu_a.sem, glu_a.at(L, e + 1))
                nc.vector.tensor_tensor(g, t, banks[2 * j + 1][:, 0:N], ALU.mult).then_inc(glu_free.sem, 1)
                nc.vector.wait_ge(glu_free.sem, glu_free.at(L, e + 1))
                nc.vector.tensor_tensor(t, g, rs[:, :], ALU.mult).then_inc(glu_h.sem, 1)
                split()
                nc.vector.wait_ge(glu_hh.sem, glu_hh.at(L, e + 1))
                nc.vector.tensor_tensor(hl_tile(f), t, hh_tile(f).bitcast(F32), ALU.subtract).then_inc(h_ready.sem, 1)

            def unit(f, j, r, first=False):
                e = ph * FT + f
                nc.vector.wait_ge(gate_ready.sem, gate_ready.at(L, e + 1))
                split = lambda: split_tail(nc.vector, w_tail_v, L, u0 + f + AHEAD, (r + AHEAD) % RING, UT - DS_FFN, UT)
                if first:
                    dve_factor(L, n, split)
                    dve_spread(L, n)
                nc.vector.wait_ge(h_ready.sem, h_ready.at(L, e + 1 - RING))
                nc.vector.tensor_tensor(tile_of(gbuf, j), banks[2 * j][:, 0:N], rs[:, :], ALU.mult).then_inc(glu_g.sem, 1)
                finish(f, j, (lambda: None) if first else split)

            unit(0, 1, u0 % RING, True)
            with nc.vector.Fori(0, FT // RING) as i:
                for j in range(RING):
                    unit(3 * i + (1 + j), (2 + j) % RING, (u0 + 1 + j) % RING)

        def hh_tile(f):
            return tile_of(hh, f) if isinstance(f, int) else hh[:, bass.ds(f * N, N)]

        def hl_tile(f):
            return tile_of(hl, f) if isinstance(f, int) else hl[:, bass.ds(f * N, N)]

        def act_gate_up(L, ph):
            u0 = (U_G1, U_G2)[ph]

            def unit(f, j, r, use):
                e = ph * FT + f
                split_head(L, u0 + f + AHEAD, (r + AHEAD) % RING, use)
                nc.scalar.wait_ge(glu_g.sem, glu_g.at(L, e + 1))
                nc.scalar.activation(tile_of(tbuf, j), tile_of(gbuf, j), ACT.Tanh, scale=0.5).then_inc(glu_t.sem, 1)
                nc.scalar.wait_ge(glu_h.sem, glu_h.at(L, e + 1))
                nc.scalar.copy(hh_tile(f), tile_of(tbuf, j)).then_inc(glu_hh.sem, 1)

            unit(0, 1, u0 % RING, (u0 + AHEAD) // RING)
            with nc.scalar.Fori(0, FT // RING) as i:
                for j in range(RING):
                    unit(3 * i + (1 + j), (2 + j) % RING, (u0 + 1 + j) % RING, i + (u0 + 1 + j + AHEAD) // RING)

        def pool_units(L, u0, count, share):
            if count // RING:
                with nc.gpsimd.Fori(0, count // RING) as i:
                    for j in range(RING):
                        split_tail(nc.gpsimd, w_tail_p, L, 3 * i + (u0 + AHEAD + j), (u0 + AHEAD + j) % RING, 0, UT - share)
            for u in range(u0 + count // RING * RING, u0 + count):
                split_tail(nc.gpsimd, w_tail_p, L, u + AHEAD, (u + AHEAD) % RING, 0, UT - share)

        def pe_down(L, ph):
            u0 = (U_D1, U_D2)[ph]
            e0 = (0, 16)[ph]
            with nc.tensor.Fori(0, KT // 2) as i:
                for j in range(3):
                    wait_unit(L, 3 * i + (u0 + j))
                    if j == 0:
                        nc.tensor.wait_ge(h_ready.sem, h_ready.at(L, ph * FT + FT - 2))
                    for n in range(UT * j, min(UT * (j + 1), 2 * FT)):
                        m, f = n // FT, n % FT
                        if f == 0:
                            nc.tensor.wait_ge(x_done.sem, x_done.at(L, 2 * i + (e0 + m - 1)))
                        if n == FT - 2:
                            nc.tensor.wait_ge(h_ready.sem, h_ready.at(L, ph * FT + FT))
                        mm = product(banks[7 if m == 0 else 0][:, 0:N], (u0 + j) % RING, n % UT, tile_of(hh, f),
                                     tile_of(hl, f), f == 0, f == FT - 1)
                        if n == FT - 1:
                            mm.then_inc(out_ready.sem, 1)
                        elif n % UT == UT - 1 or n == 2 * FT - 1:
                            mm.then_inc(w_used.sem, 1)

        def dve_down(L, ph):
            u0, e0 = (U_D1, U_D2)[ph], (0, 16)[ph]
            col = (C_MIX, C_N1NEXT)[ph]
            for m in range(KT):
                for u in {0: (0,), 1: (1, 2)}[m % 2]:
                    u += u0 + m // 2 * 3
                    split_tail(nc.vector, w_tail_v, L, u + AHEAD, (u + AHEAD) % RING, UT - DS_FFN, UT)
                dve_residual(L, e0 + m, m, u0 + m // 2 * 3 + 2, banks[0 if m % 2 else 7], 0.25)
                dve_tail(L, e0 + m, m, col)

        def act_down(L, ph):
            u0, e0 = (U_D1, U_D2)[ph], (0, 16)[ph]
            col = (C_MIX, C_N1NEXT)[ph]
            for m in range(KT):
                for u in {0: (0,), 1: (1, 2)}[m % 2]:
                    u += u0 + m // 2 * 3
                    split_head(L, u + AHEAD, (u + AHEAD) % RING, (u + AHEAD) // RING)
                act_operand(L, e0 + m, m, col)
        def steps(name):
            return Steps(ctx.enter_context(nc.semaphore(name)), name, plan)

        gt = place("gt", 16 * N, at=arena)
        z = place("z", H * N, at=arena + 16 * N)
        CW = T + 3 + B
        craw_at = arena + 20 * N
        craw = place("craw", 12 * CW, at=craw_at)
        cv_at = craw_at + -(-12 * CW // 8) * 8
        cv = place("cv", 12 * N, at=cv_at)
        top[0] = max(top[0], -(-(cv_at + 12 * N) // 8) * 8)
        mixh = place("mixh", KT * N, F32R, at=craw_at)
        assert KT * N <= 12 * CW
        mixl_v = place("mixl_v", 4 * N, F32R, at=cv_at + 8 * N)
        mixl_z = place("mixl_z", 4 * N, F32R, at=arena + 16 * N)
        act_scr, sq4, z_scr, k_scr = gt[:, 0:4 * N], gt[:, 4 * N:8 * N], gt[:, 8 * N:12 * N], gt[:, 12 * N:13 * N]
        rope_a, rope_b = gt[:, 13 * N:14 * N], gt[:, 14 * N:15 * N]
        aq_at = top[0]
        aq = place("aq", 4 * N)
        oah = place("oah", 4 * N, F32R, at=aq_at)
        oal = place("oal", 4 * N, F32R, at=top[0])
        ak, av = place("ak", N), place("av", N)
        kT = place("kT", N)
        cst = place("cst", 12 * 3 * B)
        assert 3 * N + 12 * 3 * B >= 4 * N
        kc = place("kc", B * P)
        vc = place("vc", B * P)
        st_at = top[0] - 2 * B * P
        states = place("states", 2 * B * P, at=st_at)
        rows1 = place("rows1", 512, at=top[0])
        ktok, vtok = place("ktok", 3 * P), place("vtok", 3 * P)
        otok = place("otok", 2 * 512)
        names = ("K", "T", "U", "Y", "B", "P")
        m0T_at = top[0] + 512
        M = [{n: place("m0" + n, 512) for n in names},
             {n: place("m1" + n, 512, at=craw_at + 512 * i) for i, n in enumerate(names)}]
        sm_at = top[0]
        smx = nc.alloc_sbuf_tensor_at("smx", [P, 4 * 384], F32, offset=base0 + 4 * gbuf_at)
        sm = [smx[:, 384 * i:384 * (i + 1)] for i in range(2)]
        ptb = [smx[:, 384 * (2 + i):384 * (3 + i)] for i in range(2)]
        drow = smx
        assert 2 * B * P <= 8 * N and 8 * N <= 5 * 512
        states2 = nc.alloc_sbuf_tensor_at("states2", [P, 2 * B * P], F32, offset=base0 + 4 * cv_at)
        odh = place("odh", H * N, F32R, at=m0T_at)
        odl = place("odl", H * N, F32R, at=m0T_at + 4 * N)
        ba8 = place("ba8", N)
        bt = place("bt", 24)
        small = place("small", 12 * 12)
        x2, ab, e1, lnv, sp_, g_, bet, th, negA, egx = [small[:, 12 * i:12 * (i + 1)] for i in range(10)]
        eg = place("eg", 24)
        kbs, hbs, rqg = place("kbs", 8), place("hbs", 8), place("rqg", 8)
        dx, abc = place("dx", 64), place("abc", 64)
        pa_, pb_ = place("pa_", 32), place("pb_", 32)
        st, rkq = place("st", 80), place("rkq", 80)
        kq2 = place("kq2", 64)
        avar, arst = place("avar", 6), place("arst", 6)
        qvar, rqa = place("qvar", 16), place("rqa", 16)
        svar, srst = place("svar", 1), place("srst", 1)
        mx, nm, den, esk, rec = [place(n, 16) for n in ("mx", "nm", "den", "esk", "rec")]
        sT, sl, pts = place("sT", 64), place("sl", 130), place("pts", 64)
        rmat, pvs, oas = [place(n, 32) for n in ("rmat", "pvs", "oas")]
        prod, qsq = place("prod", 64), place("qsq", 64)
        smax, snm, sden, sesk, srec = [place(n, 1) for n in ("smax", "snm", "sden", "sesk", "srec")]
        oss, ovar, orst = place("oss", 8), place("ovar", 8), place("orst", 8)
        qkp, qkb, dlt, tmp32, osq, osv, osr = [place(n, 32) for n in ("qkp", "qkb", "dlt", "tmp32", "osq", "osv", "osr")]
        rows0 = place("rows0", 512, at=sq_at)
        assert base0 + 4 * top[0] <= nc.sbuf_usable_end, (top[0], nc.sbuf_usable_end)

        win_ready = sig("win_ready", 19)
        win_free = sig("win_free", 38, 2)
        pe_ba, pe_dn, pe_at, pe_sd = steps("pe_ba"), steps("pe_dn"), steps("pe_at"), steps("pe_sd")
        v_ba, v_conv, v_dn, v_at, v_sd = steps("v_ba"), steps("v_conv"), steps("v_dn"), steps("v_at"), steps("v_sd")
        a_ba, a_conv, a_dn, a_at, a_sd = steps("a_ba"), steps("a_conv"), steps("a_dn"), steps("a_at"), steps("a_sd")
        g_mix = steps("g_mix")
        v_gate, a_gate = steps("v_gate"), steps("a_gate")
        pe_ad, v_ad, a_ad = steps("pe_ad"), steps("v_ad"), steps("a_ad")
        d_cst, d_kc, d_vc = sig("d_cst", 16), sig("d_kc", 16), sig("d_vc", 16)
        d_state = [sig("d_state0", 16), sig("d_state1", 16)]
        d_stout = sig("d_stout", 64)
        d_conv = sig("d_conv", 48)
        d_kv = sig("d_kv", 64)
        d_s2 = sig("d_s2", 16)
        d_shift = ctx.enter_context(nc.semaphore("d_shift"))

        TE, VE, SE, GE = nc.tensor, nc.vector, nc.scalar, nc.gpsimd
        one_col = con[:, K_ONES:K_ONES + 1]
        ident, ones = con[:, K_ID:K_ID + P], con[:, K_ONES:K_ONES + P]

        def turn(out, src):
            n = src.shape[0]
            if n == P and src.shape[1] == P:
                return TE.transpose(out, src, ident)
            return TE.matmul(out, src, con[0:n, K_ID:K_ID + n], start=True, stop=True)

        def mixl(m):
            return tile_of(mixl_v, m) if m < 4 else tile_of(mixl_z, m - 4)

        def hd4(t):
            return t.rearrange("p (h d) -> p h d", h=4)

        def hs(t, h):
            return t[:, h * P:(h + 1) * P]

        def cvt(group, h):
            n = {"q": 0, "k": 4, "v": 8}[group] + h
            return cv[:, n * N:(n + 1) * N]

        def cv4(group):
            n = {"q": 0, "k": 4, "v": 8}[group]
            return cv[:, n * N:(n + 4) * N].rearrange("p (h t) -> p h t", h=4)

        def bc(ap, n):
            return ap.unsqueeze(2).to_broadcast([ap.shape[0], ap.shape[1], n])

        def bcm(ap, n):
            return ap.unsqueeze(1).to_broadcast([ap.shape[0], n, ap.shape[1]])

        def tok(c):
            return slice(c * P, (c + 1) * P)

        BA_, B7 = banks[6], banks[7]
        CB = [(banks[2], banks[3]), (banks[4], banks[5])]

        def pe_win(L, i, mid):
            u, t0 = U_IN + i // 2, KT * (i % 2)
            if i % 2 == 0:
                wait_unit(L, u)
            TE.wait_ge(win_free.sem, win_free.at(L, i - 1))
            for k in range(KT):
                if k == KT // 2:
                    mid()
                if i == 8:
                    pe_stats(L, "k", k)
                if i == 11:
                    pe_stats(L, "q", k)
                if i == 20:
                    pe_q_stats(L, k)
                if i == 21:
                    pe_s_scores(L, k)
                if i in (31, 33):
                    pe_pred(L, i // 33, k)
                mm = product(banks[i % 2][:, 0:N], u % RING, t0 + k, tile_of(xh, k), tile_of(xl, k), k == 0, k == KT - 1)
            if i % 2:
                mm.then_inc(w_used.sem, 1)
            else:
                mm.then_inc(win_ready.sem, 1)

        def dve_evac(L, i, out):
            if i % 2:
                VE.wait_ge(w_used.sem, w_used.at(L, U_IN + i // 2 + 1))
            else:
                VE.wait_ge(win_ready.sem, win_ready.at(L, i // 2 + 1))
            VE.tensor_tensor(out, banks[i % 2][:, 0:N], rs[:, :], ALU.mult).then_inc(win_free.sem, 1)

        def pe_ba_product(L):
            wait_unit(L, U_BA)
            for k in range(KT):
                TE.wait_ge(xl_done.sem, xl_done.at(L, k + 1))
                mm = product(banks[7][:, 0:N], U_BA % RING, k, tile_of(xh, k), tile_of(xl, k), k == 0, k == KT - 1)
            mm.then_inc(w_used.sem, 1)

        def dve_ba_scale(L):
            VE.wait_ge(w_used.sem, w_used.at(L, U_BA + 1))
            VE.tensor_tensor(ba8[0:8, :], banks[7][0:8, 0:N], rs[0:8, :], ALU.mult).then_inc(v_ba.sem, v_ba.mark("ba8"))

        def pe_ba_turn(L):
            TE.wait_ge(v_ba.sem, v_ba.at(L, "ba8"))
            for b, (c0, c1, _, p1) in enumerate(BLK):
                mm = turn(BA_[0:p1, 272 + 8 * b:280 + 8 * b], ba8[0:8, c0:c1])
            mm.then_inc(pe_ba.sem, pe_ba.mark("turned"))

        def dve_ba(L):
            VE.wait_ge(pe_ba.sem, pe_ba.at(L, "turned"))
            VE.tensor_copy(bt[:, 0:16], BA_[:, 272:288]).then_inc(v_ba.sem, v_ba.mark("bt"))
            VE.tensor_copy(bt[0:B, 16:24], BA_[0:B, 288:296]).then_inc(v_ba.sem, v_ba.mark("bt2"))
            VE.wait_ge(v_ba.sem, v_ba.at(L, "bt2"))
            btv = bt[:, :].rearrange("p (b c) -> p b c", b=3)
            VE.tensor_tensor(x2.rearrange("p (b c) -> p b c", b=3), btv[:, :, 4:8], bcm(par[:, C_DT:C_DT + 4], 3),
                             ALU.add).then_inc(v_ba.sem, v_ba.mark("x2"))
            VE.wait_ge(v_ba.sem, v_ba.at(L, "x2"))
            VE.scalar_tensor_tensor(out=ab, in0=x2, scalar=-1.0, in1=x2, op0=ALU.mult,
                                    op1=ALU.max).then_inc(v_ba.sem, v_ba.mark("abs"))

        def dve_ba_beta(L):
            VE.wait_ge(a_ba.sem, a_ba.at(L, "exp"))
            VE.tensor_scalar(e1, e1, 1.0, None, ALU.add).then_inc(v_ba.sem, v_ba.mark("1+e"))
            VE.tensor_scalar(bet, th, 0.5, 0.5, ALU.mult, ALU.add).then_inc(v_ba.sem, v_ba.mark("beta"))

        def dve_ba_decay(L):
            VE.wait_ge(a_ba.sem, a_ba.at(L, "ln"))
            VE.scalar_tensor_tensor(out=sp_, in0=x2, scalar=0.0, in1=lnv, op0=ALU.max,
                                    op1=ALU.add).then_inc(v_ba.sem, v_ba.mark("softplus"))
            VE.wait_ge(v_ba.sem, v_ba.at(L, "softplus"))
            VE.scalar_tensor_tensor(out=g_.rearrange("p (b c) -> p b c", b=3), in0=sp_.rearrange("p (b c) -> p b c", b=3),
                                    scalar=-1.0, in1=bcm(negA[:, 0:4], 3), op0=ALU.mult,
                                    op1=ALU.mult).then_inc(v_ba.sem, v_ba.mark("g"))
            VE.tensor_scalar(hbs[:, :], bet[:, 0:8], 0.5, None, ALU.mult).then_inc(v_ba.sem, v_ba.mark("hb"))

        def dve_ba_sample(L):
            VE.wait_ge(a_ba.sem, a_ba.at(L, "sample decay"))
            d4 = dx[0:B, :].rearrange("p (v h b) -> p v h b", v=2, h=4)
            VE.tensor_tensor(d4[:, 0], bc(egx[0:B, 0:4], B), bcm(con[0:B, K_ID:K_ID + B], 4),
                             ALU.mult).then_inc(v_ba.sem, v_ba.mark("dx0"))
            VE.tensor_tensor(d4[:, 1], bc(bet[0:B, 8:12], B), bcm(con[0:B, K_ID:K_ID + B], 4),
                             ALU.mult).then_inc(v_ba.sem, v_ba.mark("dx"))

        def act_ba(L):
            SE.wait_ge(v_ba.sem, v_ba.at(L, "bt2"))
            SE.activation(th.rearrange("p (b c) -> p b c", b=3), bt[:, :].rearrange("p (b c) -> p b c", b=3)[:, :, 0:4],
                          ACT.Tanh, scale=0.5).then_inc(a_ba.sem, a_ba.mark("tanh"))
            SE.activation(negA[:, 0:4], par[:, C_ALOG:C_ALOG + 4], ACT.Exp).then_inc(a_ba.sem, a_ba.mark("A"))
            SE.wait_ge(v_ba.sem, v_ba.at(L, "abs"))
            SE.activation(e1, ab, ACT.Exp, scale=-1.0).then_inc(a_ba.sem, a_ba.mark("exp"))

        def act_ba_ln(L):
            SE.wait_ge(v_ba.sem, v_ba.at(L, "1+e"))
            SE.activation(lnv, e1, ACT.Ln).then_inc(a_ba.sem, a_ba.mark("ln"))

        def act_ba_sample(L):
            SE.wait_ge(v_ba.sem, v_ba.at(L, "g"))
            SE.activation(egx[0:B, 0:4], g_[0:B, 8:12], ACT.Exp).then_inc(a_ba.sem, a_ba.mark("sample decay"))

        def pe_decays(L):
            TE.wait_ge(v_ba.sem, v_ba.at(L, "dx"))
            for n, k in enumerate((K_LE, K_GT, K_ONES)):
                TE.matmul(BA_[:, 304 + 8 * n:312 + 8 * n], con[:, k:k + P], g_[:, 0:8], start=True, stop=True)
            TE.matmul(BA_[:, 336:400], con[0:B, K_ONES:K_ONES + P], dx[0:B, :], start=True,
                      stop=True).then_inc(pe_ba.sem, pe_ba.mark("decays"))

        def act_decays(L):
            SE.wait_ge(pe_ba.sem, pe_ba.at(L, "decays"))
            SE.activation(eg[:, :], BA_[:, 304:328], ACT.Exp).then_inc(a_ba.sem, a_ba.mark("eg"))

        def dve_decays(L):
            VE.wait_ge(pe_ba.sem, pe_ba.at(L, "decays"))
            VE.wait_ge(a_ba.sem, a_ba.at(L, "eg"))
            VE.tensor_copy(abc[:, :], BA_[:, 336:400]).then_inc(v_ba.sem, v_ba.mark("abc"))
            VE.tensor_tensor(kbs[:, :], bet[:, 0:8], eg[:, 0:8], ALU.mult).then_inc(v_ba.sem, v_ba.mark("kb"))

        GRP = ("k", "q", "v")

        def dve_conv(L, i):
            src = craw[:, i * CW:(i + 1) * CW]
            out = cvt(GRP[i // 4], i % 4)[:, 0:T]
            VE.wait_ge(win_free.sem, win_free.at(L, i + 1))
            VE.tensor_scalar(out, src[:, 0:T], par[:, C_CONV + 4 * i:C_CONV + 4 * i + 1], None,
                             ALU.mult).then_inc(v_conv.sem, v_conv.mark("tap0", i))
            for tap in range(1, CONV_W):
                VE.wait_ge(v_conv.sem, v_conv.at(L, f"tap{tap - 1}", i))
                VE.scalar_tensor_tensor(out=out, in0=src[:, tap:tap + T], scalar=par[:, C_CONV + 4 * i + tap:C_CONV + 4 * i + tap + 1],
                                        in1=out, op0=ALU.mult, op1=ALU.add).then_inc(v_conv.sem, v_conv.mark(f"tap{tap}", i))

        def pool_conv(L, g):
            GE.wait_ge(win_free.sem, win_free.at(L, 4 * g + 4))
            if g == 0:
                GE.wait_ge(d_cst.sem, d_cst.at(L, 16))
            cs = cst[:, g * 96:(g + 1) * 96].rearrange("p (c t b) -> p c t b", c=4, t=3)
            new = craw[:, 4 * g * CW:(4 * g + 4) * CW].rearrange("p (c w) -> p c w", c=4)[:, :, T + 3:CW]
            pa4, pb4 = [t[:, :].rearrange("p (c b) -> p c b", c=4) for t in (pa_, pb_)]
            for tap in range(CONV_W):
                w = bc(par[:, C_CONV + 16 * g:C_CONV + 16 * g + 16].rearrange("p (c t) -> p c t", t=4)[:, :, tap], B)
                GE.tensor_tensor(pb4 if tap else pa4, cs[:, :, tap] if tap < 3 else new, w,
                                 ALU.mult).then_inc(g_mix.sem, g_mix.mark("mul", g, tap))
                GE.wait_ge(g_mix.sem, g_mix.at(L, "mul", g, tap))
                if tap:
                    out = pa4 if tap < 3 else cv4(GRP[g])[:, :, T:N]
                    GE.tensor_tensor(out, pa4, pb4, ALU.add).then_inc(g_mix.sem, g_mix.mark("add", g, tap))
                    GE.wait_ge(g_mix.sem, g_mix.at(L, "add", g, tap))

        def act_conv(L, g):
            grp = GRP[g]
            SE.wait_ge(v_conv.sem, v_conv.at(L, "tap3", 4 * g + 3))
            SE.wait_ge(g_mix.sem, g_mix.at(L, "add", g, 3))
            if g:
                SE.wait_ge(v_conv.sem, v_conv.at(L, "silu", g - 1))
            SE.activation(act_scr, cv[:, cv_off(grp):cv_off(grp) + 4 * N], ACT.Tanh,
                          scale=0.5).then_inc(a_conv.sem, a_conv.mark("tanh", g))

        def act_conv_sq(L, g):
            grp = GRP[g]
            SE.wait_ge(v_conv.sem, v_conv.at(L, "silu", g))
            if grp == "q":
                SE.wait_ge(pe_dn.sem, pe_dn.at(L, "stats", "k"))
            SE.activation(sq4, cv[:, cv_off(grp):cv_off(grp) + 4 * N], ACT.Square).then_inc(a_conv.sem, a_conv.mark("sq", grp))

        def cv_off(grp):
            return {"q": 0, "k": 4, "v": 8}[grp] * N

        def dve_silu(L, g):
            grp = GRP[g]
            VE.wait_ge(a_conv.sem, a_conv.at(L, "tanh", g))
            t = cv[:, cv_off(grp):cv_off(grp) + 4 * N]
            VE.scalar_tensor_tensor(out=t, in0=act_scr, scalar=1.0, in1=t, op0=ALU.add,
                                    op1=ALU.mult).then_inc(v_conv.sem, v_conv.mark("silu", g))

        def pe_stats(L, grp, n):
            o, c, h = {"k": 400, "q": 440}[grp], n // 4, n % 4
            s3 = sq4.rearrange("p (h t) -> p h t", h=4)
            if n == 0:
                TE.wait_ge(a_conv.sem, a_conv.at(L, "sq", grp))
            TE.matmul(B7[:, o + n:o + n + 1], s3[:, h, tok(c)], one_col, start=True, stop=True)
            if n == 7:
                TE.matmul(B7[:, o + 8:o + 40], ones, s3[:, :, T:N], start=True,
                          stop=True).then_inc(pe_dn.sem, pe_dn.mark("stats", grp))

        def dve_stats(L, grp):
            o = {"k": 0, "q": 40}[grp]
            VE.wait_ge(pe_dn.sem, pe_dn.at(L, "stats", grp))
            VE.tensor_scalar(st[:, o:o + 40], B7[:, 400 + o:440 + o], 1.0, 4 * EPS, ALU.mult,
                             ALU.add).then_inc(v_dn.sem, v_dn.mark("ss", grp))

        def pool_stats(L, grp):
            o = {"k": 0, "q": 40}[grp]
            GE.wait_ge(v_dn.sem, v_dn.at(L, "ss", grp))
            GE.tensor_tensor(rkq[:, o:o + 8], st[:, o:o + 8], mhalf[:, 0:8], ALU.pow).then_inc(g_mix.sem, g_mix.mark("rsqrt", grp))

        def pool_stats_sample(L, grp):
            o = {"k": 8, "q": 48}[grp]
            GE.tensor_tensor(rkq[:, o:o + 32], st[:, o:o + 32], mhalf[:, 0:32],
                             ALU.pow).then_inc(g_mix.sem, g_mix.mark("rsqrt sample", grp))

        def dve_q_factor(L):
            VE.wait_ge(g_mix.sem, g_mix.at(L, "rsqrt", "q"))
            VE.tensor_scalar(rkq[:, 40:48], rkq[:, 40:48], float(DK) ** -0.5, None, ALU.mult).then_inc(v_dn.sem, v_dn.mark("rq"))
            VE.wait_ge(v_dn.sem, v_dn.at(L, "rq"))
            VE.tensor_tensor(rqg[:, :], rkq[:, 40:48], eg[:, 0:8], ALU.mult).then_inc(v_dn.sem, v_dn.mark("rqg"))

        def dve_sample_kq(L, grp):
            VE.wait_ge(g_mix.sem, g_mix.at(L, "rsqrt sample", grp))
            n, o, scale = {"k": (0, 8, 1.0), "q": (32, 48, float(DK) ** -0.5)}[grp]
            VE.scalar_tensor_tensor(out=kq2[:, n:n + 32].rearrange("p (h b) -> p h b", h=4), in0=cv4(grp)[:, :, T:N], scalar=scale,
                                    in1=rkq[:, o:o + 32].rearrange("p (h b) -> p h b", h=4), op0=ALU.mult,
                                    op1=ALU.mult).then_inc(v_dn.sem, v_dn.mark("sample", grp))

        def dve_decay_lhs(L, c):
            if c:
                VE.wait_ge(d_conv.sem, d_conv.at(L, 48))
                VE.wait_ge(g_mix.sem, g_mix.at(L, "add", 2, 3))
            for h in range(H):
                VE.tensor_scalar(hs(M[c]["B"], h), con[:, K_LE:K_LE + P], g_[:, 4 * c + h:4 * c + h + 1], None,
                                 ALU.mult).then_inc(v_dn.sem, v_dn.mark("tg", c, h))

        def pe_decay(L, c):
            TE.wait_ge(v_dn.sem, v_dn.at(L, "tg", c, 3))
            for h in range(H):
                mm = TE.matmul(hs(CB[c][0], h), hs(M[c]["B"], h), con[:, K_GT:K_GT + P], start=True, stop=True)
            mm.then_inc(pe_dn.sem, pe_dn.mark("D", c))

        def act_decay(L, c):
            SE.wait_ge(pe_dn.sem, pe_dn.at(L, "D", c))
            SE.activation(M[c]["P"][:, :], CB[c][0][:, :], ACT.Exp).then_inc(a_dn.sem, a_dn.mark("E", c))

        def dve_decay(L, c):
            VE.wait_ge(a_dn.sem, a_dn.at(L, "E", c))
            VE.tensor_tensor(hd4(M[c]["P"][:, :]), hd4(M[c]["P"][:, :]), bcm(con[:, K_TRIL:K_TRIL + P], 4),
                             ALU.mult).then_inc(v_dn.sem, v_dn.mark("E", c))

        def pe_turn(L, c, src, bank, name, wait):
            TE.wait_ge(wait[0].sem, wait[0].at(L, *wait[1]))
            for h in range(H):
                mm = TE.transpose(hs(bank, h), src(h), ident)
            mm.then_inc(pe_dn.sem, pe_dn.mark(name, c))

        def pe_k_turn(L, c):
            TE.wait_ge(a_dn.sem, a_dn.at(L, "E", c))
            pe_turn(L, c, lambda h: cvt("k", h)[:, tok(c)], CB[c][0], "k tok", (v_conv, ("silu", 0)))

        def dve_kn(L, c):
            VE.wait_ge(pe_dn.sem, pe_dn.at(L, "k tok", c))
            VE.wait_ge(g_mix.sem, g_mix.at(L, "rsqrt", "k"))
            VE.tensor_tensor(hd4(M[c]["K"][:, :]), hd4(CB[c][0][:, :]), bc(rkq[:, 4 * c:4 * c + 4], P),
                             ALU.mult).then_inc(v_dn.sem, v_dn.mark("K", c))

        def pe_kT(L, c):
            pe_turn(L, c, lambda h: hs(M[c]["K"], h), CB[c][1], "kT", (v_dn, ("K", c)))

        def act_kT(L, c):
            SE.wait_ge(pe_dn.sem, pe_dn.at(L, "kT", c))
            SE.copy(M[c]["T"][:, :], CB[c][1][:, :]).then_inc(a_dn.sem, a_dn.mark("kT", c))

        def pe_kk(L, c):
            TE.wait_ge(a_dn.sem, a_dn.at(L, "kT", c))
            for h in range(H):
                mm = TE.matmul(hs(CB[c][0], h), hs(M[c]["T"], h), hs(M[c]["T"], h), start=True, stop=True)
            mm.then_inc(pe_dn.sem, pe_dn.mark("kk", c))

        def dve_A(L, c):
            VE.wait_ge(pe_dn.sem, pe_dn.at(L, "kk", c))
            VE.wait_ge(v_dn.sem, v_dn.at(L, "E", c))
            for h in range(H):
                VE.scalar_tensor_tensor(out=hs(M[c]["Y"], h), in0=hs(CB[c][0], h), scalar=bet[:, 4 * c + h:4 * c + h + 1],
                                        in1=hs(M[c]["P"], h), op0=ALU.mult, op1=ALU.mult).then_inc(v_dn.sem, v_dn.mark("A", c, h))

        def pe_B(L, c):
            pe_turn(L, c, lambda h: hs(M[c]["Y"], h), CB[c][1], "B", (v_dn, ("A", c, 3)))

        def act_B(L, c):
            SE.wait_ge(pe_dn.sem, pe_dn.at(L, "B", c))
            SE.copy(M[c]["B"][:, :], CB[c][1][:, :]).then_inc(a_dn.sem, a_dn.mark("B", c))

        def dve_U0(L, c):
            VE.wait_ge(a_dn.sem, a_dn.at(L, "B", c))
            VE.tensor_tensor(hd4(M[c]["U"][:, :]), hd4(M[c]["B"][:, :]), bcm(con[:, K_M0:K_M0 + P], 4),
                             ALU.mult).then_inc(v_dn.sem, v_dn.mark("U00", c))
            VE.wait_ge(v_dn.sem, v_dn.at(L, "U00", c))
            VE.tensor_tensor(hd4(M[c]["U"][:, :]), bcm(ident, 4), hd4(M[c]["U"][:, :]),
                             ALU.subtract).then_inc(v_dn.sem, v_dn.mark("U0", c))

        def pe_T0(L, c):
            TE.wait_ge(a_dn.sem, a_dn.at(L, "B", c))
            pe_turn(L, c, lambda h: hs(M[c]["U"], h), CB[c][1], "T0", (v_dn, ("U0", c)))

        def act_T0(L, c):
            SE.wait_ge(pe_dn.sem, pe_dn.at(L, "T0", c))
            SE.copy(M[c]["T"][:, :], CB[c][1][:, :]).then_inc(a_dn.sem, a_dn.mark("T0", c))

        def even(t, h, s):
            return hs(t, h).rearrange("p (n two e) -> p n two e", two=2, e=s)[:, :, 0]

        def pe_Y(L, c, lv):
            if lv == 1:
                TE.wait_ge(a_dn.sem, a_dn.at(L, "T0", c))
            else:
                TE.wait_ge(a_dn.sem, a_dn.at(L, "U", c, lv - 1))
            for h in range(H):
                mm = TE.matmul(CB[c][0][:, 64 * h:64 * h + 64], hs(M[c]["B"], h), even(M[c]["T"], h, 2 ** lv),
                               start=True, stop=True)
            mm.then_inc(pe_dn.sem, pe_dn.mark("Y", c, lv))

        def dve_Y(L, c, lv):
            VE.wait_ge(pe_dn.sem, pe_dn.at(L, "Y", c, lv))
            VE.tensor_tensor(hd4(M[c]["Y"][:, 0:256]), hd4(CB[c][0][:, 0:256]),
                             bcm(con[:, K_LEV + 64 * (lv - 1):K_LEV + 64 * lv], 4),
                             ALU.mult).then_inc(v_dn.sem, v_dn.mark("Y", c, lv))

        def pe_Z(L, c, lv):
            TE.wait_ge(v_dn.sem, v_dn.at(L, "Y", c, lv))
            if lv > 1:
                TE.wait_ge(a_dn.sem, a_dn.at(L, "U", c, lv - 1))
            for h in range(H):
                mm = TE.matmul(CB[c][1][:, 64 * h:64 * h + 64], hs(M[c]["U"], h), M[c]["Y"][:, 64 * h:64 * h + 64],
                               start=True, stop=True)
            mm.then_inc(pe_dn.sem, pe_dn.mark("Z", c, lv))

        def dve_Z(L, c, lv):
            VE.wait_ge(pe_dn.sem, pe_dn.at(L, "Z", c, lv))
            s = 2 ** lv
            t = M[c]["T"][:, :].rearrange("p (n two e) -> p n two e", two=2, e=s)[:, :, 0]
            VE.tensor_tensor(t, t, CB[c][1][:, 0:256].rearrange("p (n e) -> p n e", e=s),
                             ALU.subtract).then_inc(v_dn.sem, v_dn.mark("T", c, lv))

        def pe_U(L, c, lv):
            pe_turn(L, c, lambda h: hs(M[c]["T"], h), CB[c][0], f"U{lv}", (v_dn, ("T", c, lv)))

        def act_U(L, c, lv):
            SE.wait_ge(pe_dn.sem, pe_dn.at(L, f"U{lv}", c))
            SE.copy(M[c]["U"][:, :], CB[c][0][:, :]).then_inc(a_dn.sem, a_dn.mark("U", c, lv))

        QKB = BA_

        def pe_qk_product(L, c):
            TE.wait_ge(v_conv.sem, v_conv.at(L, "silu", 1))
            TE.wait_ge(a_dn.sem, a_dn.at(L, "kT", c))
            if c:
                TE.wait_ge(a_at.sem, a_at.at(L, "vtok"))
            else:
                TE.wait_ge(v_ba.sem, v_ba.at(L, "kb"))
            for h in range(H):
                mm = TE.matmul(hs(QKB, h), cvt("q", h)[:, tok(c)], hs(M[c]["T"], h), start=True, stop=True)
            mm.then_inc(pe_dn.sem, pe_dn.mark("qk", c))

        def dve_qk(L, c):
            VE.wait_ge(pe_dn.sem, pe_dn.at(L, "qk", c))
            VE.wait_ge(v_dn.sem, v_dn.at(L, "rq"))
            for h in range(H):
                VE.scalar_tensor_tensor(out=hs(M[c]["P"], h), in0=hs(QKB, h), scalar=rkq[:, 40 + 4 * c + h:41 + 4 * c + h],
                                        in1=hs(M[c]["P"], h), op0=ALU.mult, op1=ALU.mult).then_inc(v_dn.sem, v_dn.mark("P", c, h))

        def pe_PT(L, c):
            pe_turn(L, c, lambda h: hs(M[c]["P"], h), QKB, "PT", (v_dn, ("P", c, 3)))

        def act_PT(L, c):
            SE.wait_ge(pe_dn.sem, pe_dn.at(L, "PT", c))
            SE.copy(M[c]["P"][:, :], QKB[:, :]).then_inc(a_dn.sem, a_dn.mark("PT", c))

        def pe_v_turn(L, c):
            TE.wait_ge(v_dn.sem, v_dn.at(L, "T", c, 6))
            pe_turn(L, c, lambda h: cvt("v", h)[:, tok(c)], CB[c][1], "v tok", (v_conv, ("silu", 2)))

        def dve_bV(L, c):
            VE.wait_ge(pe_dn.sem, pe_dn.at(L, "v tok", c))
            VE.tensor_tensor(hd4(M[c]["B"][:, :]), hd4(CB[c][1][:, :]), bc(hbs[:, 4 * c:4 * c + 4], P),
                             ALU.mult).then_inc(v_dn.sem, v_dn.mark("bV", c))
            if c:
                VE.wait_ge(pe_dn.sem, pe_dn.at(L, "U6", c))
                VE.tensor_tensor(hd4(M[c]["T"][:, :]), hd4(M[c]["K"][:, :]), bc(kbs[:, 4 * c:4 * c + 4], P),
                                 ALU.mult).then_inc(v_dn.sem, v_dn.mark("Kb"))
            VE.tensor_tensor(hd4(M[c]["Y"][:, :]), hd4(M[c]["K"][:, :]), bc(eg[:, 8 + 4 * c:12 + 4 * c], P),
                             ALU.mult).then_inc(v_dn.sem, v_dn.mark("Kdec", c))

        def pe_u0(L):
            TE.wait_ge(v_dn.sem, v_dn.at(L, "Kdec", 1))
            TE.wait_ge(a_dn.sem, a_dn.at(L, "U", 0, 6))
            TE.wait_ge(a_dn.sem, a_dn.at(L, "U", 1, 6))
            for h in range(H):
                mm = TE.matmul(hs(CB[0][0], h), hs(M[0]["U"], h), hs(M[0]["B"], h), start=True, stop=True)
            mm.then_inc(pe_dn.sem, pe_dn.mark("u0"))
            for h in range(H):
                mm = TE.matmul(hs(CB[1][1], h), hs(M[1]["T"], h), hs(M[1]["U"], h), start=True, stop=True)
            mm.then_inc(pe_dn.sem, pe_dn.mark("wT"))

        def act_u0(L):
            SE.wait_ge(pe_dn.sem, pe_dn.at(L, "u0"))
            SE.copy(M[0]["K"][:, :], CB[0][0][:, :]).then_inc(a_dn.sem, a_dn.mark("u0"))
            SE.wait_ge(pe_dn.sem, pe_dn.at(L, "wT"))
            SE.activation(M[0]["T"][:, :], CB[1][1][:, :], ACT.Copy, scale=-1.0).then_inc(a_dn.sem, a_dn.mark("wT"))

        def pe_S1(L):
            TE.wait_ge(a_dn.sem, a_dn.at(L, "u0"))
            for h in range(H):
                mm = TE.matmul(hs(CB[0][0], h), hs(M[0]["Y"], h), hs(M[0]["K"], h), start=True, stop=True)
            mm.then_inc(pe_dn.sem, pe_dn.mark("S1"))
            for h in range(H):
                mm = TE.matmul(hs(CB[0][1], h), hs(M[0]["P"], h), hs(M[0]["K"], h), start=True, stop=True)
            mm.then_inc(pe_dn.sem, pe_dn.mark("o0"))

        def act_S1(L):
            SE.wait_ge(pe_dn.sem, pe_dn.at(L, "S1"))
            SE.copy(M[0]["U"][:, :], CB[0][0][:, :]).then_inc(a_dn.sem, a_dn.mark("S1"))

        def dve_o0(L):
            VE.wait_ge(pe_dn.sem, pe_dn.at(L, "o0"))
            VE.tensor_copy(M[0]["B"][:, :], CB[0][1][:, :]).then_inc(v_dn.sem, v_dn.mark("o", 0))

        def pe_u1(L):
            TE.wait_ge(a_dn.sem, a_dn.at(L, "S1"))
            for h in range(H):
                TE.matmul(hs(CB[1][0], h), hs(M[1]["U"], h), hs(M[1]["B"], h), start=True, stop=False)
                mm = TE.matmul(hs(CB[1][0], h), hs(M[0]["T"], h), hs(M[0]["U"], h), start=False, stop=True)
            mm.then_inc(pe_dn.sem, pe_dn.mark("u1"))
            for h in range(H):
                mm = TE.matmul(hs(CB[1][1], h), cvt("q", h)[:, tok(1)], hs(M[0]["U"], h), start=True, stop=True)
            mm.then_inc(pe_dn.sem, pe_dn.mark("qS"))

        def act_u1(L):
            SE.wait_ge(pe_dn.sem, pe_dn.at(L, "u1"))
            SE.copy(M[1]["K"][:, :], CB[1][0][:, :]).then_inc(a_dn.sem, a_dn.mark("u1"))

        def dve_qS(L):
            VE.wait_ge(pe_dn.sem, pe_dn.at(L, "qS"))
            VE.tensor_tensor(hd4(M[0]["P"][:, :]), hd4(CB[1][1][:, :]), bc(rqg[:, 4:8], P),
                             ALU.mult).then_inc(v_dn.sem, v_dn.mark("qS"))

        def pe_o1(L):
            TE.wait_ge(a_dn.sem, a_dn.at(L, "u1"))
            TE.wait_ge(v_dn.sem, v_dn.at(L, "o", 0))
            for h in range(H):
                mm = TE.matmul(hs(CB[0][1], h), hs(M[1]["P"], h), hs(M[1]["K"], h), start=True, stop=True)
            mm.then_inc(pe_dn.sem, pe_dn.mark("o1"))
            for h in range(H):
                mm = TE.matmul(hs(CB[0][0], h), hs(M[1]["Y"], h), hs(M[1]["K"], h), start=True, stop=True)
            mm.then_inc(pe_dn.sem, pe_dn.mark("S2"))

        def dve_o1(L):
            VE.wait_ge(pe_dn.sem, pe_dn.at(L, "o1"))
            VE.wait_ge(v_dn.sem, v_dn.at(L, "qS"))
            VE.tensor_tensor(M[1]["B"][:, :], CB[0][1][:, :], M[0]["P"][:, :], ALU.add).then_inc(v_dn.sem, v_dn.mark("o", 1))
            VE.wait_ge(pe_dn.sem, pe_dn.at(L, "S2"))
            for h in range(H):
                VE.scalar_tensor_tensor(out=hs(M[0]["K"], h), in0=hs(M[0]["U"], h), scalar=eg[:, 20 + h:21 + h],
                                        in1=hs(CB[0][0], h), op0=ALU.mult, op1=ALU.add).then_inc(v_dn.sem, v_dn.mark("S2", h))

        def act_onorm(L, c):
            SE.wait_ge(v_dn.sem, v_dn.at(L, "o", c))
            for h in range(H):
                SE.activation(hs(M[0][("T", "Y")[c]], h), hs(M[c]["B"], h), ACT.Square,
                              accum_out=oss[:, 4 * c + h:4 * c + h + 1]).then_inc(a_dn.sem, a_dn.mark("oss", c, h))

        def dve_onorm(L):
            VE.wait_ge(a_dn.sem, a_dn.at(L, "oss", 1, 3))
            VE.tensor_scalar(ovar[:, :], oss[:, :], 1.0 / DK, EPS, ALU.mult, ALU.add).then_inc(v_dn.sem, v_dn.mark("ovar"))

        def pool_onorm(L):
            GE.wait_ge(v_dn.sem, v_dn.at(L, "ovar"))
            GE.tensor_tensor(orst[:, :], ovar[:, :], mhalf[:, 0:8], ALU.pow).then_inc(g_mix.sem, g_mix.mark("orst"))

        def dve_oscale(L):
            VE.wait_ge(g_mix.sem, g_mix.at(L, "orst"))
            for c in range(2):
                VE.tensor_tensor(hd4(M[c]["B"][:, :]), hd4(M[c]["B"][:, :]), bc(orst[:, 4 * c:4 * c + 4], P),
                                 ALU.mult).then_inc(v_dn.sem, v_dn.mark("on", c))

        def pe_oT(L, c):
            if c == 0:
                TE.wait_ge(a_dn.sem, a_dn.at(L, "u1"))
            else:
                TE.wait_ge(v_dn.sem, v_dn.at(L, "qS"))
            pe_turn(L, c, lambda h: hs(M[c]["B"], h), CB[1][c], "oT", (v_dn, ("on", c)))

        def dve_oT(L, c):
            VE.wait_ge(pe_dn.sem, pe_dn.at(L, "oT", c))
            if c == 0:
                VE.wait_ge(v_gate.sem, v_gate.at(L, "z"))
            z4 = z[:, :].rearrange("p (h t) -> p h t", h=4)
            VE.tensor_tensor(z4[:, :, tok(c)], hd4(CB[1][c][:, :]), z4[:, :, tok(c)],
                             ALU.mult).then_inc(v_dn.sem, v_dn.mark("od", c))

        def act_od(L):
            SE.wait_ge(v_dn.sem, v_dn.at(L, "od", 1))
            SE.wait_ge(v_sd.sem, v_sd.at(L, "od"))
            SE.wait_ge(pe_sd.sem, pe_sd.at(L, "pred"))
            SE.copy(odh[:, :], z[:, :]).then_inc(a_dn.sem, a_dn.mark("odh"))

        def dve_od(L):
            VE.wait_ge(a_dn.sem, a_dn.at(L, "odh"))
            VE.tensor_tensor(odl[:, :], z[:, :], odh[:, :].bitcast(F32), ALU.subtract).then_inc(v_dn.sem, v_dn.mark("odl"))

        def act_z(L):
            SE.wait_ge(win_free.sem, win_free.at(L, 22))
            SE.activation(z_scr, z[:, :], ACT.Tanh, scale=0.5).then_inc(a_gate.sem, a_gate.mark("z"))

        def dve_z(L):
            VE.wait_ge(a_gate.sem, a_gate.at(L, "z"))
            VE.scalar_tensor_tensor(out=z[:, :], in0=z_scr, scalar=1.0, in1=z[:, :], op0=ALU.add,
                                    op1=ALU.mult).then_inc(v_gate.sem, v_gate.mark("z0"))
            VE.wait_ge(v_gate.sem, v_gate.at(L, "z0"))
            VE.tensor_scalar(z[:, :], z[:, :], par[:, C_ONORM:C_ONORM + 1], 0.5, ALU.mult,
                             ALU.mult).then_inc(v_gate.sem, v_gate.mark("z"))

        def act_gate(L, m):
            SE.wait_ge(win_free.sem, win_free.at(L, 22 + 2 * m + 2))
            t = gt[:, 2 * m * N:(2 * m + 2) * N]
            SE.activation(t, t, ACT.Tanh, scale=0.5).then_inc(a_gate.sem, a_gate.mark("gate", m))
        def act_k_sq(L):
            SE.wait_ge(win_free.sem, win_free.at(L, 13))
            SE.activation(k_scr, ak[:, :], ACT.Square).then_inc(a_at.sem, a_at.mark("k sq"))

        def pe_k_rope(L):
            TE.wait_ge(win_free.sem, win_free.at(L, 13))
            TE.matmul(B7[:, 0:N], con[:, K_PERM:K_PERM + P], ak[:, :], start=True, stop=True)
            TE.wait_ge(a_at.sem, a_at.at(L, "k sq"))
            for b, (c0, c1, _, p1) in enumerate(BLK):
                mm = TE.matmul(B7[0:p1, 300 + 2 * b:302 + 2 * b], k_scr[:, c0:c1], con[:, K_BLK2:K_BLK2 + 2],
                               start=True, stop=True)
            mm.then_inc(pe_at.sem, pe_at.mark("k rope"))

        def dve_rope(L, src, out, w, wr, key):
            VE.scalar_tensor_tensor(out=rope_a, in0=src, scalar=par[:, w:w + 1], in1=con[:, K_COS:K_COS + N],
                                    op0=ALU.mult, op1=ALU.mult).then_inc(v_at.sem, v_at.mark("cos", key))
            VE.scalar_tensor_tensor(out=rope_b, in0=B7[:, 0:N], scalar=par[:, wr:wr + 1], in1=con[:, K_SIN:K_SIN + N],
                                    op0=ALU.mult, op1=ALU.mult).then_inc(v_at.sem, v_at.mark("sin", key))
            VE.wait_ge(v_at.sem, v_at.at(L, "sin", key))
            VE.tensor_tensor(out, rope_a, rope_b, ALU.add).then_inc(v_at.sem, v_at.mark("rope", key))

        def dve_k_rope(L):
            VE.wait_ge(pe_at.sem, pe_at.at(L, "k rope"))
            VE.tensor_scalar(avar[:, 0:4], B7[:, 300:304], 1.0 / HEAD_DIM, EPS, ALU.mult, ALU.add).then_inc(v_at.sem, v_at.mark("kv0"))
            VE.tensor_scalar(avar[0:B, 4:6], B7[0:B, 304:306], 1.0 / HEAD_DIM, EPS, ALU.mult, ALU.add).then_inc(v_at.sem, v_at.mark("kvar"))
            dve_rope(L, ak[:, :], kT[:, :], C_KW, C_KWR, "k")

        def pool_k(L):
            GE.wait_ge(v_at.sem, v_at.at(L, "kvar"))
            GE.tensor_tensor(arst[:, :], avar[:, :], mhalf[:, 0:6], ALU.pow).then_inc(g_mix.sem, g_mix.mark("k rsqrt"))

        def pe_k_turn_att(L):
            TE.wait_ge(v_at.sem, v_at.at(L, "rope", "k"))
            TE.wait_ge(a_dn.sem, a_dn.at(L, "PT", 0))
            for b, (c0, c1, _, p1) in enumerate(BLK):
                mm = turn(BA_[0:p1, b * P:(b + 1) * P], kT[:, c0:c1])
            mm.then_inc(pe_at.sem, pe_at.mark("k tok"))

        def dve_k_norm(L):
            VE.wait_ge(pe_at.sem, pe_at.at(L, "k tok"))
            VE.wait_ge(g_mix.sem, g_mix.at(L, "k rsqrt"))
            k3 = ktok[:, 0:2 * P].rearrange("p (g d) -> p g d", d=HEAD_DIM)
            VE.tensor_tensor(k3, BA_[:, 0:2 * P].rearrange("p (g d) -> p g d", d=HEAD_DIM), bc(arst[:, 0:4], HEAD_DIM),
                             ALU.mult).then_inc(v_at.sem, v_at.mark("ktok0"))
            VE.tensor_tensor(ktok[0:B, 2 * P:3 * P].rearrange("p (g d) -> p g d", d=HEAD_DIM),
                             BA_[0:B, 2 * P:3 * P].rearrange("p (g d) -> p g d", d=HEAD_DIM), bc(arst[0:B, 4:6], HEAD_DIM),
                             ALU.mult).then_inc(v_at.sem, v_at.mark("ktok"))

        def pe_k_back(L):
            TE.wait_ge(v_at.sem, v_at.at(L, "ktok"))
            for b, (c0, c1, _, p1) in enumerate(BLK):
                mm = turn(B7[:, c0:c1], ktok[0:p1, b * P:(b + 1) * P])
            mm.then_inc(pe_at.sem, pe_at.mark("kT"))

        def dve_k_back(L):
            VE.wait_ge(pe_at.sem, pe_at.at(L, "kT"))
            VE.tensor_copy(kT[:, :], B7[:, 0:N]).then_inc(v_at.sem, v_at.mark("kT"))

        def pe_v_turn_att(L):
            TE.wait_ge(win_free.sem, win_free.at(L, 14))
            TE.wait_ge(v_at.sem, v_at.at(L, "ktok"))
            for b, (c0, c1, _, p1) in enumerate(BLK):
                mm = turn(BA_[0:p1, b * P:(b + 1) * P], av[:, c0:c1])
            mm.then_inc(pe_at.sem, pe_at.mark("v tok"))

        def act_v_tok(L):
            SE.wait_ge(pe_at.sem, pe_at.at(L, "v tok"))
            SE.copy(vtok[:, 0:2 * P], BA_[:, 0:2 * P]).then_inc(a_at.sem, a_at.mark("vtok0"))
            SE.copy(vtok[0:B, 2 * P:3 * P], BA_[0:B, 2 * P:3 * P]).then_inc(a_at.sem, a_at.mark("vtok"))

        def act_q_sq(L, t):
            SE.wait_ge(win_free.sem, win_free.at(L, 15 + t))
            if t == 0:
                SE.wait_ge(pe_dn.sem, pe_dn.at(L, "stats", "q"))
            SE.activation(sq4[:, t * N:(t + 1) * N], tile_of(aq, t), ACT.Square).then_inc(a_at.sem, a_at.mark("q sq", t))

        def pe_q_rope(L, t):
            TE.wait_ge(win_free.sem, win_free.at(L, 15 + t))
            if t == 0:
                TE.wait_ge(v_at.sem, v_at.at(L, "kT"))
            else:
                TE.wait_ge(v_at.sem, v_at.at(L, "sin", t - 1))
            TE.matmul(B7[:, 0:N], con[:, K_PERM:K_PERM + P], tile_of(aq, t), start=True,
                      stop=True).then_inc(pe_at.sem, pe_at.mark("q rot", t))

        def dve_q_rope(L, t):
            VE.wait_ge(pe_at.sem, pe_at.at(L, "q rot", t))
            VE.wait_ge(v_at.sem, v_at.at(L, "rope", "k" if t == 0 else t - 1))
            VE.wait_ge(a_at.sem, a_at.at(L, "q sq", t))
            dve_rope(L, tile_of(aq, t), tile_of(aq, t), C_QW, C_QWR, t)

        def fence(L, mm, name):
            mm.then_inc(pe_at.sem, pe_at.mark(name))
            TE.wait_ge(pe_at.sem, pe_at.at(L, name))

        def dve_q_sq(L):
            VE.wait_ge(a_at.sem, a_at.at(L, "q sq", 3))
            for kv in range(2):
                half = slice(64 * kv, 64 * kv + 64)
                VE.tensor_copy(qsq[half, 32 * kv:32 * kv + 32].rearrange("p (t b) -> p t b", t=4),
                               sq4.rearrange("p (h t) -> p h t", h=4)[half, :, T:N]).then_inc(v_at.sem, v_at.mark("q sq", kv))

        def pe_q_stats(L, n):
            t, b = n % 4, n // 4
            if n == 0:
                TE.wait_ge(a_at.sem, a_at.at(L, "q sq", 3))
                TE.wait_ge(a_dn.sem, a_dn.at(L, "PT", 1))
            s3 = sq4.rearrange("p (h t) -> p h t", h=4)
            TE.matmul(BA_[:, 400 + 8 * b + 2 * t:402 + 8 * b + 2 * t], s3[:, t, tok(b)], con[:, K_BLK2:K_BLK2 + 2],
                      start=True, stop=True)
            if n == 7:
                TE.wait_ge(v_at.sem, v_at.at(L, "q sq", 1))
                TE.matmul(BA_[0:64, 65:66], qsq[:, :], one_col, start=True, stop=True).then_inc(pe_at.sem, pe_at.mark("q stats"))

        def dve_q_stats(L):
            VE.wait_ge(pe_at.sem, pe_at.at(L, "q stats"))
            VE.tensor_scalar(qvar[:, :], BA_[:, 400:416], 1.0 / HEAD_DIM, EPS, ALU.mult, ALU.add).then_inc(v_at.sem, v_at.mark("qvar"))
            VE.tensor_scalar(svar[0:64, :], BA_[0:64, 65:66], 1.0 / HEAD_DIM, EPS, ALU.mult, ALU.add).then_inc(v_at.sem, v_at.mark("svar"))
            VE.wait_ge(v_at.sem, v_at.at(L, "rope", 3))
            for kv in range(2):
                half = slice(64 * kv, 64 * kv + 64)
                VE.tensor_tensor(prod[half, 32 * kv:32 * kv + 32].rearrange("p (t b) -> p t b", t=4),
                                 aq[:, :].rearrange("p (t n) -> p t n", t=4)[half, :, T:N], bcm(kT[half, T:N], 4),
                                 ALU.mult).then_inc(v_at.sem, v_at.mark("prod", kv))
            VE.wait_ge(g_mix.sem, g_mix.at(L, "q rsqrt"))
            VE.tensor_scalar(rqa[:, :], rqa[:, :], HEAD_DIM ** -0.5, None, ALU.mult).then_inc(v_at.sem, v_at.mark("rqa"))

        def pool_q(L):
            GE.wait_ge(v_at.sem, v_at.at(L, "svar"))
            GE.tensor_tensor(rqa[:, :], qvar[:, :], mhalf[:, 0:16], ALU.pow).then_inc(g_mix.sem, g_mix.mark("q rsqrt"))
            GE.tensor_tensor(srst[0:64, :], svar[0:64, :], mhalf[0:64, 0:1], ALU.pow).then_inc(g_mix.sem, g_mix.mark("s rsqrt"))

        def pe_s_scores(L, n):
            kv = n // 4
            if n == 0:
                TE.wait_ge(d_kc.sem, d_kc.at(L, 16))
                TE.wait_ge(v_at.sem, v_at.at(L, "rope", 3))
                TE.wait_ge(v_at.sem, v_at.at(L, "svar"))
            q3 = aq[:, :].rearrange("p (t n) -> p t n", t=4)
            half = slice(64 * kv, 64 * kv + 64)
            for b in (2 * (n % 4), 2 * (n % 4) + 1):
                mm = TE.matmul(BA_[:, 32 * kv + b:32 * kv + b + 25:8], kc[half, b * P:(b + 1) * P], q3[half, :, T + b],
                               start=True, stop=True)
            if n % 4 == 3:
                fence(L, mm, f"s scores {kv}")
            if n == 7:
                TE.wait_ge(v_at.sem, v_at.at(L, "prod", 1))
                TE.matmul(BA_[0:64, 64:65], prod[:, :], one_col, start=True, stop=True).then_inc(pe_at.sem, pe_at.mark("s scores"))

        def dve_s_scores(L):
            VE.wait_ge(pe_at.sem, pe_at.at(L, "s scores"))
            VE.tensor_copy(sT[:, :], BA_[:, 0:64]).then_inc(v_at.sem, v_at.mark("sT"))
            VE.wait_ge(g_mix.sem, g_mix.at(L, "s rsqrt"))
            VE.tensor_scalar(sl[0:64, P:P + 1], BA_[0:64, 64:65], srst[0:64, :], HEAD_DIM ** -0.5, ALU.mult,
                             ALU.mult).then_inc(v_at.sem, v_at.mark("s new"))

        def pe_s_turn(L):
            TE.wait_ge(v_at.sem, v_at.at(L, "s new"))
            turn(BA_[0:64, P:2 * P], sT[:, :]).then_inc(pe_at.sem, pe_at.mark("s turn"))

        def dve_s_soft(L):
            VE.wait_ge(pe_at.sem, pe_at.at(L, "s turn"))
            VE.tensor_scalar(sl[0:64, 0:P], BA_[0:64, P:2 * P], srst[0:64, :], HEAD_DIM ** -0.5, ALU.mult,
                             ALU.mult).then_inc(v_at.sem, v_at.mark("sl"))
            VE.wait_ge(v_at.sem, v_at.at(L, "sl"))
            VE.tensor_reduce(smax[0:64, :], sl[0:64, 0:P + 1], AX.X, ALU.max).then_inc(v_at.sem, v_at.mark("smax"))
            VE.wait_ge(v_at.sem, v_at.at(L, "smax"))
            VE.tensor_scalar(snm[0:64, :], smax[0:64, :], par[0:64, C_SINKROW:C_SINKROW + 1], -1.0, ALU.max,
                             ALU.mult).then_inc(v_at.sem, v_at.mark("snm"))

        def act_s_soft(L):
            SE.wait_ge(v_at.sem, v_at.at(L, "snm"))
            SE.activation(sl[0:64, 0:P + 1], sl[0:64, 0:P + 1], ACT.Exp, bias=snm[0:64, :],
                          accum_out=sden[0:64, :]).then_inc(a_at.sem, a_at.mark("s exp"))
            SE.activation(sesk[0:64, :], par[0:64, C_SINKROW:C_SINKROW + 1], ACT.Exp,
                          bias=snm[0:64, :]).then_inc(a_at.sem, a_at.mark("s sink"))

        def dve_s_probs(L):
            VE.wait_ge(a_at.sem, a_at.at(L, "s sink"))
            VE.tensor_tensor(sden[0:64, :], sden[0:64, :], sesk[0:64, :], ALU.add).then_inc(v_at.sem, v_at.mark("sden"))
            VE.wait_ge(v_at.sem, v_at.at(L, "sden"))
            VE.reciprocal(srec[0:64, :], sden[0:64, :]).then_inc(v_at.sem, v_at.mark("srec"))
            VE.wait_ge(v_at.sem, v_at.at(L, "srec"))
            VE.tensor_scalar(sl[0:64, 0:P + 1], sl[0:64, 0:P + 1], srec[0:64, :], None, ALU.mult).then_inc(v_at.sem, v_at.mark("probs"))
            VE.wait_ge(v_at.sem, v_at.at(L, "probs"))
            VE.tensor_scalar(rmat[0:64, :], con[0:64, K_MROW:K_MROW + 32], sl[0:64, P:P + 1], None,
                             ALU.mult).then_inc(v_at.sem, v_at.mark("rmat"))

        def pe_s_probs(L):
            TE.wait_ge(v_at.sem, v_at.at(L, "rmat"))
            turn(BA_[:, 256:320], sl[0:64, 0:P])
            TE.matmul(BA_[:, 320:352], con[0:64, K_SEL:K_SEL + P], rmat[0:64, :], start=True,
                      stop=True).then_inc(pe_at.sem, pe_at.mark("s probs"))

        def dve_s_new(L):
            VE.wait_ge(pe_at.sem, pe_at.at(L, "s probs"))
            VE.tensor_copy(pts[:, :], BA_[:, 256:320]).then_inc(v_at.sem, v_at.mark("pts"))
            VE.tensor_tensor(pvs[:, :].rearrange("p (t b) -> p t b", t=4), BA_[:, 320:352].rearrange("p (t b) -> p t b", t=4),
                             bcm(av[:, T:N], 4), ALU.mult).then_inc(v_at.sem, v_at.mark("pvs"))

        def pe_s_pv(L):
            TE.wait_ge(d_vc.sem, d_vc.at(L, 16))
            TE.wait_ge(v_at.sem, v_at.at(L, "pvs"))
            for kv in range(2):
                half = slice(64 * kv, 64 * kv + 64)
                for b in range(B):
                    mm = TE.matmul(BA_[half, 352 + b:352 + b + 25:8], vc[:, b * P + 64 * kv:b * P + 64 * kv + 64],
                                   pts[:, 32 * kv + b:32 * kv + b + 25:8], start=True, stop=True)
            mm.then_inc(pe_at.sem, pe_at.mark("s pv"))

        def dve_s_pv(L):
            VE.wait_ge(pe_at.sem, pe_at.at(L, "s pv"))
            VE.tensor_tensor(oas[:, :], BA_[:, 352:384], pvs[:, :], ALU.add).then_inc(v_at.sem, v_at.mark("oas"))

        def pe_scores(L, n):
            t, kv = n // 2, n % 2
            half, bk = slice(64 * kv, 64 * kv + 64), banks[6 + n % 2]
            if n >= 2:
                TE.wait_ge(a_at.sem, a_at.at(L, "otok", n - 2))
            elif n == 1:
                TE.wait_ge(v_at.sem, v_at.at(L, "rope", 3))
                TE.wait_ge(v_dn.sem, v_dn.at(L, "ss", "q"))
            else:
                TE.wait_ge(v_at.sem, v_at.at(L, "oas"))
            q = tile_of(aq, t)
            TE.matmul(bk[:, 0:P], q[half, 0:P], kT[half, 0:P], start=True, stop=True)
            TE.matmul(bk[:, P:3 * P], q[half, P:T], kT[half, 0:T], start=True,
                      stop=True).then_inc(pe_at.sem, pe_at.mark("scores", n))

        def dve_scores(L, n):
            VE.wait_ge(pe_at.sem, pe_at.at(L, "scores", n))
            if n >= 2:
                VE.wait_ge(pe_at.sem, pe_at.at(L, "probs", n - 2))
            s, bk = sm[n % 2], banks[6 + n % 2]
            for b, (lo, hi, m) in enumerate(((0, P, K_AM0), (P, 3 * P, K_AM1))):
                VE.scalar_tensor_tensor(out=s[:, lo:hi], in0=bk[:, lo:hi], scalar=rqa[:, 8 * b + n:8 * b + n + 1],
                                        in1=con[:, m:m + hi - lo], op0=ALU.mult, op1=ALU.add).then_inc(v_at.sem, v_at.mark("logits", n, b))
            for b, (lo, hi) in enumerate(((0, P), (P, 3 * P))):
                VE.wait_ge(v_at.sem, v_at.at(L, "logits", n, b))
                VE.tensor_reduce(mx[:, 8 * b + n:8 * b + n + 1], s[:, lo:hi], AX.X, ALU.max).then_inc(v_at.sem, v_at.mark("max", n, b))
            VE.wait_ge(v_at.sem, v_at.at(L, "max", n, 1))
            VE.tensor_scalar(nm[:, n:n + 9:8], mx[:, n:n + 9:8], par[:, C_SINK + n:C_SINK + n + 1], -1.0, ALU.max,
                             ALU.mult).then_inc(v_at.sem, v_at.mark("nm", n))

        def act_exp(L, n):
            SE.wait_ge(v_at.sem, v_at.at(L, "nm", n))
            for b, (lo, hi) in enumerate(((0, P), (P, 3 * P))):
                SE.activation(sm[n % 2][:, lo:hi], sm[n % 2][:, lo:hi], ACT.Exp, bias=nm[:, 8 * b + n:8 * b + n + 1],
                              accum_out=den[:, 8 * b + n:8 * b + n + 1]).then_inc(a_at.sem, a_at.mark("exp", n, b))

        def pe_probs(L, n):
            TE.wait_ge(a_at.sem, a_at.at(L, "exp", n, 1))
            for j in range(3):
                mm = TE.transpose(banks[6 + n % 2][:, j * P:(j + 1) * P], sm[n % 2][:, j * P:(j + 1) * P], ident)
            mm.then_inc(pe_at.sem, pe_at.mark("probs", n))

        def act_probs(L, n):
            SE.wait_ge(pe_at.sem, pe_at.at(L, "probs", n))
            if n >= 2:
                SE.wait_ge(pe_at.sem, pe_at.at(L, "pv", n - 2))
            SE.copy(ptb[n % 2], banks[6 + n % 2][:, 0:3 * P]).then_inc(a_at.sem, a_at.mark("probs", n))

        def pe_pv(L, n):
            kv, bk, p = n % 2, banks[6 + n % 2], ptb[n % 2]
            TE.wait_ge(a_at.sem, a_at.at(L, "probs", n))
            d = slice(64 * kv, 64 * kv + 64)
            TE.matmul(bk[:, 384:448], p[:, 0:P], vtok[:, 0:P][:, d], start=True, stop=True)
            TE.matmul(bk[:, 448:512], p[:, P:2 * P], vtok[:, 0:P][:, d], start=True, stop=False)
            TE.matmul(bk[:, 448:512], p[:, 2 * P:3 * P], vtok[:, P:2 * P][:, d], start=False,
                      stop=True).then_inc(pe_at.sem, pe_at.mark("pv", n))

        def act_pv(L, n):
            SE.wait_ge(pe_at.sem, pe_at.at(L, "pv", n))
            SE.copy(otok[:, :].rearrange("p (b c) -> p b c", b=2)[:, :, 64 * n:64 * n + 64],
                    banks[6 + n % 2][:, 384:512].rearrange("p (b c) -> p b c", b=2)).then_inc(a_at.sem, a_at.mark("otok", n))

        def dve_den(L):
            VE.wait_ge(v_at.sem, v_at.at(L, "nm", 7))
            VE.tensor_tensor(esk[:, :].rearrange("p (b n) -> p b n", b=2), nm[:, :].rearrange("p (b n) -> p b n", b=2),
                             bcm(par[:, C_SINK:C_SINK + 8], 2), ALU.add).then_inc(v_at.sem, v_at.mark("esk"))
            VE.wait_ge(a_at.sem, a_at.at(L, "sink"))
            VE.tensor_tensor(den[:, :], den[:, :], esk[:, :], ALU.add).then_inc(v_at.sem, v_at.mark("den"))
            VE.wait_ge(v_at.sem, v_at.at(L, "den"))
            VE.reciprocal(rec[:, :], den[:, :]).then_inc(v_at.sem, v_at.mark("rec"))
            VE.wait_ge(v_at.sem, v_at.at(L, "rec"))
            VE.wait_ge(a_at.sem, a_at.at(L, "otok", 7))
            for b in range(2):
                o3 = otok[:, 512 * b:512 * b + 512].rearrange("p (n d) -> p n d", d=HEAD_DIM)
                VE.tensor_tensor(o3, o3, bc(rec[:, 8 * b:8 * b + 8], HEAD_DIM), ALU.mult).then_inc(v_at.sem, v_at.mark("on", b))

        def act_sink(L):
            SE.wait_ge(v_at.sem, v_at.at(L, "esk"))
            SE.activation(esk[:, :], esk[:, :], ACT.Exp).then_inc(a_at.sem, a_at.mark("sink"))

        def pe_o_turn(L):
            for b in range(2):
                TE.wait_ge(v_at.sem, v_at.at(L, "on", b))
                for t in range(4):
                    mm = TE.transpose(banks[6 + b][:, t * P:(t + 1) * P], otok[:, 512 * b + t * P:512 * b + (t + 1) * P], ident)
                mm.then_inc(pe_at.sem, pe_at.mark("oT", b))

        def act_oa(L):
            h3 = oah[:, :].rearrange("p (t n) -> p t n", t=4)
            for b in range(2):
                SE.wait_ge(pe_at.sem, pe_at.at(L, "oT", b))
                SE.copy(h3[:, :, tok(b)], banks[6 + b][:, :].rearrange("p (t n) -> p t n", t=4)).then_inc(a_at.sem, a_at.mark("oah", b))
            SE.copy(h3[:, :, T:N], oas[:, :].rearrange("p (t b) -> p t b", t=4)).then_inc(a_at.sem, a_at.mark("oah", 2))

        def dve_oa(L):
            h3 = oah[:, :].rearrange("p (t n) -> p t n", t=4).bitcast(F32)
            l3 = oal[:, :].rearrange("p (t n) -> p t n", t=4)
            for b in range(2):
                VE.wait_ge(a_at.sem, a_at.at(L, "oah", b))
                VE.tensor_tensor(l3[:, :, tok(b)], banks[6 + b][:, :].rearrange("p (t n) -> p t n", t=4), h3[:, :, tok(b)],
                                 ALU.subtract).then_inc(v_at.sem, v_at.mark("oal", b))
            VE.wait_ge(a_at.sem, a_at.at(L, "oah", 2))
            VE.tensor_tensor(l3[:, :, T:N], oas[:, :].rearrange("p (t b) -> p t b", t=4), h3[:, :, T:N],
                             ALU.subtract).then_inc(v_at.sem, v_at.mark("oal", 2))

        def state(h, b):
            return (states, states2)[h // 2][:, (h % 2) * B * P + b * P:(h % 2) * B * P + (b + 1) * P]

        def col16(t, r):
            return t[:, 16 * r:16 * r + 16]

        def dve_qk_sample(L):
            VE.wait_ge(v_dn.sem, v_dn.at(L, "sample", "q"))
            VE.tensor_tensor(qkp[:, :], kq2[:, 0:32], kq2[:, 32:64], ALU.mult).then_inc(v_sd.sem, v_sd.mark("qkp"))

        def pe_pred(L, r, n):
            SDB, h = banks[3], 2 * r + n // 4
            if r == 0 and n == 0:
                TE.wait_ge(v_dn.sem, v_dn.at(L, "S2", 3))
                TE.wait_ge(v_sd.sem, v_sd.at(L, "qkp"))
                TE.matmul(SDB[:, 64:96], ones, qkp[:, :], start=True, stop=True)
            if n == 0:
                if r:
                    TE.wait_ge(v_sd.sem, v_sd.at(L, "o", 0))
                TE.wait_ge(d_state[r].sem, d_state[r].at(L, 16))
            k3 = kq2[:, :].rearrange("p (v s) -> p v s", v=2)
            for b in (2 * (n % 4), 2 * (n % 4) + 1):
                s = 8 * h + b
                mm = TE.matmul(SDB[:, 2 * s:2 * s + 2], state(h, b), k3[:, :, s], start=True, stop=True)
            if n == 7:
                mm.then_inc(pe_sd.sem, pe_sd.mark("pred", r))

        def dve_delta(L, r):
            SDB = banks[3]
            VE.wait_ge(pe_sd.sem, pe_sd.at(L, "pred", r))
            if r == 0:
                VE.tensor_copy(qkb[:, :], SDB[:, 64:96]).then_inc(v_sd.sem, v_sd.mark("qkb"))
            pr = SDB[:, 32 * r:32 * r + 32].rearrange("p (s v) -> p s v", v=2)
            a, bt_, d, t = col16(abc, r), abc[:, 32 + 16 * r:48 + 16 * r], col16(dlt, r), col16(tmp32, r)
            VE.tensor_tensor(d, pr[:, :, 0], a, ALU.mult).then_inc(v_sd.sem, v_sd.mark("a pk", r))
            VE.tensor_tensor(t, pr[:, :, 1], a, ALU.mult).then_inc(v_sd.sem, v_sd.mark("a pq", r))
            VE.wait_ge(v_sd.sem, v_sd.at(L, "a pk", r))
            v2 = cv4("v")[:, 2 * r:2 * r + 2, T:N]
            VE.scalar_tensor_tensor(out=d.rearrange("p (h b) -> p h b", h=2), in0=v2, scalar=0.5,
                                    in1=d.rearrange("p (h b) -> p h b", h=2), op0=ALU.mult,
                                    op1=ALU.subtract).then_inc(v_sd.sem, v_sd.mark("v-", r))
            VE.wait_ge(v_sd.sem, v_sd.at(L, "v-", r))
            VE.tensor_tensor(d, d, bt_, ALU.mult).then_inc(v_sd.sem, v_sd.mark("delta", r))
            VE.wait_ge(v_sd.sem, v_sd.at(L, "delta", r))
            VE.tensor_tensor(col16(osq, r), col16(qkb, r), d, ALU.mult).then_inc(v_sd.sem, v_sd.mark("qk d", r))
            VE.wait_ge(v_sd.sem, v_sd.at(L, "qk d", r))
            VE.tensor_tensor(t, t, col16(osq, r), ALU.add).then_inc(v_sd.sem, v_sd.mark("o", r))
            if r:
                VE.wait_ge(v_sd.sem, v_sd.at(L, "o", 1))
                VE.tensor_tensor(osq[:, :], tmp32[:, :], tmp32[:, :], ALU.mult).then_inc(v_sd.sem, v_sd.mark("o sq"))

        def pe_rows(L, r):
            TE.wait_ge(v_sd.sem, v_sd.at(L, "delta", r))
            if r:
                TE.wait_ge(a_sd.sem, a_sd.at(L, "rows", 0))
            for j in range(2):
                s = 8 * (2 * r + j)
                turn(hs(banks[2][0:B, :], j), dlt[:, s:s + B])
                mm = turn(hs(banks[2][0:B, :], 2 + j), kq2[:, s:s + B])
            mm.then_inc(pe_sd.sem, pe_sd.mark("rows", r))

        def act_rows(L, r):
            SE.wait_ge(pe_sd.sem, pe_sd.at(L, "rows", r))
            if r:
                SE.wait_ge(d_kv.sem, d_kv.at(L, 64))
            SE.copy((rows0, rows1)[r][0:B, :], banks[2][0:B, :]).then_inc(a_sd.sem, a_sd.mark("rows", r))

        def drow(h):
            return (otok, smx)[h % 2][0:B, 0:B * P]

        def dve_drow(L, h):
            VE.wait_ge(a_sd.sem, a_sd.at(L, "rows", 0))
            if h == 0:
                VE.wait_ge(pe_at.sem, pe_at.at(L, "oT", 1))
            d = rows0[0:B, P * h:P * h + P]
            VE.tensor_tensor(drow(h).rearrange("p (b e) -> p b e", b=B), bcm(d, B), bc(con[0:B, K_ID:K_ID + B], P),
                             ALU.mult).then_inc(v_sd.sem, v_sd.mark("drow", h))

        def act_drow(L, h):
            if h == 2:
                SE.wait_ge(a_sd.sem, a_sd.at(L, "rows", 1))
            SE.wait_ge(pe_sd.sem, pe_sd.at(L, "outer", h - 2))
            for b in range(B):
                SE.activation(drow(h)[:, b * P:(b + 1) * P], rows1[0:B, P * (h - 2):P * (h - 1)], ACT.Copy,
                              scale=con[0:B, K_ID + b:K_ID + b + 1]).then_inc(a_sd.sem, a_sd.mark("drow", h, b))

        def outer_banks(h):
            return ((banks[2], banks[3]), (banks[4], banks[5]))[h % 2]

        def pe_outer(L, h):
            r, j = h // 2, h % 2
            if r:
                TE.wait_ge(a_sd.sem, a_sd.at(L, "drow", h, B - 1))
            else:
                TE.wait_ge(v_sd.sem, v_sd.at(L, "drow", h))
            if h == 0:
                TE.wait_ge(v_sd.sem, v_sd.at(L, "osv"))
                TE.wait_ge(a_sd.sem, a_sd.at(L, "rows", 1))
            if h == 1:
                TE.wait_ge(v_dn.sem, v_dn.at(L, "od", 1))
            if h == 2:
                TE.wait_ge(v_sd.sem, v_sd.at(L, "S", 0, 7))
            if h == 3:
                TE.wait_ge(v_sd.sem, v_sd.at(L, "S", 1, 7))
            krow = (rows0, rows1)[r][0:B, P * (2 + j):P * (3 + j)]
            for n in range(2):
                mm = TE.matmul(outer_banks(h)[n][:, :], krow, drow(h)[:, 512 * n:512 * n + 512], start=True, stop=True)
            mm.then_inc(pe_sd.sem, pe_sd.mark("outer", h))

        def dve_state(L, h):
            VE.wait_ge(pe_sd.sem, pe_sd.at(L, "outer", h))
            for b in range(B):
                s = 8 * h + b
                VE.scalar_tensor_tensor(out=state(h, b), in0=state(h, b), scalar=abc[:, s:s + 1],
                                        in1=hs(outer_banks(h)[b // 4], b % 4), op0=ALU.mult,
                                        op1=ALU.add).then_inc(v_sd.sem, v_sd.mark("S", h, b))

        def act_state_out(L, h):
            SE.wait_ge(v_sd.sem, v_sd.at(L, "S", h, 7))
            o = h * B * P
            SE.dma_start(outs["dns"][L, :, o:o + B * P], (states, states2)[h // 2][:, (h % 2) * B * P:(h % 2 + 1) * B * P]
                         ).then_inc(d_stout.sem, 16)

        def pe_onorm(L):
            TE.wait_ge(v_sd.sem, v_sd.at(L, "o sq"))
            TE.matmul(banks[3][:, 128:160], ones, osq[:, :], start=True, stop=True).then_inc(pe_sd.sem, pe_sd.mark("oss"))

        def dve_onorm_sample(L):
            VE.wait_ge(pe_sd.sem, pe_sd.at(L, "oss"))
            VE.tensor_scalar(osv[:, :], banks[3][:, 128:160], 1.0 / DK, EPS, ALU.mult, ALU.add).then_inc(v_sd.sem, v_sd.mark("osv"))

        def pool_onorm_sample(L):
            GE.wait_ge(v_sd.sem, v_sd.at(L, "osv"))
            GE.tensor_tensor(osr[:, :], osv[:, :], mhalf[:, 0:32], ALU.pow).then_inc(g_mix.sem, g_mix.mark("osr"))

        def dve_od_sample(L):
            VE.wait_ge(g_mix.sem, g_mix.at(L, "osr"))
            VE.tensor_tensor(tmp32[:, :], tmp32[:, :], osr[:, :], ALU.mult).then_inc(v_sd.sem, v_sd.mark("on"))
            VE.wait_ge(v_sd.sem, v_sd.at(L, "on"))
            z3 = z[:, :].rearrange("p (h t) -> p h t", h=4)[:, :, T:N]
            VE.tensor_tensor(z3, z3, tmp32[:, :].rearrange("p (h b) -> p h b", h=4),
                             ALU.mult).then_inc(v_sd.sem, v_sd.mark("od"))

        def pe_branches(L, m, branch):
            u, t0 = U_AD + m // 2, KT * (m % 2)
            if m % 2 == 0 and branch == "a":
                wait_unit(L, u)
            if m == 0 and branch == "a":
                TE.wait_ge(v_at.sem, v_at.at(L, "oal", 2))
                TE.wait_ge(win_free.sem, win_free.at(L, 38))
            if m >= 2:
                TE.wait_ge(v_ad.sem, v_ad.at(L, branch, m - 2))
            if m == 0 and branch == "d":
                TE.wait_ge(v_dn.sem, v_dn.at(L, "odl"))
            bank, t1, hi, lo = {"a": (banks[m % 2], t0, oah, oal), "d": (banks[6 + m % 2], t0 + 4, odh, odl)}[branch]
            for t in range(4):
                mm = product(bank[:, 0:N], u % RING, t1 + t, tile_of(hi, t), tile_of(lo, t), t == 0, t == 3)
            if m % 2 and branch == "d":
                mm.then_inc(w_used.sem, 1)
            else:
                mm.then_inc(pe_ad.sem, pe_ad.mark(branch, m))

        def dve_branches(L, m):
            ga, gd = tile_of(gt, 2 * m), tile_of(gt, 2 * m + 1)
            VE.wait_ge(a_gate.sem, a_gate.at(L, "gate", m))
            VE.wait_ge(pe_ad.sem, pe_ad.at(L, "a", m))
            VE.scalar_tensor_tensor(out=ga, in0=ga, scalar=1.0, in1=banks[m % 2][:, 0:N], op0=ALU.add,
                                    op1=ALU.mult).then_inc(v_ad.sem, v_ad.mark("a", m))
            if m % 2:
                VE.wait_ge(w_used.sem, w_used.at(L, U_AD + m // 2 + 1))
            else:
                VE.wait_ge(pe_ad.sem, pe_ad.at(L, "d", m))
            VE.scalar_tensor_tensor(out=gd, in0=gd, scalar=1.0, in1=banks[6 + m % 2][:, 0:N], op0=ALU.add,
                                    op1=ALU.mult).then_inc(v_ad.sem, v_ad.mark("d", m))
            VE.wait_ge(v_ad.sem, v_ad.at(L, "d", m))
            VE.tensor_tensor(ga, ga, gd, ALU.add).then_inc(v_ad.sem, v_ad.mark("mix", m))

        def act_branches(L, m):
            SE.wait_ge(v_ad.sem, v_ad.at(L, "mix", m))
            SE.copy(tile_of(mixh, m), tile_of(gt, 2 * m)).then_inc(a_ad.sem, a_ad.mark("mixh", m))

        def dve_mix_tail(L, m):
            VE.wait_ge(a_ad.sem, a_ad.at(L, "mixh", m))
            VE.tensor_tensor(mixl(m), tile_of(gt, 2 * m), tile_of(mixh, m).bitcast(F32),
                             ALU.subtract).then_inc(v_ad.sem, v_ad.mark("mixl", m))

        def pe_out(L, m):
            u, t0 = U_WO + m // 2, KT * (m % 2)
            if m % 2 == 0:
                wait_unit(L, u)
            if m < 2:
                TE.wait_ge(v_ad.sem, v_ad.at(L, "d", 7) if m else v_ad.at(L, "a", 6))
            else:
                TE.wait_ge(x_done.sem, x_done.at(L, 8 + m - 1))
            for k in range(KT):
                if m == 0:
                    TE.wait_ge(v_ad.sem, v_ad.at(L, "mixl", k))
                mm = product(banks[7 if m % 2 else 0][:, 0:N], u % RING, t0 + k, tile_of(mixh, k), mixl(k),
                             k == 0, k == KT - 1)
            mm.then_inc(w_used.sem if m % 2 else out_ready.sem, 1)

        LEV0, LEV1 = 27, 36

        def pe_slot(L, s):
            if s == 4:
                pe_ba_turn(L)
            if s == 13:
                pe_decay(L, 0)
            if s == 17:
                pe_k_turn(L, 0)
            if s == 19:
                pe_decays(L)
            if s == 20:
                pe_kT(L, 0)
            if s == 22:
                pe_kk(L, 0)
            for c, s0 in ((0, LEV0), (1, LEV1)):
                if s0 <= s < s0 + 18:
                    (pe_Y, pe_Z, pe_U)[(s - s0) % 3](L, c, (s - s0) // 3 + 1)
            if s == 24:
                pe_qk_product(L, 0)
                pe_B(L, 0)
            if s == 26:
                pe_T0(L, 0)
            if s == 27:
                pe_PT(L, 0)
            if s == 28:
                pe_decay(L, 1)
                pe_k_rope(L)
            if s == 29:
                pe_k_turn(L, 1)
            if s == 30:
                pe_k_turn_att(L)
            if s == 31:
                pe_kT(L, 1)
            if s == 32:
                pe_kk(L, 1)
                pe_k_back(L)
            if s == 33:
                pe_B(L, 1)
                pe_v_turn_att(L)
            if s == 34:
                pe_q_rope(L, 0)
            if s == 35:
                pe_qk_product(L, 1)
                pe_T0(L, 1)
            if s == 36:
                pe_q_rope(L, 1)
            if s == 37:
                pe_PT(L, 1)
            if s == 38:
                pe_q_rope(L, 2)
            if s == 40:
                pe_q_rope(L, 3)
            if s == 44:
                pe_v_turn(L, 0)
            if s == 45:
                pe_s_turn(L)
            for n in range(8):
                if s == 50 + 2 * n:
                    pe_scores(L, n)
                if s == 52 + 2 * n:
                    pe_probs(L, n)
                if s == 53 + 2 * n:
                    pe_pv(L, n)
            if s == 48:
                pe_s_probs(L)
            if s == 49:
                pe_s_pv(L)
            if s == 54:
                pe_v_turn(L, 1)
            if s == 56:
                pe_u0(L)
            if s == 57:
                pe_S1(L)
            if s == 58:
                pe_u1(L)
            if s == 60:
                pe_o1(L)
            if s == 64:
                pe_rows(L, 0)
            if s == 65:
                pe_oT(L, 0)
                pe_oT(L, 1)
            if s == 70:
                pe_o_turn(L)
                pe_rows(L, 1)
                pe_onorm(L)
            if s == 74:
                pe_outer(L, 0)
            if s == 75:
                pe_outer(L, 1)

        def dve_slot(L, s):
            if s == 5:
                dve_ba(L)
            if s == 6:
                dve_ba_beta(L)
            if s == 8:
                dve_ba_decay(L)
            if s == 9:
                dve_ba_sample(L)
            if s == 10:
                dve_decay_lhs(L, 0)
            if s == 11:
                dve_silu(L, 0)
            if s == 14:
                dve_decay(L, 0)
            if s == 17:
                dve_stats(L, "k")
            if s == 18:
                dve_silu(L, 1)
                dve_kn(L, 0)
            for c, s0 in ((0, LEV0), (1, LEV1)):
                if s0 <= s < s0 + 18 and (s - s0) % 3 < 2:
                    (dve_Y, dve_Z)[(s - s0) % 3](L, c, (s - s0) // 3 + 1)
            if s == 19:
                dve_decays(L)
            if s == 22:
                dve_A(L, 0)
            if s == 23:
                dve_stats(L, "q")
            if s == 25:
                dve_U0(L, 0)
                dve_q_factor(L)
                dve_qk(L, 0)
            if s == 27:
                dve_decay_lhs(L, 1)
            if s == 28:
                dve_decay(L, 1)
                dve_silu(L, 2)
                dve_k_rope(L)
            if s == 29:
                dve_kn(L, 1)
            if s == 30:
                dve_k_norm(L)
            if s == 32:
                dve_A(L, 1)
                dve_k_back(L)
            if s == 33:
                dve_U0(L, 1)
            if s == 34:
                dve_q_rope(L, 0)
            if s == 35:
                dve_qk(L, 1)
            if s == 36:
                dve_q_rope(L, 1)
            if s == 38:
                dve_q_rope(L, 2)
            if s == 40:
                dve_q_rope(L, 3)
                dve_q_sq(L)
            if s == 41:
                dve_q_stats(L)
            if s == 44:
                dve_s_scores(L)
            if s == 45:
                dve_bV(L, 0)
                dve_z(L)
                dve_s_soft(L)
            if s == 47:
                dve_s_probs(L)
            for n in range(8):
                if s == 50 + 2 * n:
                    dve_scores(L, n)
            if s == 48:
                dve_sample_kq(L, "k")
                dve_sample_kq(L, "q")
                dve_s_new(L)
            if s == 49:
                dve_s_pv(L)
            if s == 54:
                dve_bV(L, 1)
                dve_qk_sample(L)
            if s == 57:
                dve_o0(L)
            if s == 58:
                dve_qS(L)
            if s == 60:
                dve_o1(L)
            if s == 62:
                dve_onorm(L)
                dve_oscale(L)
            if s == 63:
                dve_delta(L, 0)
            if s == 65:
                dve_oT(L, 0)
                dve_oT(L, 1)
            if s == 68:
                dve_den(L)
                dve_delta(L, 1)
            if s == 70:
                dve_oa(L)
                dve_onorm_sample(L)
            if s == 72:
                dve_drow(L, 0)
                dve_drow(L, 1)
            if s == 74:
                dve_od_sample(L)
            if s == 75:
                dve_state(L, 0)
                dve_od(L)

        def act_slot(L, s):
            if s == 5:
                act_ba(L)
            if s == 7:
                act_ba_ln(L)
            if s == 9:
                act_ba_sample(L)
            if s == 10:
                act_conv(L, 0)
            if s == 13:
                act_conv_sq(L, 0)
                act_decay(L, 0)
            if s == 18:
                act_conv(L, 1)
            if s == 19:
                act_decays(L)
            if s == 20:
                act_conv_sq(L, 1)
                act_kT(L, 0)
            if s == 24:
                act_conv_out(L)
                act_B(L, 0)
            for c, s0 in ((0, LEV0), (1, LEV1)):
                if s0 <= s < s0 + 18 and (s - s0) % 3 == 2:
                    act_U(L, c, (s - s0) // 3 + 1)
            if s == 26:
                act_k_sq(L)
                act_T0(L, 0)
            if s == 27:
                act_PT(L, 0)
                act_conv(L, 2)
            if s == 28:
                act_decay(L, 1)
            if s == 31:
                act_kT(L, 1)
            if s == 33:
                act_B(L, 1)
                act_v_tok(L)
                act_q_sq(L, 0)
            if s == 35:
                act_T0(L, 1)
                act_q_sq(L, 1)
            if s == 37:
                act_q_sq(L, 2)
                act_PT(L, 1)
                act_kv_out(L)
            if s == 39:
                act_q_sq(L, 3)
            if s == 44:
                act_z(L)
            for n in range(8):
                if s == 50 + 2 * n:
                    act_exp(L, n)
                if s == 52 + 2 * n:
                    act_probs(L, n)
                if s == 53 + 2 * n:
                    act_pv(L, n)
            if s == 45:
                act_s_soft(L)
            if s == 50:
                act_states_in(L, 0)
            if s == 56:
                act_u0(L)
            if s == 57:
                act_S1(L)
            if s == 58:
                act_u1(L)
            if s == 60:
                act_onorm(L, 0)
                act_onorm(L, 1)
                act_states_in(L, 1)
            if s == 64:
                act_s2_out(L)
                act_rows(L, 0)
            if s >= 49 and s % 4 == 1 and (s - 49) // 4 < 7:
                act_gate(L, (s - 49) // 4)
            if s == 68:
                act_sink(L)
            if s == 70:
                act_oa(L)
            if s == 71:
                act_rows(L, 1)
            if s == 75:
                act_gate(L, 7)
                act_od(L)

        def pool_slot(L, s):
            if s in (7, 15, 23):
                pool_conv(L, (s - 7) // 8)
            if s == 17:
                pool_stats(L, "k")
            if s == 23:
                pool_stats(L, "q")
            if s == 28:
                pool_k(L)
            if s == 32:
                pool_stats_sample(L, "k")
            if s == 36:
                pool_stats_sample(L, "q")
            if s == 41:
                pool_q(L)
            if s == 62:
                pool_onorm(L)
            if s == 70:
                pool_onorm_sample(L)

        def act_loads(L):
            SE.dma_start(cst[:, :], ins["cst"][L, :, :]).then_inc(d_cst.sem, 16)
            SE.dma_start(kc[:, :], ins["kct"][L, :, :]).then_inc(d_kc.sem, 16)
            SE.dma_start(vc[:, :], ins["vct"][L, :, :]).then_inc(d_vc.sem, 16)

        def act_conv_out(L):
            raw3 = craw[:, :].rearrange("p (c w) -> p c w", c=12)
            SE.wait_ge(win_free.sem, win_free.at(L, 12))
            SE.dma_start(outs["convp"][L, :, :].rearrange("p (c t) -> p c t", c=12), raw3[:, :, T:T + 3]).then_inc(d_conv.sem, 16)
            o4 = outs["convs"][L, :, :].rearrange("p (c t) -> p c t", c=12)
            SE.dma_start(o4[:, :, 16:24], raw3[:, :, T + 3:CW]).then_inc(d_conv.sem, 16)
            SE.dma_start(o4[:, :, 0:16], cst[:, :].rearrange("p (c t) -> p c t", c=12)[:, :, 8:24]).then_inc(d_conv.sem, 16)

        def act_kv_out(L):
            SE.wait_ge(v_at.sem, v_at.at(L, "ktok"))
            SE.wait_ge(a_at.sem, a_at.at(L, "vtok"))
            for name, t in (("k", ktok), ("v", vtok)):
                SE.dma_start(outs[name + "p"][L, :, :], t[:, P:2 * P]).then_inc(d_kv.sem, 16)
                SE.dma_start(outs[name + "s"][L, :, WINDOW - 1, :], t[0:B, 2 * P:3 * P]).then_inc(d_kv.sem, 16)

        def act_states_in(L, r):
            if r == 0:
                SE.wait_ge(pe_at.sem, pe_at.at(L, "s pv"))
            else:
                SE.wait_ge(pe_dn.sem, pe_dn.at(L, "qS"))
            SE.dma_start((states, states2)[r][:, :], ins["states"][L, :, r * 2 * B * P:(r + 1) * 2 * B * P]
                         ).then_inc(d_state[r].sem, 16)

        def act_s2_out(L):
            SE.wait_ge(v_dn.sem, v_dn.at(L, "S2", 3))
            SE.dma_start(outs["dnp"][L, :, :], M[0]["K"][:, :]).then_inc(d_s2.sem, 16)

        def act_out_done(L):
            for s in (d_conv, d_kv, d_s2, d_stout):
                SE.wait_ge(s.sem, s.at(L, s.per_layer))

        def pe_mix(L):
            TE.wait_ge(consts_in, 16)
            pe_ba_product(L)
            pe_sums(L, 1)
            for i in range(W_IN_TILES):
                if i == 0:
                    pe_win(L, 0, lambda: None)
                else:
                    pe_win(L, i, lambda: (pe_spread(L, 1) if i == 1 else None, pe_slot(L, 2 * i)))
                pe_slot(L, 2 * i + 1)
            for m, branch in ((0, "a"), (1, "a"), (0, "d"), (1, "d")):
                pe_branches(L, m, branch)
            for m in range(2, KT):
                pe_branches(L, m, "a")
                pe_branches(L, m, "d")
                if m < 4:
                    pe_outer(L, m)
            for m in range(KT):
                pe_out(L, m)

        def evac_target(i):
            if i < 12:
                return craw[:, i * CW + 3:(i + 1) * CW]
            if i < 14:
                return (ak, av)[i - 12][:, :]
            if i < 18:
                return tile_of(aq, i - 14)
            if i < 22:
                return tile_of(z, i - 18)
            return tile_of(gt, i - 22)

        def dve_mix(L):
            VE.wait_ge(consts_in, 16)
            split_tail(VE, w_tail_v, L, U_BA + AHEAD, (U_BA + AHEAD) % RING, UT - DS_MIX, UT)
            VE.wait_ge(out_ready.sem, out_ready.at(L, 4))
            VE.memset(craw[:, :].rearrange("p (c w) -> p c w", c=12)[:, :, 0:3], 0.0).then_inc(v_conv.sem, v_conv.mark("pad"))
            dve_factor(L, 1)
            dve_spread(L, 1)
            dve_ba_scale(L)
            for i in range(W_IN_TILES):
                if i:
                    dve_slot(L, 2 * i)
                if i == 22:
                    VE.wait_ge(v_conv.sem, v_conv.at(L, "silu", 2))
                dve_evac(L, i, evac_target(i))
                if i < 12:
                    if i == 0:
                        VE.wait_ge(v_conv.sem, v_conv.at(L, "pad"))
                    dve_conv(L, i)
                if i % 2 == 0:
                    u = U_IN + i // 2 + AHEAD
                    split_tail(VE, w_tail_v, L, u, u % RING, UT - DS_MIX, UT)
                dve_slot(L, 2 * i + 1)
            for m in range(KT):
                dve_branches(L, m)
                if m:
                    dve_mix_tail(L, m - 1)
                if m % 2 == 0:
                    u = U_AD + m // 2 + AHEAD
                    split_tail(VE, w_tail_v, L, u, u % RING, UT - DS_MIX, UT)
                if m in (0, 2, 4):
                    dve_state(L, 1 + m // 2)
            dve_mix_tail(L, 7)
            for m in range(KT):
                if m % 2 == 0:
                    u = U_WO + m // 2 + AHEAD
                    split_tail(VE, w_tail_v, L, u, u % RING, UT - DS_MIX, UT)
                dve_residual(L, 8 + m, m, U_WO + m // 2, banks[7 if m % 2 else 0], 0.5)
                dve_tail(L, 8 + m, m, C_N2)

        def act_mix(L):
            split_head(L, U_BA + AHEAD, (U_BA + AHEAD) % RING, (U_BA + AHEAD) // RING)
            for i in range(W_IN_TILES):
                if i % 2 == 0:
                    u = U_IN + i // 2 + AHEAD
                    split_head(L, u, u % RING, u // RING)
                if i:
                    act_slot(L, 2 * i)
                act_slot(L, 2 * i + 1)
            for m in range(KT):
                if m % 2 == 0:
                    u = U_AD + m // 2 + AHEAD
                    split_head(L, u, u % RING, u // RING)
                if m in (0, 1):
                    act_drow(L, 2 + m)
                act_branches(L, m)
                if m in (0, 1, 3, 5):
                    act_state_out(L, (m + 1) // 2)
            for m in range(KT):
                if m % 2 == 0:
                    u = U_WO + m // 2 + AHEAD
                    split_head(L, u, u % RING, u // RING)
                act_operand(L, 8 + m, m, C_N2)

        def pool_tail(L, u, half=None):
            if half != 1:
                split_tail(GE, None if half == 0 else w_tail_p, L, u, u % RING, 0, UT // 2 if half == 0 else UT - DS_MIX)
            else:
                split_tail(GE, w_tail_p, L, u, u % RING, UT // 2, UT - DS_MIX)

        def pool_mix(L):
            pool_factor(L, 1)
            pool_tail(L, U_BA + AHEAD)
            for i in range(W_IN_TILES):
                pool_tail(L, U_IN + i // 2 + AHEAD, i % 2)
                if i:
                    pool_slot(L, 2 * i)
                pool_slot(L, 2 * i + 1)
            for u in range(U_AD, U_WO + 4):
                pool_tail(L, u + AHEAD)

        def mix_sync(sp):
            sp.wait_ge(d_shift, 64)
            for s in (d_conv, d_kv, d_s2, d_stout):
                sp.wait_ge(s.sem, DEPTH * s.per_layer)

        def act_end(act):
            pass

        block = ctx.enter_context(nc.Block())

        @block.sync
        def _(sp):

            def load(u, r, free):
                if free is not None:
                    sp.wait_ge(w_head.sem, free)
                    sp.wait_ge(w_tail_p.sem, free)
                    sp.wait_ge(w_tail_v.sem, free)
                src = stream[u] if isinstance(u, int) else stream[u, :, :]
                sp.dma_start(raw[:, r * UT * P:(r + 1) * UT * P], src).then_inc(w_loaded[r], 16)

            load(0, 0, None)
            sp.dma_start(par_all[:, :], params).then_inc(par_in, 16)
            half = KT // 2 * N
            for n in range(2):
                sp.dma_start(x[:, n * half:(n + 1) * half], xT[:, n * half:(n + 1) * half]).then_inc(x_in[n], 16)
            sp.dma_start(con[:, 0:K_LE], consts[:, 0:K_LE]).then_inc(ones_in, 16)
            load(1, 1, None)
            sp.dma_start(con[:, K_LE:NCON], consts[:, K_LE:NCON]).then_inc(consts_in, 16)
            load(2, 2, None)
            with sp.Fori(1, STREAM // RING) as i:
                for r in range(RING):
                    load(RING * i + r, r, RING * i + (r - RING + 1))
            for u in range(STREAM // RING * RING, STREAM):
                load(u, u % RING, u - RING + 1)
            for m in (4, 6, 7, 8):
                sp.wait_ge(x_done.sem, x_done.at(DEPTH - 1, 16 + m))
                lo = {4: 0, 6: 4, 7: 6, 8: 7}[m]
                sp.dma_start(outs["y"][:, lo * N:m * N], x[:, lo * N:m * N]).then_inc(y_out, 16)
            sp.wait_ge(y_out, 64)
            mix_sync(sp)

        @block.gpsimd
        def _(pool):
            nc.gpsimd.memset(mhalf[:, :], -0.5).then_inc(ready0, 1)
            pool.wait_ge(ready0, 9)
            split_tail(nc.gpsimd, w_tail_p, 0, 0, 0, 0, DS_FIRST)
            for m in range(KT):
                if m % (KT // 2) == 0:
                    pool.wait_ge(x_in[m // (KT // 2)], 16)
                if m >= 2:
                    pool.wait_ge(acc_done.sem, m - 1)
                nc.gpsimd.tensor_tensor(tile_of(sq, m % 2), tile_of(x, m), tile_of(x, m), ALU.mult).then_inc(sq_done.sem, 1)
            split_tail(nc.gpsimd, w_tail_p, 0, 1, 1, 0, UT - DS_FFN)
            for name in ("k", "v"):
                for l in range(DEPTH):
                    pool.dma_start(outs[name + "s"][l, :, 0:WINDOW - 1, :], ins[name + "cache"][l, :, 1:WINDOW, :]
                                   ).then_inc(d_shift, 16)
            with pool.Fori(0, DEPTH) as L:
                pool_factor(L, 0)
                pool_units(L, 0, U_BA, DS_FFN)
                pool_mix(L)
                pool_factor(L, 2)
                pool_units(L, U_G2, UNITS - U_G2, DS_FFN)

        @block.scalar
        def _(act):
            act.wait_ge(w_loaded[0], 16)
            nc.scalar.copy(slot(whi, 0), slot(raw, 0)).then_inc(w_head.sem, 1)
            act.wait_ge(par_in, 16)
            for m in range(KT):
                if m % (KT // 2) == 0:
                    act.wait_ge(x_in[m // (KT // 2)], 16)
                nc.scalar.activation(tile_of(xh, m), tile_of(x, m), ACT.Copy,
                                     scale=par_all[:, C_N1 + m:C_N1 + m + 1]).then_inc(xh_done.sem, 1)
            act.wait_ge(w_loaded[1], 16)
            nc.scalar.copy(slot(whi, 1), slot(raw, 1)).then_inc(w_head.sem, 1)
            with act.Fori(0, DEPTH) as L:
                act_loads(L)
                act.wait_ge(par_ready.sem, par_ready.at(L, 1))
                act_gate_up(L, 0)
                act_down(L, 0)
                act_mix(L)
                act_out_done(L)
                act_gate_up(L, 1)
                act_down(L, 1)

        @block.tensor
        def _(pe):
            nc.tensor.sem_inc(w_used.sem, 1)
            with pe.Fori(0, DEPTH) as L:
                pe_gate_up(L, 0)
                pe_down(L, 0)
                pe_mix(L)
                pe_gate_up(L, 1)
                pe_down(L, 1)

        @block.vector
        def _(dve):
            nc.vector.memset(acc[:, :], 0.0).then_inc(acc_clear.sem, 1)
            nc.vector.memset(small[:, :], 0.0).then_inc(ready0, 1)
            nc.vector.memset(bt[:, :], 0.0).then_inc(ready0, 1)
            nc.vector.memset(avar[:, :], 1.0).then_inc(ready0, 1)
            nc.vector.memset(prod[:, :], 0.0).then_inc(ready0, 1)
            nc.vector.memset(qsq[:, :], 0.0).then_inc(ready0, 1)
            nc.vector.sem_inc(win_free.sem, 2)
            nc.vector.memset(var[:, :], 1.0).then_inc(ready0, 1)
            nc.vector.memset(rst[:, :], 1.0).then_inc(ready0, 1)
            nc.vector.memset(rs[:, :], 1.0).then_inc(ready0, 1)
            nc.vector.sem_inc(glu_free.sem, RING)
            nc.vector.sem_inc(h_ready.sem, RING)
            nc.vector.sem_inc(x_done.sem, KT)
            split_tail(nc.vector, w_tail_v, 0, 0, 0, DS_FIRST, UT)
            dve.wait_ge(par_in, 16)
            dve.wait_ge(acc_clear.sem, 1)
            for m in range(KT):
                if m % (KT // 2) == 0:
                    dve.wait_ge(x_in[m // (KT // 2)], 16)
                dve.wait_ge(xh_done.sem, m + 1)
                nc.vector.scalar_tensor_tensor(out=tile_of(xl, m), in0=tile_of(x, m), scalar=par_all[:, C_N1 + m:C_N1 + m + 1],
                                               in1=tile_of(xh, m).bitcast(F32), op0=ALU.mult,
                                               op1=ALU.subtract).then_inc(xl_done.sem, 1)
                if m:
                    dve.wait_ge(acc_done.sem, m)
                dve.wait_ge(sq_done.sem, m + 1)
                nc.vector.tensor_tensor(acc[:, :], acc[:, :], tile_of(sq, m % 2), ALU.add).then_inc(acc_done.sem, 1)
            split_tail(nc.vector, w_tail_v, 0, 1, 1, UT - DS_FFN, UT)
            dve.wait_ge(ones_in, 16)
            with dve.Fori(0, DEPTH) as L:
                dve.wait_ge(xh_done.sem, xh_done.at(L, 0))
                dve.wait_ge(xl_done.sem, xl_done.at(L, 0))
                nc.vector.tensor_copy(par[:, :], par_all[:, bass.ds(L * NPAR, NPAR)]).then_inc(par_ready.sem, 1)
                dve.wait_ge(par_ready.sem, par_ready.at(L, 1))
                dve_gate_up(L, 0)
                dve_down(L, 0)
                dve_mix(L)
                dve_gate_up(L, 1)
                dve_down(L, 1)


def kernel(**inputs):
    import concourse.bacc as bacc
    from concourse.bass_utils import run_bass_kernel_spmd as run

    a = {k: np.asarray(v) for k, v in inputs.items()}
    tokens = np.concatenate([a["x_prompt"][0], a["x_sample"][:, 0]], axis=0)
    kcache, vcache = (a[n].reshape(DEPTH, B, WINDOW, P) for n in ("cache_swa_k", "cache_swa_v"))
    conv = a["state_conv"].reshape(DEPTH, B, CONV_W - 1, 3, H, P)[:, :, :, [1, 0, 2]]
    arrays = {
        "stream": host_stream(a),
        "xT": tokens.T.reshape(KT, P, N).transpose(1, 0, 2).reshape(P, KT * N).copy(),
        "params": host_params(a),
        "consts": host_constants(),
        "kct": kcache.transpose(0, 3, 1, 2).reshape(DEPTH, P, B * P).copy(),
        "vct": vcache.transpose(0, 2, 1, 3).reshape(DEPTH, P, B * P).copy(),
        "kcache": kcache.copy(),
        "vcache": vcache.copy(),
        "cst": conv.transpose(0, 5, 3, 4, 2, 1).reshape(DEPTH, P, 12 * 3 * B).copy(),
        "states": a["state_dn"].transpose(0, 3, 2, 1, 4).reshape(DEPTH, DK, H * B * DK).copy(),
    }
    shapes = {
        "y": (P, KT * N),
        "kp": (DEPTH, WINDOW, P), "vp": (DEPTH, WINDOW, P),
        "ks": (DEPTH, B, WINDOW, P), "vs": (DEPTH, B, WINDOW, P),
        "dnp": (DEPTH, DK, H * DK), "dns": (DEPTH, DK, H * B * DK),
        "convp": (DEPTH, P, 12 * 3), "convs": (DEPTH, P, 12 * 3 * B),
    }
    plan = {}
    for _ in range(2):
        nc = bacc.Bacc("TRN2", target_bir_lowering=False, num_devices=1)
        args = {k: nc.dram_tensor(k, v.shape, F32, kind="ExternalInput").ap() for k, v in arrays.items()}
        outs = {k: nc.dram_tensor("out_" + k, s, F32, kind="ExternalOutput").ap() for k, s in shapes.items()}
        build(nc, args["stream"], args["xT"], args["params"], args["consts"], outs, args, plan)
    r = run(nc, [arrays], core_ids=[0]).results[0]
    y = r["out_y"].reshape(P, KT, N).transpose(2, 1, 0).reshape(N, D_MODEL)
    heads = (N_KV, HEAD_DIM)

    def conv_rows(t, n):
        t = t.reshape(DEPTH, P, 3, H, 3, n)[:, :, [1, 0, 2]]
        return t.transpose(0, 5, 4, 2, 3, 1).reshape(DEPTH, n, 3, 12 * P)

    return (y[:T].reshape(1, T, D_MODEL), y[T:].reshape(B, 1, D_MODEL),
            r["out_kp"].reshape(DEPTH, 1, WINDOW, *heads), r["out_vp"].reshape(DEPTH, 1, WINDOW, *heads),
            r["out_dnp"].reshape(DEPTH, 1, DK, H, DK).transpose(0, 1, 3, 2, 4), conv_rows(r["out_convp"], 1),
            r["out_ks"].reshape(DEPTH, B, WINDOW, *heads), r["out_vs"].reshape(DEPTH, B, WINDOW, *heads),
            r["out_dns"].reshape(DEPTH, DK, H, B, DK).transpose(0, 3, 2, 1, 4), conv_rows(r["out_convs"], B))
```
